# Optimizing a Trainium2 kernel written in Bass

```python
import math
import jax, jax.numpy as jnp
from jax import lax
import numpy as np

D_MODEL = 2048
BATCH = 1
SEQ = 256
DEPTH = 2

N_MIXERS = 4
N_REPEAT = max(DEPTH // N_MIXERS, 1)
BLK = 128
NEG = -1e30
EPS = 1e-6
F32 = jnp.float32

REL_BUCKETS = 32
REL_MAX_DIST = 2048
REL_HEADS = 32

MLA_HEADS = 16
MLA_Q_RANK = 512
MLA_KV_RANK = 512
MLA_NOPE = 128
MLA_ROPE = 64
MLA_V = 128
ROPE_THETA = 10000.0

SWA_Q_HEADS = 32
SWA_KV_HEADS = 4
SWA_HEAD_DIM = 64
SWA_WINDOW = 128

DIL_HEADS = 32
DIL_HEAD_DIM = 64
DIL_PAIRS = ((128, 1), (512, 4), (2048, 16))

FOX_HEADS = 16
FOX_HEAD_DIM = 128

D_FF = 5632
CONV_WIDTH = 3

kernel_name = 'hybrid_interleaved_mla_swa_dilated_fox'

def _rmsnorm(x, g):
    xf = x.astype(F32)
    y = xf * lax.rsqrt(jnp.mean(xf * xf, axis=-1, keepdims=True) + EPS)
    return (y * g.astype(F32)).astype(x.dtype)

def _rope(x, positions):
    half = x.shape[-1] // 2
    inv_freq = ROPE_THETA ** (-jnp.arange(half, dtype=F32) / half)
    ang = positions.astype(F32)[:, :, None] * inv_freq
    ang = ang.reshape(ang.shape[:2] + (1,) * (x.ndim - 3) + (half,))
    cos, sin = jnp.cos(ang), jnp.sin(ang)
    x1 = x[..., :half].astype(F32)
    x2 = x[..., half:].astype(F32)
    return jnp.concatenate([x1 * cos - x2 * sin, x2 * cos + x1 * sin], axis=-1).astype(x.dtype)

def _t5_bucket(n):
    exact = REL_BUCKETS // 2
    nf = jnp.maximum(n, 1).astype(F32)
    large = exact + (jnp.log(nf / exact) / math.log(REL_MAX_DIST / exact) * (REL_BUCKETS - exact)).astype(jnp.int32)
    return jnp.where(n < exact, n, jnp.minimum(large, REL_BUCKETS - 1))

def _banded_stats(q, k, v, bias, max_dist):
    n, L, hk, g, dh = q.shape
    nb = L // BLK
    qb = q.reshape(n, nb, BLK, hk, g, dh)

    def band(a):
        ab = a.reshape(n, nb, BLK, hk, dh)
        prev = jnp.pad(ab, ((0, 0), (1, 0), (0, 0), (0, 0), (0, 0)))[:, :-1]
        return jnp.concatenate([prev, ab], axis=2)

    kb, vb = band(k), band(v)
    s = jnp.einsum('nbqhgd,nbkhd->nbhgqk', qb, kb, preferred_element_type=F32)
    qi = jnp.arange(BLK)[:, None]
    kj = jnp.arange(2 * BLK)[None, :]
    dist = qi + BLK - kj
    in_seq = jnp.arange(nb)[:, None, None] * BLK + kj - BLK >= 0
    valid = (dist >= 0) & (dist <= max_dist) & in_seq
    b = bias.astype(F32)[:, :, jnp.clip(dist, 0, max_dist)]
    s = jnp.where(valid[None, :, None, None], s + b, NEG)
    m = jnp.max(s, axis=-1)
    p = jnp.exp(s - m[..., None])
    l = jnp.sum(p, axis=-1)
    acc = jnp.einsum('nbhgqk,nbkhd->nbqhgd', p.astype(v.dtype), vb, preferred_element_type=F32)
    to_seq = lambda a: jnp.moveaxis(a, -1, 2).reshape(n, L, hk, g)
    return to_seq(m), to_seq(l), acc.reshape(n, L, hk, g, dh)

def _mla(h, positions, w_in, g_q, g_kv, w_qb, w_kvb, w_o):
    bsz, t, _ = h.shape
    qk_dim = MLA_NOPE + MLA_ROPE
    lat = h @ w_in
    c_q = _rmsnorm(lat[..., :MLA_Q_RANK], g_q)
    c_kv = _rmsnorm(lat[..., MLA_Q_RANK:MLA_Q_RANK + MLA_KV_RANK], g_kv)
    k_rope = _rope(lat[..., MLA_Q_RANK + MLA_KV_RANK:], positions)
    q = (c_q @ w_qb).reshape(bsz, t, MLA_HEADS, qk_dim) * qk_dim ** -0.5
    q_nope = q[..., :MLA_NOPE]
    q_rope = _rope(q[..., MLA_NOPE:], positions)
    kv = (c_kv @ w_kvb).reshape(bsz, t, MLA_HEADS, MLA_NOPE + MLA_V)
    k_nope, v = kv[..., :MLA_NOPE], kv[..., MLA_NOPE:]
    nb = t // BLK
    blocks = lambda a: a.reshape((bsz, nb, BLK) + a.shape[2:]).swapaxes(0, 1)
    kpos = jnp.arange(t)

    def block(args):
        qn, qr, i = args
        s = (jnp.einsum('bqhd,bkhd->bhqk', qn, k_nope, preferred_element_type=F32)
             + jnp.einsum('bqhd,bkd->bhqk', qr, k_rope, preferred_element_type=F32))
        qpos = i * BLK + jnp.arange(BLK)
        s = jnp.where(kpos[None, :] <= qpos[:, None], s, NEG)
        p = jax.nn.softmax(s, axis=-1)
        return jnp.einsum('bhqk,bkhd->bqhd', p.astype(v.dtype), v, preferred_element_type=F32)

    o = lax.map(block, (blocks(q_nope), blocks(q_rope), jnp.arange(nb)))
    o = o.swapaxes(0, 1).reshape(bsz, t, MLA_HEADS * MLA_V).astype(h.dtype)
    return o @ w_o

def _swa_sinks(h, rel_bias, w_qkv, b_qkv, sinks, w_o, b_o):
    bsz, t, _ = h.shape
    grp = SWA_Q_HEADS // SWA_KV_HEADS
    nq = SWA_Q_HEADS * SWA_HEAD_DIM
    nk = SWA_KV_HEADS * SWA_HEAD_DIM
    qkv = h @ w_qkv + b_qkv
    q = qkv[..., :nq].reshape(bsz, t, SWA_KV_HEADS, grp, SWA_HEAD_DIM) * SWA_HEAD_DIM ** -0.5
    k = qkv[..., nq:nq + nk].reshape(bsz, t, SWA_KV_HEADS, SWA_HEAD_DIM)
    v = qkv[..., nq + nk:].reshape(bsz, t, SWA_KV_HEADS, SWA_HEAD_DIM)
    bias = rel_bias[_t5_bucket(jnp.arange(SWA_WINDOW))].T.reshape(SWA_KV_HEADS, grp, SWA_WINDOW)
    m, l, acc = _banded_stats(q, k, v, bias, SWA_WINDOW - 1)
    sink = sinks.astype(F32).reshape(SWA_KV_HEADS, grp)
    m2 = jnp.maximum(m, sink)
    a = jnp.exp(m - m2)
    den = l * a + jnp.exp(sink - m2)
    o = acc * (a / den)[..., None]
    return o.reshape(bsz, t, nq).astype(h.dtype) @ w_o + b_o

def _dilated_attention(h, rel_bias, w_qkv, w_o):
    bsz, t, _ = h.shape
    q, k, v = jnp.split(h @ w_qkv, 3, axis=-1)
    q = q.reshape(bsz, t, DIL_HEADS, 1, DIL_HEAD_DIM) * DIL_HEAD_DIM ** -0.5
    k = k.reshape(bsz, t, DIL_HEADS, DIL_HEAD_DIM)
    v = v.reshape(bsz, t, DIL_HEADS, DIL_HEAD_DIM)
    ms, ls, accs = [], [], []
    for window, rate in DIL_PAIRS:
        n_keys = window // rate
        ts = t // rate
        lp = -(-ts // BLK) * BLK

        def to_sub(a):
            a = a.reshape((bsz, ts, rate) + a.shape[2:]).swapaxes(1, 2).reshape((bsz * rate, ts) + a.shape[2:])
            return jnp.pad(a, ((0, 0), (0, lp - ts)) + ((0, 0),) * (a.ndim - 2))

        def from_sub(a):
            a = a[:, :ts]
            return a.reshape((bsz, rate, ts) + a.shape[2:]).swapaxes(1, 2).reshape((bsz, t) + a.shape[2:])

        bias = rel_bias[_t5_bucket(rate * jnp.arange(n_keys + 1))].T[:, None, :]
        m, l, acc = _banded_stats(to_sub(q), to_sub(k), to_sub(v), bias, n_keys)
        ms.append(from_sub(m))
        ls.append(from_sub(l))
        accs.append(from_sub(acc))
    m = jnp.stack(ms)
    l = jnp.stack(ls)
    acc = jnp.stack(accs)
    wgt = jnp.exp(m - jnp.max(m, axis=0))
    o = jnp.sum(acc * wgt[..., None], axis=0) / jnp.sum(l * wgt, axis=0)[..., None]
    return o.reshape(bsz, t, DIL_HEADS * DIL_HEAD_DIM).astype(h.dtype) @ w_o

def _forgetting_attention(h, w_in, b_f, w_o):
    bsz, t, _ = h.shape
    hd = FOX_HEADS * FOX_HEAD_DIM
    proj = h @ w_in
    q = proj[..., :hd].reshape(bsz, t, FOX_HEADS, FOX_HEAD_DIM) * FOX_HEAD_DIM ** -0.5
    k = proj[..., hd:2 * hd].reshape(bsz, t, FOX_HEADS, FOX_HEAD_DIM)
    v = proj[..., 2 * hd:3 * hd].reshape(bsz, t, FOX_HEADS, FOX_HEAD_DIM)
    log_f = jax.nn.log_sigmoid(proj[..., 3 * hd:].astype(F32) + b_f.astype(F32))
    cum = jnp.cumsum(log_f, axis=1).transpose(0, 2, 1)
    nb = t // BLK
    q_blocks = q.reshape(bsz, nb, BLK, FOX_HEADS, FOX_HEAD_DIM).swapaxes(0, 1)
    c_blocks = cum.reshape(bsz, FOX_HEADS, nb, BLK).transpose(2, 0, 1, 3)
    kpos = jnp.arange(t)

    def block(args):
        qb, cb, i = args
        s = jnp.einsum('bqhd,bkhd->bhqk', qb, k, preferred_element_type=F32)
        s = s + cb[..., None] - cum[:, :, None, :]
        qpos = i * BLK + jnp.arange(BLK)
        s = jnp.where(kpos[None, :] <= qpos[:, None], s, NEG)
        p = jax.nn.softmax(s, axis=-1)
        return jnp.einsum('bhqk,bkhd->bqhd', p.astype(v.dtype), v, preferred_element_type=F32)

    o = lax.map(block, (q_blocks, c_blocks, jnp.arange(nb)))
    o = o.swapaxes(0, 1).reshape(bsz, t, hd).astype(h.dtype)
    return o @ w_o

def _conv_ffn(h, w_in, conv_w, conv_b, w_out):
    t = h.shape[1]
    u = h @ w_in
    up = jnp.pad(u, ((0, 0), (CONV_WIDTH - 1, 0), (0, 0)))
    c = conv_b + up[:, 0:t] * conv_w[0]
    for j in range(1, CONV_WIDTH):
        c = c + up[:, j:j + t] * conv_w[j]
    gate, val = jnp.split(c, 2, axis=-1)
    return (jax.nn.silu(gate) * val) @ w_out

def setup_inputs(seed: int = 0) -> dict:
    key = jax.random.key(seed)
    ks = iter(jax.random.split(key, 32))
    R, D = N_REPEAT, D_MODEL

    def w(shape, fan_in):
        return jax.random.normal(next(ks), shape, F32) * fan_in ** -0.5

    def gain(shape):
        return 1.0 + 0.02 * jax.random.normal(next(ks), shape, F32)

    def small(shape, scale):
        return scale * jax.random.normal(next(ks), shape, F32)

    x = jax.random.normal(next(ks), (BATCH, SEQ, D), F32)
    offset = jax.random.randint(next(ks), (BATCH, 1), 0, 1024, dtype=jnp.int32)
    positions = offset + jnp.arange(SEQ, dtype=jnp.int32)[None, :]
    swa_qkv = (SWA_Q_HEADS + 2 * SWA_KV_HEADS) * SWA_HEAD_DIM
    return {
        'x': x,
        'positions': positions,
        'rel_bias': small((REL_BUCKETS, REL_HEADS), 0.3),
        'norm_mix': gain((DEPTH, D)),
        'norm_ffn': gain((DEPTH, D)),
        'mla_w_in': w((R, D, MLA_Q_RANK + MLA_KV_RANK + MLA_ROPE), D),
        'mla_g_q': gain((R, MLA_Q_RANK)),
        'mla_g_kv': gain((R, MLA_KV_RANK)),
        'mla_w_qb': w((R, MLA_Q_RANK, MLA_HEADS * (MLA_NOPE + MLA_ROPE)), MLA_Q_RANK),
        'mla_w_kvb': w((R, MLA_KV_RANK, MLA_HEADS * (MLA_NOPE + MLA_V)), MLA_KV_RANK),
        'mla_w_o': w((R, MLA_HEADS * MLA_V, D), MLA_HEADS * MLA_V),
        'swa_w_qkv': w((R, D, swa_qkv), D),
        'swa_b_qkv': small((R, swa_qkv), 0.02),
        'swa_sinks': small((R, SWA_Q_HEADS), 0.5),
        'swa_w_o': w((R, SWA_Q_HEADS * SWA_HEAD_DIM, D), SWA_Q_HEADS * SWA_HEAD_DIM),
        'swa_b_o': small((R, D), 0.02),
        'dil_w_qkv': w((R, D, 3 * DIL_HEADS * DIL_HEAD_DIM), D),
        'dil_w_o': w((R, DIL_HEADS * DIL_HEAD_DIM, D), DIL_HEADS * DIL_HEAD_DIM),
        'fox_w_in': w((R, D, 3 * FOX_HEADS * FOX_HEAD_DIM + FOX_HEADS), D),
        'fox_b_f': 2.0 + small((R, FOX_HEADS), 0.5),
        'fox_w_o': w((R, FOX_HEADS * FOX_HEAD_DIM, D), FOX_HEADS * FOX_HEAD_DIM),
        'ffn_w_in': w((DEPTH, D, 2 * D_FF), D),
        'ffn_conv_w': w((DEPTH, CONV_WIDTH, 2 * D_FF), CONV_WIDTH),
        'ffn_conv_b': small((DEPTH, 2 * D_FF), 0.01),
        'ffn_w_out': w((DEPTH, D_FF, D), D_FF),
        'final_norm': gain((D,)),
    }

def reference(x, positions, rel_bias, norm_mix, norm_ffn,
              mla_w_in, mla_g_q, mla_g_kv, mla_w_qb, mla_w_kvb, mla_w_o,
              swa_w_qkv, swa_b_qkv, swa_sinks, swa_w_o, swa_b_o,
              dil_w_qkv, dil_w_o,
              fox_w_in, fox_b_f, fox_w_o,
              ffn_w_in, ffn_conv_w, ffn_conv_b, ffn_w_out,
              final_norm):
    h = x
    for i in range(DEPTH):
        kind = i % N_MIXERS
        r = i // N_MIXERS
        a = _rmsnorm(h, norm_mix[i])
        if kind == 0:
            y = _mla(a, positions, mla_w_in[r], mla_g_q[r], mla_g_kv[r], mla_w_qb[r], mla_w_kvb[r], mla_w_o[r])
        elif kind == 1:
            y = _swa_sinks(a, rel_bias, swa_w_qkv[r], swa_b_qkv[r], swa_sinks[r], swa_w_o[r], swa_b_o[r])
        elif kind == 2:
            y = _dilated_attention(a, rel_bias, dil_w_qkv[r], dil_w_o[r])
        else:
            y = _forgetting_attention(a, fox_w_in[r], fox_b_f[r], fox_w_o[r])
        h = h + y
        h = h + _conv_ffn(_rmsnorm(h, norm_ffn[i]), ffn_w_in[i], ffn_conv_w[i], ffn_conv_b[i], ffn_w_out[i])
    return _rmsnorm(h, final_norm)


_drawn_inputs = setup_inputs


def setup_inputs(seed=0):
    import zlib

    import numpy as np

    out = dict(_drawn_inputs(seed))
    spreads = {}
    factors = {'norm_mix': 5.507,
     'norm_ffn': 2.704,
     'mla_g_q': 8.0,
     'mla_g_kv': 8.0,
     'swa_b_qkv': 3.205,
     'swa_sinks': 31.234,
     'swa_b_o': 24.264,
     'ffn_conv_b': 5.372,
     'final_norm': 7.424}
    for name, (base, spread) in spreads.items():
        noise = np.random.default_rng([zlib.crc32(name.encode()), seed]).standard_normal(out[name].shape)
        drawn = base * np.exp(spread * noise) if base else spread * noise
        out[name] = __import__('jax').numpy.asarray(drawn.astype(out[name].dtype))
    for name, factor in factors.items():
        out[name] = (out[name] * factor).astype(out[name].dtype)
    return out
```

```python
import math
from contextlib import ExitStack

import numpy as np
import concourse.bass as bass
from concourse import mybir

F32 = mybir.dt.float32
F32R = mybir.dt.float32r
I32 = mybir.dt.int32
ALU = mybir.AluOpType
ACT = mybir.ActivationFunctionType

P = 128
T = 256
D = 2048
KT = D // P
FF = 5632
FT = FF // P
RANK = 512
HEADS_A, NOPE, ROPE, VDIM = 16, 128, 64, 128
HEADS_B, KV_B, DH = 32, 4, 64
QKV_B = (HEADS_B + 2 * KV_B) * DH
EPS = 1e-6
NEG = -1e30
THETA = 10000.0
BUCKETS, MAX_DIST, WINDOW = 32, 2048, 128

SLOTS = 4
CH = 1024
AHEAD = 8
COLS = 512
DMAS = 2

PC_MIX, PC_FFN, PC_FIN, PC_GQ, PC_GKV, PC_BQKV, PC_BO = 0, 32, 64, 80, 84, 88, 108
PC_END0 = 124
PC_CONVW = 128
CT = 2 * FT
PC_CONVB = PC_CONVW + 2 * 3 * CT
PC_END = PC_CONVB + 2 * CT


class Phase:
    def __init__(self, chunk0, chunks, group0, groups):
        self.c0, self.n, self.g0, self.ng = chunk0, chunks, group0, groups
        self.c1, self.g1 = chunk0 + chunks, group0 + groups


def phases():
    out, c, g = {}, 0, 0
    for name, n, m in (("a_in", 18, 3), ("a_q", 16, 4), ("a_kv", 16, 8), ("a_out", 32, 4),
                       ("f0_in", 176, 22), ("f0_out", 88, 4), ("b_in", 40, 5), ("b_out", 32, 4),
                       ("f1_in", 176, 22), ("f1_out", 88, 4)):
        out[name] = Phase(c, n, g, m)
        c, g = c + n, g + m
    return out, c


PH, CHUNKS = phases()
OP0 = {"x": 0, "lat": 4, "a_out": 6, "f0_in": 10, "f0_out": 21, "b_out": 25, "f1_in": 29}
SQ0 = {"x": 0, "lat": 4, "a_out": 6, "f0_out": 10, "b_out": 14, "f1_out": 18}
NORMS = ["x", "cq", "ckv", "f0", "b", "f1", "out"]
NORM_SQ = [4, 5, 6, 10, 14, 18, 22]
UNITS_A, UNITS_B = HEADS_A // 2, HEADS_B // 2


class Lin:
    def __init__(self, c, k=0, i=None):
        self.c, self.k, self.i = c, k, i

    def __add__(self, d):
        return Lin(self.c + d, self.k, self.i)

    def __sub__(self, d):
        return self + (-d)

    def times(self, m):
        return Lin(self.c * m, self.k * m, self.i)

    def over(self, d):
        assert self.i is None or self.k % d == 0
        return Lin(self.c // d, self.k // d, self.i)

    def mod(self, d):
        assert self.i is None or self.k % d == 0
        return self.c % d

    @property
    def v(self):
        return self.c if self.i is None else self.i * self.k + self.c


def sl(n, size):
    return slice(n.v, n.v + size) if n.i is None else bass.ds(n.v, size)


def repeat(eng, start, end, body):
    if end > start:
        with eng.Fori(start, end) as i:
            body(i)


class Steps:
    def __init__(self, eng, sem):
        self.eng, self.sem, self.n, self.at = eng, sem, 0, None

    def __call__(self, ins):
        ins.then_inc(self.sem, 1)
        self.n += 1
        return ins

    def sync(self):
        self.eng.wait_ge(self.sem, Lin(self.n, *(self.at or ())).v)

    def loop(self, start, end, per, body):
        n0 = self.n

        def inner(i):
            self.n, self.at = n0 - start * per, (per, i)
            body(i)
            assert self.n == n0 - start * per + per, f"steps in the loop: {self.n - n0 + start * per}"
        if end > start:
            repeat(self.eng, start, end, inner)
        self.n, self.at = n0 + (end - start) * per, None


def build(nc, x, positions, rel_bias, norm_mix, norm_ffn, mla_w_in, mla_g_q, mla_g_kv, mla_w_qb,
          mla_w_kvb, mla_w_o, swa_w_qkv, swa_b_qkv, swa_sinks, swa_w_o, swa_b_o, ffn_w_in,
          ffn_conv_w, ffn_conv_b, ffn_w_out, final_norm, c_ident, c_rot, c_invf, c_mask,
          c_onehot, out):
    bias_dram = nc.dram_tensor("bias_rows", [HEADS_B, P, 384], F32, kind="Internal").ap()

    top = [(nc.sbuf_base + 63) // 64 * 64]

    def region(nbytes):
        at = top[0]
        top[0] += (nbytes + 31) // 32 * 32
        assert top[0] <= nc.sbuf_usable_end, (top[0], nc.sbuf_usable_end)
        return at

    def place(name, shape, dt, at):
        return nc.alloc_sbuf_tensor_at(name, shape, dt, offset=at)

    def new(name, shape, dt=F32):
        return place(name, shape, dt, region(int(np.prod(shape[1:])) * 4))

    raw = [new(f"raw{s}", [P, CH]) for s in range(SLOTS)]
    w_hi = [new(f"w_hi{s}", [P, CH], F32R) for s in range(SLOTS)]
    w_lo = [new(f"w_lo{s}", [P, CH], F32R) for s in range(SLOTS)]
    h = new("h", [P, KT, T])
    tb = new("tb", [P, 4, T])
    up = new("up", [P, 4, T + 2])
    cg = new("cg", [P, 4, T])
    cv = new("cv", [P, 4, T])
    par = new("par", [P, 7 * P])
    ident = new("ident", [P, P])
    ones = new("ones", [P, P])
    rs = new("rs", [P, T])
    sqa = new("sqa", [P, T])
    eps = new("eps", [P, 2])
    rs_col = new("rs_col", [P, 6])
    nm = new("nm", [P, 2, 4])
    ls = new("ls", [P, 2, 4])
    es = new("es", [P, 2, 4])
    ri = new("ri", [P, 2, 4])
    fence = new("fence", [P, 8])

    ra = region(KT * 2 * T * 4)
    aop = place("aop", [P, KT, 2, T], F32R, ra)
    pts = place("pts", [P, 2, 384], F32, ra)
    sm = place("sm", [P, 2, 2, 384], F32, ra + 3072)
    st_q = place("st_q", [P, 2, 2, T], F32, ra + 9216)
    st_r = place("st_r", [P, 2, T], F32, ra + 13312)
    st_v = place("st_v", [P, 2, 2, T], F32, ra + 15360)
    mask = place("mask", [P, 384], F32, ra + 19456)
    kr = place("kr", [P, T], F32, ra + 20992)
    kd = place("kd", [P, KV_B, T], F32, ra + 22016)
    vb = place("vb", [P, 2, T], F32, ra + 26112)
    yt = place("yt", [P, 2, D], F32, ra)

    rg = region(FT * 2 * T * 4)
    gop = place("gop", [P, FT, 2, T], F32R, rg)
    qn = place("qn", [P, HEADS_A, T], F32, rg)
    qr = place("qr", [P, UNITS_A, T], F32, rg + 16384)
    kn = place("kn", [P, HEADS_A, T], F32, rg + 24576)
    va = place("va", [P, 2, HEADS_A * VDIM], F32, rg + 40960)
    r_o = rg + 57344
    oop = place("oop", [P, KT, 2, T], F32R, r_o)
    cop = place("cop", [P, 8, 2, T], F32R, r_o)
    cos = place("cos", [P, T], F32, r_o + 16384)
    sin = place("sin", [P, T], F32, r_o + 17408)
    rot = place("rot", [P, P], F32, r_o + 18432)
    rsq = place("rsq", [P, T], F32, r_o + 18944)
    rsk = place("rsk", [P, T], F32, r_o + 19968)
    sqb = place("sqb", [P, T], F32, r_o + 20992)
    ang = place("ang", [P, T], F32, r_o + 22016)
    turn = place("turn", [P, T], F32, r_o + 23040)
    posi = place("posi", [P, T], I32, r_o + 24064)
    invf = place("invf", [P, 1], F32, r_o + 25088)
    xin = place("xin", [P, 2, D], F32, rg)
    praw = place("praw", [P, 7, P], F32, rg + 16384)
    onehot = place("onehot", [BUCKETS + 1, 384], F32, rg + 20480)
    relb = place("relb", [BUCKETS + 1, HEADS_B], F32, rg + 22016)
    brow = place("brow", [HEADS_B, 384], F32, rg + 22528)
    qb = place("qb", [P, KT, T], F32, rg)
    bt = place("bt", [P, HEADS_B, T], F32, rg + 24576)
    st_vb = place("st_vb", [P, 2, 2, DH], F32, ra + 15360)
    st_b = place("st_b", [P, 2, 2, T], F32, ra + 16384)
    st_s = place("st_s", [P, 2, 2], F32, ra + 20480)
    sinkc = place("sinkc", [P, HEADS_B], F32, ra + 28160)
    bvrow = place("bvrow", [P, T], F32, ra + 28288)

    ctx = ExitStack()
    with ctx:
        ps = ctx.enter_context(nc.psum_tensor("ps", [P, 8, 512], F32))

        def sem(name):
            return ctx.enter_context(nc.semaphore(name))

        par_in, x_in, c_in, rope_in = sem("par_in"), sem("x_in"), sem("c_in"), sem("rope_in")
        mask_in, bias_out, bt_in, swa_in = sem("mask_in"), sem("bias_out"), sem("bt_in"), sem("swa_in")
        const_set, par_t, par_ready, x_t, h_in = sem("const_set"), sem("par_t"), sem("par_ready"), sem("x_t"), sem("h_in")
        brow_t, brow_ready = sem("brow_t"), sem("brow_ready")
        raw_full = [sem(f"raw_full{s}") for s in range(SLOTS)]
        hi_ready, lo_ready, chunk_used = sem("hi_ready"), sem("lo_ready"), sem("chunk_used")
        b_copied, banks_free = sem("b_copied"), sem("banks_free")
        t_ready, op_hi, op_lo = sem("t_ready"), sem("op_hi"), sem("op_lo")
        sq_done, ss_ready, ss_read, sqrt_done = sem("sq_done"), sem("ss_ready"), sem("ss_read"), sem("sqrt_done")
        dve_done, act_done, pool_done = sem("dve_done"), sem("act_done"), sem("pool_done")
        lat_ready, angle_ready, trig_ready = sem("lat_ready"), sem("angle_ready"), sem("trig_ready")
        ckv_cols, vb_ready = sem("ckv_cols"), sem("vb_ready")
        b2_copied, rope_x, rope_rot, rope_read = sem("b2_copied"), sem("rope_x"), sem("rope_rot"), sem("rope_read")
        q_ready, k_ready, v_ready, kd_ready, kd_src = (sem("q_ready"), sem("k_ready"), sem("v_ready"), sem("kd_ready"),
                                                        sem("kd_src"))
        conv_ready, silu_ready = sem("conv_ready"), sem("silu_ready")
        stq, stv, s_done, m_done, p_done = sem("stq"), sem("stv"), sem("s_done"), sem("m_done"), sem("p_done")
        pn_done, pt_done, ptc, pv_done, att_hi, att_lo = (sem("pn_done"), sem("pt_done"), sem("ptc"),
                                                         sem("pv_done"), sem("att_hi"), sem("att_lo"))
        y_scaled, y_t, y_read, stored = sem("y_scaled"), sem("y_t"), sem("y_read"), sem("stored")

        block = ctx.enter_context(nc.Block())

        @block.sync
        def _(sp):
            sp.dma_start(ident[:, :], c_ident).then_inc(c_in, 16)
            rows = [(norm_mix, 2 * KT), (norm_ffn, 2 * KT), (final_norm, KT), (mla_g_q, 4), (mla_g_kv, 4),
                    (swa_b_qkv, QKV_B // P), (swa_b_o, KT)]
            at = 0
            for a, n in rows:
                sp.dma_start(praw[at:at + n, 0, :], a).then_inc(par_in, 16)
                at += n
            assert at == PC_END0
            for half in range(2):
                sp.dma_start(xin[:, half, :], x[half * P:(half + 1) * P, :]).then_inc(x_in, 16)
            sp.dma_start(praw[:, 1:5, :], ffn_conv_w[0:512, :].rearrange("(b r) c -> r b c", b=4)).then_inc(par_in, 16)
            sp.dma_start(praw[0:16, 5, :], ffn_conv_w[512:528, :]).then_inc(par_in, 16)
            sp.dma_start(praw[16:128, 5, :], ffn_conv_b[0:112, :]).then_inc(par_in, 16)
            sp.dma_start(praw[0:64, 6, :], ffn_conv_b[112:176, :]).then_inc(par_in, 16)

            def load(n, parts):
                s = n.mod(SLOTS)
                if n.i is not None or n.c >= SLOTS:
                    sp.wait_ge(lo_ready, (n - (SLOTS - 1)).v)
                for dst, src in parts(raw[s]):
                    sp.dma_start(dst, src).then_inc(raw_full[s], 16)

            def rows_cols(w, row, col):
                def parts(r):
                    return [(r[:, k * COLS:(k + 1) * COLS], w[row + k * P:row + (k + 1) * P, sl(col, COLS)])
                            for k in range(2)]
                return parts

            def stream(ph, w, kts, cols):
                per = kts // 2
                turn_chunks = per * len(cols(None))
                turns = ph.n // turn_chunks

                def turn_body(i):
                    for gi, col in enumerate(cols(i)):
                        for c in range(per):
                            load(Lin(ph.c0 + gi * per + c, turn_chunks, i), rows_cols(w, c * 2 * P, col))
                repeat(sp, 0, turns, turn_body)

            ph = PH["a_in"]
            for g in range(2):
                for c in range(8):
                    load(Lin(ph.c0 + g * 8 + c), rows_cols(mla_w_in, c * 2 * P, Lin(g * COLS)))
                    if g == 0 and c == 3:
                        sp.dma_start(rot[:, :], c_rot).then_inc(rope_in, 16)
                        sp.dma_start(invf[:, :], c_invf).then_inc(rope_in, 16)
                        sp.dma_start(posi[:, :], bass.AP(positions.tensor, 0, [[0, P], [1, T]])).then_inc(rope_in, 16)
                        sp.dma_start(onehot[:, :], c_onehot).then_inc(rope_in, 16)
                        sp.dma_start(relb[0:BUCKETS, :], rel_bias).then_inc(rope_in, 16)
            for c in range(2):
                def rope_parts(r, c=c):
                    v = r[:, :].rearrange("p (k d c) -> p k d c", k=8, d=2)
                    src = mla_w_in[c * 8 * P:(c + 1) * 8 * P, 2 * RANK:2 * RANK + ROPE].rearrange("(k p) c -> p k c", p=P)
                    return [(v[:, :, d, :], src) for d in range(2)]
                load(Lin(ph.c0 + 16 + c), rope_parts)
            ph = PH["a_q"]

            def q_body(i):
                for k in range(4):
                    def q_parts(r, k=k):
                        src = mla_w_qb[k * P:(k + 1) * P, sl(Lin(0, 4 * 192, i), 4 * 192)].rearrange("p (h c) -> p h c", h=4)
                        return [(r[:, 0:512].rearrange("p (h c) -> p h c", h=4), src[:, :, 0:NOPE]),
                                (r[:, 512:768].rearrange("p (h c) -> p h c", h=4), src[:, :, NOPE:192])]
                    load(Lin(ph.c0 + k, 4, i), q_parts)
            repeat(sp, 0, 4, q_body)
            stream(PH["a_kv"], mla_w_kvb, 4, lambda i: [Lin(0, 1024, i), Lin(512, 1024, i)])
            two_groups = lambda i: [Lin(0, 1024, i), Lin(COLS, 1024, i)]
            gate_val = lambda i: [Lin(0, COLS, i), Lin(FF, COLS, i)]
            stream(PH["a_out"], mla_w_o, KT, two_groups)
            stream(PH["f0_in"], ffn_w_in[0], KT, gate_val)
            stream(PH["f0_out"], ffn_w_out[0], FT, two_groups)
            ph = PH["b_in"]
            stream(Phase(ph.c0, 32, ph.g0, 4), swa_w_qkv, KT, two_groups)
            for c in range(8):
                load(Lin(ph.c0 + 32 + c), rows_cols(swa_w_qkv, c * 2 * P, Lin(4 * COLS)))
            stream(PH["b_out"], swa_w_o, KT, two_groups)
            stream(PH["f1_in"], ffn_w_in[1], KT, gate_val)
            stream(PH["f1_out"], ffn_w_out[1], FT, two_groups)
            for half in range(2):
                sp.wait_ge(y_read, 4 * (half + 1))
                sp.dma_start(out[half * P:(half + 1) * P, :], yt[:, half, :]).then_inc(stored, 16)
            sp.wait_ge(stored, 32)
            sp.wait_ge(bias_out, 16)

        @block.tensor
        def _(pe):
            mm = nc.tensor.matmul

            def feature_tile(bank, whi, wlo, op, start, stop, cols=T):
                def high():
                    return mm(ps[:, bank, 0:2 * T], whi, op, start=start, stop=stop)

                def low():
                    return mm(ps[:, bank, 0:T], wlo, op[:, 0, :], start=False, stop=False)
                if stop:
                    low()
                    return high()
                high()
                return low()

            def w_chunk(n, op, kt0, first, last, b0, tiles=(0, 1, 2, 3)):
                s = n.mod(SLOTS)
                pe.wait_ge(lo_ready, (n + 1).v)
                for j, m in enumerate(tiles):
                    for k in range(2):
                        c = k * COLS + m * P
                        z = feature_tile(b0 + j, w_hi[s][:, c:c + P], w_lo[s][:, c:c + P],
                                         op[:, kt0 + k, :, :], first and k == 0, last and k == 1)
                return z

            def token_chunk(n, op, kt0, first, last, bank, wcols):
                s = n.mod(SLOTS)
                for half in range(2):
                    t0 = half * P
                    for k in range(2):
                        hi, lo = op[:, kt0 + k, 0, t0:t0 + P], op[:, kt0 + k, 1, t0:t0 + P]
                        o = ps[:, bank + half, 0:T]
                        mm(o, hi, wcols(w_hi[s], k), start=first and k == 0, stop=False)
                        mm(o, hi, wcols(w_lo[s], k), start=False, stop=False)
                        z = mm(o, lo, wcols(w_hi[s], k), start=False, stop=last and k == 1)
                return z

            def banks_of(g):
                if g.i is not None or g.c >= 2:
                    pe.wait_ge(banks_free, (g - 1).v)
                return 4 * g.mod(2)

            def sum_squares(norm, src, bank, cols=False):
                pe.wait_ge(sq_done, NORM_SQ[norm])
                z = mm(ps[:, bank, 0:T], ones[:, :], src[:, :], start=True, stop=True)
                if cols:
                    for half in range(2):
                        z = mm(ps[:, bank, T + half:T + half + 1], src[:, half * P:(half + 1) * P],
                               ones[:, 0:1], start=True, stop=True)
                z.then_inc(ss_ready, 1)

            pe.wait_ge(c_in, 16)
            pe.wait_ge(par_in, 11 * 16)
            for b in range(7):
                n = (PC_END0, P, P, P, P, P, 64)[b]
                z = nc.tensor.transpose(ps[:, b // 4, (b % 4) * P:(b % 4) * P + n], praw[0:n, b, :], ident[0:n, 0:n])
            z.then_inc(par_t, 1)
            pe.wait_ge(x_in, 32)
            for j in (2, 3, 4, 5, 6, 7, 0, 1):
                if j == 0:
                    pe.wait_ge(par_ready, 1)
                for m in range(2):
                    for half in range(2):
                        z = nc.tensor.transpose(ps[:, j, m * T + half * P:m * T + (half + 1) * P],
                                                xin[:, half, (2 * j + m) * P:(2 * j + m + 1) * P], ident[:, :])
                z.then_inc(x_t, 1)

            ph = PH["a_in"]
            pe.wait_ge(h_in, 8)
            for g in range(2):
                for c in range(8):
                    if g == 0 and c % 2 == 0:
                        pe.wait_ge(op_lo, OP0["x"] + c // 2 + 1)
                    if g == 1 and c == 0:
                        pe.wait_ge(ss_read, 1)
                    w_chunk(Lin(ph.c0 + g * 8 + c), aop, 2 * c, c == 0, c == 7,
                            banks_of(Lin(g)) if c == 0 else 4 * (g % 2)).then_inc(chunk_used, 1)
                    if g == 0 and c == 5:
                        sum_squares(0, sqa, 4)
            banks_of(Lin(2))
            for c in range(2):
                n = Lin(ph.c0 + 16 + c)
                pe.wait_ge(lo_ready, (n + 1).v)
                for k in range(8):
                    z = feature_tile(0, w_hi[n.mod(SLOTS)][:, k * P:(k + 1) * P], w_lo[n.mod(SLOTS)][:, k * P:(k + 1) * P],
                                     aop[:, 8 * c + k, :, :], c == 0 and k == 0, c == 1 and k == 7)
                z.then_inc(chunk_used, 1)
            pe.wait_ge(brow_ready, 1)
            mm(ps[0:HEADS_B, 1, 0:384], relb[:, :], onehot[:, :], start=True, stop=True).then_inc(brow_t, 1)
            sum_squares(1, sqa, 2)
            sum_squares(2, sqb, 3, cols=True)
            pe.wait_ge(rope_in, 5 * 16)

            def rotate(k, bank, src):
                pe.wait_ge(rope_x, k + 1)
                mm(ps[:, bank, 0:T if k == 0 else 2 * T], rot[:, :], src,
                   start=True, stop=True).then_inc(rope_rot, 1)
            rotate(0, 6, cv[:, 2, :])

            ph = PH["a_q"]
            for g in range(4):
                pe.wait_ge(banks_free, ph.g0 + g)
                if g == 0:
                    pe.wait_ge(op_lo, OP0["lat"] + 1)
                    pe.wait_ge(ss_read, 3)
                    pe.wait_ge(brow_ready, 2)
                for c in range(4):
                    n = Lin(ph.c0 + 4 * g + c)
                    s = n.mod(SLOTS)
                    pe.wait_ge(lo_ready, (n + 1).v)
                    for m in range(6):
                        z = feature_tile(m, w_hi[s][:, m * P:(m + 1) * P], w_lo[s][:, m * P:(m + 1) * P],
                                         cop[:, c, :, :], c == 0, c == 3)
                    z.then_inc(chunk_used, 1)
                pe.wait_ge(rope_read, g + 1)
                rotate(1 + g, 6, cv[:, 2:4, :])

            ph = PH["a_kv"]
            pe.wait_ge(op_lo, OP0["lat"] + 2)
            pe.wait_ge(banks_free, ph.g0)
            pe.wait_ge(rope_read, 5)

            def kv_body(i):
                for gi in range(2):
                    g = Lin(ph.g0 + gi, 2, i)
                    b0 = banks_of(g)
                    for c in range(2):
                        n = Lin(ph.c0 + 2 * gi + c, 4, i)
                        w_chunk(n, cop, 4 + 2 * c, c == 0, c == 1, b0, tiles=(0, 2))
                        token_chunk(n, cop, 4 + 2 * c, c == 0, c == 1, b0 + 2,
                                    lambda w, k: w[:, k * COLS:(k + 1) * COLS].rearrange("p (h c) -> p h c", h=2)[:, :, P:2 * P]
                                    ).then_inc(chunk_used, 1)
            repeat(pe, 0, 4, kv_body)

            def attention(u0, units, scores, values):
                def score(u):
                    pe.wait_ge(stq, (u + u0 + 1).v)
                    if u.i is not None or u.c >= 2:
                        pe.wait_ge(m_done, (u + u0 - 1).v)
                    scores(u, 2 * u.mod(2)).then_inc(s_done, 1)

                def step(u, ahead=True):
                    pe.wait_ge(pn_done, (u + u0 + 1).v)
                    if u.i is not None or u.c + u0 >= 1:
                        pe.wait_ge(ptc, (u + u0).v)
                    for hh in range(2):
                        for blk in range(3):
                            z = nc.tensor.transpose(ps[:, 4 + hh, blk * P:(blk + 1) * P],
                                                    sm[:, u.mod(2), hh, blk * P:(blk + 1) * P], ident[:, :])
                    z.then_inc(pt_done, 1)
                    if ahead:
                        score(u + 2)
                    pe.wait_ge(ptc, (u + u0 + 1).v)
                    pe.wait_ge(stv, (u + u0 + 1).v)
                    if u.i is not None or u.c >= 2:
                        pe.wait_ge(att_lo, (u + u0 - 1).v)
                    values(u, 6 + u.mod(2)).then_inc(pv_done, 1)
                score(Lin(0))
                score(Lin(1))
                step(Lin(0))
                step(Lin(1))
                repeat(pe, 1, units // 2 - 1, lambda i: [step(Lin(k, 2, i)) for k in range(2)])
                step(Lin(units - 2), ahead=False)
                step(Lin(units - 1), ahead=False)

            def scores_a(u, bank):
                p = u.mod(2)
                for hh in range(2):
                    r = slice(64 * hh, 64 * hh + 64)
                    for q0, keys, o in ((0, P, 0), (P, T, P)):
                        o = ps[:, bank + hh, o:o + keys]
                        mm(o, st_q[:, p, hh, q0:q0 + P], kn[:, sl(u.times(2) + hh, 1), 0:keys], start=True, stop=False)
                        z = mm(o, st_r[r, p, q0:q0 + P], kr[r, 0:keys], start=False, stop=True)
                return z

            def values_a(u, bank):
                p = u.mod(2)
                for hh in range(2):
                    v = slice(hh * VDIM, (hh + 1) * VDIM)
                    mm(ps[:, bank, hh * T:(hh + 1) * T], st_v[:, p, 0, v], pts[:, hh, 0:T], start=True, stop=False)
                    z = mm(ps[:, bank, hh * T + P:(hh + 1) * T], st_v[:, p, 1, v], pts[:, hh, T:384],
                           start=False, stop=True)
                return z

            pe.wait_ge(banks_free, PH["a_kv"].g1)
            pe.wait_ge(k_ready, PH["a_kv"].ng)
            attention(0, UNITS_A, scores_a, values_a)

            def groups(ph, op, kts, first_wait, norm=None, rs_cols=False, end=None):
                per = kts // 2
                turns = (ph.n // (2 * per)) if end is None else end

                def body(i, first=False):
                    for gi in range(2):
                        g = Lin(ph.g0 + gi, 2, i)
                        if first and gi == 1 and norm is not None:
                            pe.wait_ge(ss_read, norm + 1)
                        b0 = banks_of(g)
                        for c in range(per):
                            if first and gi == 0:
                                first_wait(c)
                            w_chunk(Lin(ph.c0 + gi * per + c, 2 * per, i), op, 2 * c, c == 0, c == per - 1,
                                    b0).then_inc(chunk_used, 1)
                            if first and gi == 0 and c == 4 and norm is not None:
                                pe.wait_ge(banks_free, ph.g0)
                                sum_squares(norm, sqa, 4 - b0, rs_cols)
                body(None, True) if turns else None
                repeat(pe, 1, turns, body)

            def att_wait(done):
                return lambda c: pe.wait_ge(att_lo, done) if c == 0 else None

            def op_wait(base):
                return lambda c: pe.wait_ge(op_lo, base + c // 2 + 1) if c % 2 == 0 else None

            groups(PH["a_out"], oop, KT, att_wait(UNITS_A))
            groups(PH["f0_in"], aop, KT, op_wait(OP0["a_out"]), norm=3)
            groups(PH["f0_out"], gop, FT, op_wait(OP0["f0_in"]))

            ph = PH["b_in"]
            groups(ph, aop, KT, op_wait(OP0["f0_out"]), norm=4, rs_cols=True, end=2)
            b0 = banks_of(Lin(ph.g0 + 4))
            for c in range(8):
                n = Lin(ph.c0 + 32 + c)
                w_chunk(n, aop, 2 * c, c == 0, c == 7, b0, tiles=(0, 1))
                token_chunk(n, aop, 2 * c, c == 0, c == 7, b0 + 2,
                            lambda w, k: w[:, k * COLS + T:(k + 1) * COLS]).then_inc(chunk_used, 1)

            def scores_b(u, bank):
                p = u.mod(2)
                for hh in range(2):
                    r = slice(64 * hh, 64 * hh + 64)
                    for q0, keys, o in ((0, P, 0), (P, T, P)):
                        z = mm(ps[:, bank + hh, o:o + keys], st_q[r, p, 0, q0:q0 + P], st_q[r, p, 1, 0:keys],
                               start=True, stop=True)
                return z

            def values_b(u, bank):
                p = u.mod(2)
                for hh in range(2):
                    r = slice(64 * hh, 64 * hh + 64)
                    mm(ps[r, bank, 0:T], st_vb[:, p, 0, :], pts[:, hh, 0:T], start=True, stop=False)
                    z = mm(ps[r, bank, P:T], st_vb[:, p, 1, :], pts[:, hh, T:384], start=False, stop=True)
                return z

            pe.wait_ge(banks_free, ph.g1)
            attention(UNITS_A, UNITS_B, scores_b, values_b)
            groups(PH["b_out"], oop, KT, att_wait(UNITS_A + UNITS_B))
            groups(PH["f1_in"], aop, KT, op_wait(OP0["b_out"]), norm=5)
            groups(PH["f1_out"], gop, FT, op_wait(OP0["f1_in"]))

            pe.wait_ge(banks_free, PH["f1_out"].g1)
            pe.wait_ge(sq_done, NORM_SQ[6])
            for half in range(2):
                z = mm(ps[:, 0, T + half:T + half + 1], sqa[:, half * P:(half + 1) * P], ones[:, 0:1],
                       start=True, stop=True)
            z.then_inc(ss_ready, 1)
            for half in range(2):
                for q in range(4):
                    if half == 0:
                        pe.wait_ge(y_scaled, q + 1)
                    if q == 0:
                        pe.wait_ge(y_read, 4 * half) if half else pe.wait_ge(ss_read, 7)
                    for j in range(4):
                        z = nc.tensor.transpose(ps[:, 4 * (1 - half) + q, j * P:(j + 1) * P],
                                                h[:, 4 * q + j, half * P:(half + 1) * P], ident[:, :])
                    z.then_inc(y_t, 1)

        @block.scalar
        def _(act):
            f = nc.scalar.activation
            done = Steps(act, act_done)

            def split(n):
                if n.i is None and n.c >= CHUNKS:
                    return
                s = n.mod(SLOTS)
                act.wait_ge(raw_full[s], (n.over(SLOTS).times(16 * DMAS) + 16 * DMAS).v)
                if n.i is not None or n.c >= SLOTS:
                    act.wait_ge(chunk_used, (n - (SLOTS - 1)).v)
                f(w_hi[s][:, :], raw[s][:, :], ACT.Copy).then_inc(hi_ready, 1)

            def b_half(g, last_chunk, tiles=4, bias=None):
                act.wait_ge(chunk_used, (last_chunk + 1).v)
                if g.i is not None or g.c >= 1:
                    act.wait_ge(banks_free, g.v)
                b0 = 4 * g.mod(2)
                if bias is None:
                    f(tb[:, 0:tiles, :], ps[:, b0:b0 + tiles, T:2 * T], ACT.Copy).then_inc(b_copied, 1)
                    return
                for j in range(tiles):
                    z = f(tb[:, j, :], ps[:, b0 + j, T:2 * T], ACT.Identity, bias=bias(j))
                z.then_inc(b_copied, 1)

            def op_high(k, dst):
                act.wait_ge(t_ready, (k + 1).v)
                f(dst, cv[:, :, :], ACT.Copy).then_inc(op_hi, 1)

            def norm_root(norm, dst, bank, width, scale=1.0, cols=None):
                act.wait_ge(ss_ready, norm + 1)
                act.wait_ge(const_set, 1)
                z = f(dst, ps[:, bank, 0:T], ACT.Sqrt, bias=eps[:, 1:2] if scale != 1.0 else eps[:, 0:1],
                      scale=1.0 / width / scale ** 2)
                if cols is not None:
                    z = f(rs_col[:, cols:cols + 2], ps[:, bank, T:T + 2], ACT.Sqrt, bias=eps[:, 0:1], scale=1.0 / width)
                z.then_inc(ss_read, 1)

            act.wait_ge(par_t, 1)
            f(par[:, 0:PC_END0], ps[:, 0, 0:PC_END0], ACT.Copy)
            f(par[:, P:512], ps[:, 0, P:512], ACT.Copy)
            f(par[:, 512:PC_END], ps[:, 1, 0:PC_END - 512], ACT.Copy).then_inc(par_ready, 1)
            order = (2, 3, 4, 5, 6, 7, 0, 1)
            for n, j in enumerate(order):
                act.wait_ge(x_t, n + 1)
                f(h[:, 2 * j:2 * j + 2, :], ps[:, j, :].rearrange("p (m t) -> p m t", m=2), ACT.Copy).then_inc(h_in, 1)
            for c in range(SLOTS):
                split(Lin(c))
            for q in range(4):
                op_high(Lin(OP0["x"] + q), aop[:, 4 * q:4 * q + 4, 0, :])
            for c in range(SLOTS, AHEAD):
                split(Lin(c))
            norm_root(0, rs[:, :], 4, D)

            ph = PH["a_in"]
            for c in range(AHEAD, ph.n + AHEAD):
                split(Lin(c))
                if c == AHEAD + 1:
                    act.wait_ge(angle_ready, 1)
                    f(sin[:, :], sin[:, :], ACT.Sin)
                    f(cos[:, :], cos[:, :], ACT.Sin).then_inc(trig_ready, 1)
                if c in (11, 19):
                    g = (c - 11) // 8
                    b_half(Lin(g), Lin(8 * g + 7))
                    op_high(Lin(OP0["lat"] + g), cop[:, 4 * g:4 * g + 4, 0, :])
                if c == 21:
                    b_half(Lin(2), Lin(17), tiles=1)
                    act.wait_ge(brow_t, 1)
                    f(brow[:, :], ps[0:HEADS_B, 1, 0:384], ACT.Copy).then_inc(brow_ready, 1)
                    act.wait_ge(ss_ready, 2)
                    norm_root(1, rsq[:, :], 2, RANK, scale=(NOPE + ROPE) ** -0.5)
                    norm_root(2, rsk[:, :], 3, RANK, cols=0)

            ph = PH["a_q"]

            for g in range(4):
                act.wait_ge(rope_read, g + 1)
                act.wait_ge(chunk_used, ph.c0 + 4 * g + 4)
                act.wait_ge(banks_free, ph.g0 + g)
                f(tb[:, 0:4, :], ps[:, 0:4, T:2 * T], ACT.Copy).then_inc(b_copied, 1)
                f(cv[:, 0:2, :], ps[:, 4:6, T:2 * T], ACT.Copy).then_inc(b2_copied, 1)
                for c in range(4):
                    split(Lin(ph.c0 + AHEAD + 4 * g + c))

            ph = PH["a_kv"]

            def kv_body(i):
                for gi in range(2):
                    g = Lin(ph.g0 + gi, 2, i)
                    b0 = 4 * g.mod(2)
                    act.wait_ge(chunk_used, Lin(ph.c0 + 2 * gi + 2, 4, i).v)
                    act.wait_ge(ckv_cols, 1)
                    for half in range(2):
                        f(va[:, half, sl(Lin(T * gi, 2 * T, i), T)], ps[:, b0 + 2 + half, 0:T], ACT.Copy,
                          scale=rs_col[:, half:half + 1]).then_inc(v_ready, 1)
                    b_half(g, Lin(ph.c0 + 2 * gi + 1, 4, i), tiles=2)
                for c in range(4):
                    split(Lin(ph.c0 + AHEAD + c, 4, i))
            repeat(act, 0, 3, kv_body)
            for gi in range(2):
                g = Lin(ph.g0 + 6 + gi)
                b0 = 4 * g.mod(2)
                act.wait_ge(chunk_used, ph.c0 + 14 + 2 * gi)
                for half in range(2):
                    f(va[:, half, T * (6 + gi):T * (7 + gi)], ps[:, b0 + 2 + half, 0:T], ACT.Copy,
                      scale=rs_col[:, half:half + 1]).then_inc(v_ready, 1)
                b_half(g, Lin(ph.c0 + 13 + 2 * gi), tiles=2)

            def attention(u0, units, sinks, out_high):
                def exps(u):
                    p = u.mod(2)
                    act.wait_ge(m_done, (u + u0 + 1).v)
                    for hh in range(2):
                        for q, cols in ((0, slice(0, P)), (1, slice(P, 384))):
                            k = 2 * hh + q
                            z = f(sm[:, p, hh, cols], sm[:, p, hh, cols], ACT.Exp, bias=nm[:, p, k:k + 1],
                                  accum_out=ls[:, p, k:k + 1])
                    if sinks:
                        for hh in range(2):
                            z = f(es[:, p, 2 * hh:2 * hh + 2], nm[:, p, 2 * hh:2 * hh + 2], ACT.Exp,
                                  bias=st_s[:, p, hh:hh + 1])
                    z.then_inc(p_done, 1)

                def pt_copy(u):
                    act.wait_ge(pt_done, (u + u0 + 1).v)
                    if u.i is not None or u.c + u0 >= 1:
                        act.wait_ge(pv_done, (u + u0).v)
                    f(pts[:, :, :], ps[:, 4:6, 0:384], ACT.Copy).then_inc(ptc, 1)

                def o_high(u):
                    act.wait_ge(pv_done, (u + u0 + 1).v)
                    out_high(u).then_inc(att_hi, 1)

                exps(Lin(0))
                exps(Lin(1))
                pt_copy(Lin(0))

                def step(u, ahead=True):
                    if ahead:
                        exps(u + 1)
                    pt_copy(u)
                    o_high(u - 1)
                repeat(act, 0, units // 2 - 1, lambda i: [step(Lin(1 + k, 2, i)) for k in range(2)])
                step(Lin(units - 1), ahead=False)
                o_high(Lin(units - 1))

            attention(0, UNITS_A, False,
                      lambda u: f(oop[:, sl(u.times(2), 2), 0, :],
                                  ps[:, 6 + u.mod(2), :].rearrange("p (m t) -> p m t", m=2), ACT.Copy))
            for c in range(SLOTS, AHEAD):
                split(Lin(PH["a_out"].c0 + c))

            def residual(ph, kts, k0, norm_next, bias=None, last=False):
                per = kts // 2
                turns = ph.n // (2 * per)

                def body(i):
                    for j in range(2 * per):
                        split(Lin(ph.c0 + AHEAD + j, 2 * per, i))
                        gi, at = divmod(j, per)
                        if at == per - 5:
                            b_half(Lin(ph.g0 + gi, 2, i), Lin(ph.c0 + gi * per + per - 1, 2 * per, i),
                                   bias=bias and (lambda t: par[:, sl(Lin(bias + 4 * gi + t, 8, i), 1)]))
                        if at == per - 3 and k0 is not None:
                            op_high(Lin(k0 + gi, 2, i), aop[:, sl(Lin(4 * gi, 8, i), 4), 0, :])
                if last:
                    for t in range(turns):
                        body_static(ph, per, t, k0, bias)
                else:
                    repeat(act, 0, turns, body)

            def body_static(ph, per, t, k0, bias):
                for j in range(2 * per):
                    split(Lin(ph.c0 + AHEAD + j + 2 * per * t))
                    gi, at = divmod(j, per)
                    if at == per - 5:
                        b_half(Lin(ph.g0 + gi + 2 * t), Lin(ph.c0 + gi * per + per - 1 + 2 * per * t))

            def ffn_in(ph, k0):
                def body(i):
                    for j in range(16):
                        split(Lin(ph.c0 + AHEAD + j, 16, i))
                        if j in (3, 11):
                            gi = j // 8
                            b_half(Lin(ph.g0 + gi, 2, i), Lin(ph.c0 + 8 * gi + 7, 16, i))
                        if j == 8:
                            act.wait_ge(conv_ready, Lin(k0 - CONV0[k0] + 1, 1, i).v)
                            f(cg[:, :, :], cg[:, :, :], ACT.Silu).then_inc(silu_ready, 1)
                        if j == 14:
                            op_high(Lin(k0, 1, i), gop[:, sl(Lin(0, 4, i), 4), 0, :])
                repeat(act, 0, 11, body)

            residual(PH["a_out"], KT, OP0["a_out"], 3)
            norm_root(3, rs[:, :], 4 - 4 * (PH["f0_in"].g0 % 2), D)
            ffn_in(PH["f0_in"], OP0["f0_in"])
            residual(PH["f0_out"], FT, OP0["f0_out"], 4)
            norm_root(4, rs[:, :], 4 - 4 * (PH["b_in"].g0 % 2), D, cols=2)

            ph = PH["b_in"]

            def b_body(i):
                for j in range(16):
                    split(Lin(ph.c0 + AHEAD + j, 16, i))
                    if j in (3, 11):
                        gi = j // 8
                        b_half(Lin(ph.g0 + gi, 2, i), Lin(ph.c0 + 8 * gi + 7, 16, i))
            repeat(act, 0, 2, b_body)
            for j in range(SLOTS):
                split(Lin(ph.c1 + j))
            b_half(Lin(ph.g0 + 4), Lin(ph.c1 - 1), tiles=2)
            act.wait_ge(kd_src, 1)
            for kv in range(KV_B):
                for d in range(2):
                    z = f(kd[64 * d:64 * d + 64, kv, :], cv[64 * (kv % 2):64 * (kv % 2) + 64, kv // 2, :], ACT.Copy)
            z.then_inc(kd_ready, 1)
            attention(UNITS_A, UNITS_B, True,
                      lambda u: f(oop[:, sl(u, 1), 0, :], ps[:, 6 + u.mod(2), 0:T], ACT.Copy))
            for c in range(SLOTS, AHEAD):
                split(Lin(PH["b_out"].c0 + c))
            residual(PH["b_out"], KT, OP0["b_out"], 5, bias=PC_BO)
            norm_root(5, rs[:, :], 4 - 4 * (PH["f1_in"].g0 % 2), D)
            ffn_in(PH["f1_in"], OP0["f1_in"])
            residual(PH["f1_out"], FT, None, 6, last=True)

            act.wait_ge(ss_ready, 7)
            f(rs_col[:, 4:6], ps[:, 0, T:T + 2], ACT.Sqrt, bias=eps[:, 0:1], scale=1.0 / D).then_inc(ss_read, 1)
            act.wait_ge(sqrt_done, 1)
            for half in range(2):
                for q in range(4):
                    act.wait_ge(y_t, 4 * half + q + 1)
                    f(yt[:, half, q * 512:(q + 1) * 512], ps[:, 4 * (1 - half) + q, :], ACT.Copy,
                      scale=rs_col[:, 4 + half:5 + half]).then_inc(y_read, 1)

        @block.vector
        def _(dve):
            v = nc.vector
            done = Steps(dve, dve_done)

            def split(n):
                if n.i is None and n.c >= CHUNKS:
                    return
                s = n.mod(SLOTS)
                dve.wait_ge(hi_ready, (n + 1).v)
                v.tensor_tensor(w_lo[s][:, :], raw[s][:, :], w_hi[s][:, :].bitcast(F32), ALU.subtract).then_inc(lo_ready, 1)

            def spread(a, tiles):
                return bass.AP(a.tensor, a.offset, [list(a.ap[0]), [0, tiles], [1, T]])

            def col(n):
                return par[:, sl(n, 1)]

            def gains(k, src, gain, tiles=4):
                if k.i is not None or k.c >= 1:
                    dve.wait_ge(op_lo, k.v)
                for j in range(tiles):
                    z = v.tensor_scalar(cv[:, j, :], src(j), col(gain + j), None, ALU.mult)
                z.then_inc(t_ready, 1)

            def op_low(k, dst, hi):
                dve.wait_ge(op_hi, (k + 1).v)
                v.tensor_tensor(dst, cv[:, :, :], hi.bitcast(F32), ALU.subtract).then_inc(op_lo, 1)

            def operand(k, op, tile0):
                op_low(k, op[:, sl(tile0, 4), 1, :], op[:, sl(tile0, 4), 0, :])

            dve.wait_ge(par_ready, 1)
            dve.wait_ge(h_in, 8)
            for q in range(4):
                if q == 0:
                    gains(Lin(0), lambda j: h[:, j, :], Lin(PC_MIX))
                    for c in range(SLOTS):
                        split(Lin(c))
                else:
                    gains(Lin(q), lambda j: h[:, 4 * q + j, :], Lin(PC_MIX + 4 * q))
                operand(Lin(q), aop, Lin(4 * q))
            for c in range(SLOTS, AHEAD):
                split(Lin(c))

            def inverse(norm, dst):
                dve.wait_ge(ss_read, norm + 1)
                for d in dst:
                    done(v.reciprocal(d, d))
                done.sync()
            inverse(0, [rs[:, :]])

            def angles():
                dve.wait_ge(rope_in, 5 * 16)
                done(v.tensor_copy(turn[:, :], posi[:, :]))
                done.sync()
                done(v.tensor_scalar(ang[:, :], turn[:, :], invf[:, 0:1], None, ALU.mult))
                done.sync()
                magic = 1.5 * 2.0 ** 23
                done(v.tensor_scalar(turn[:, :], ang[:, :], 1.0 / (2 * math.pi), magic, ALU.mult, ALU.add))
                done.sync()
                done(v.tensor_scalar(turn[:, :], turn[:, :], magic, None, ALU.subtract))
                done.sync()
                c1 = 6.28125
                c2 = float(np.float32(np.round((2 * math.pi - c1) * 2 ** 20) / 2 ** 20))
                c3 = 2 * math.pi - c1 - c2
                for c in (c1, c2, c3):
                    done(v.scalar_tensor_tensor(ang[:, :], turn[:, :], -c, ang[:, :], ALU.mult, ALU.add))
                    done.sync()
                lim = 3.1415925
                done(v.tensor_scalar(sin[:, :], ang[:, :], lim, -lim, ALU.min, ALU.max))
                done(v.tensor_scalar(cos[:, :], ang[:, :], math.pi / 2, None, ALU.add))
                done.sync()
                done(v.tensor_scalar(turn[:, :], cos[:, :], math.pi, -2 * math.pi, ALU.is_gt, ALU.mult))
                done.sync()
                done(v.tensor_tensor(cos[:, :], cos[:, :], turn[:, :], ALU.add))
                done.sync()
                v.tensor_scalar(cos[:, :], cos[:, :], lim, -lim, ALU.min, ALU.max).then_inc(angle_ready, 1)

            def sum_banks(g, tiles, dst, src=None):
                dve.wait_ge(b_copied, (g + 1).v)
                b0 = 4 * g.mod(2)
                return v.tensor_tensor(dst, ps[:, b0:b0 + tiles, 0:T], tb[:, 0:tiles, :], ALU.add)

            def over_rms(g, tiles, dst, r):
                sum_banks(g, tiles, dst).then_inc(banks_free, 1)
                dve.wait_ge(banks_free, (g + 1).v)
                return v.tensor_tensor(dst, dst, spread(r[:, :], tiles), ALU.mult)

            def scaled(g, tiles, dst, r):
                done(over_rms(g, tiles, dst, r))
                done.sync()

            ph = PH["a_in"]
            for c in range(AHEAD, ph.n + AHEAD):
                split(Lin(c))
                if c == AHEAD:
                    angles()
                if c in (11, 19):
                    g = (c - 11) // 8
                    if g == 1:
                        dve.wait_ge(sq_done, SQ0["lat"] + 1)
                    over_rms(Lin(g), 4, cg[:, :, :], rs).then_inc(lat_ready, 1)
                    dve.wait_ge(lat_ready, g + 1)
                    gains(Lin(OP0["lat"] + g), lambda j: cg[:, j, :], Lin(PC_GQ if g == 0 else PC_GKV))
                    operand(Lin(OP0["lat"] + g), cop, Lin(4 * g))
                if c == 21:
                    dve.wait_ge(trig_ready, 1)
                    dve.wait_ge(op_lo, OP0["lat"] + 2)
                    g = Lin(2)
                    sum_banks(g, 1, cv[:, 2:3, :]).then_inc(banks_free, 1)
                    dve.wait_ge(banks_free, 3)
                    v.tensor_tensor(cv[:, 2, :], cv[:, 2, :], rs[:, :], ALU.mult).then_inc(rope_x, 1)
                    dve.wait_ge(rope_x, 1)
                    inverse(1, [rsq[:, :]])
                    inverse(2, [rsk[:, :]])
                    v.reciprocal(rs_col[:, 0:2], rs_col[:, 0:2]).then_inc(ckv_cols, 1)
                    dve.wait_ge(rope_rot, 1)
                    done(v.tensor_tensor(tb[:, 3, :], ps[:, 6, 0:T], sin[:, :], ALU.mult))
                    done(v.tensor_tensor(cv[:, 2, :], cv[:, 2, :], cos[:, :], ALU.mult))
                    done.sync()
                    v.tensor_tensor(kr[:, :], cv[:, 2, :], tb[:, 3, :], ALU.add).then_inc(rope_read, 1)

            ph = PH["a_q"]
            for g in range(4):
                dve.wait_ge(b_copied, ph.g0 + g + 1)
                done(v.tensor_tensor(cg[:, :, :], ps[:, 0:4, 0:T], tb[:, :, :], ALU.add))
                dve.wait_ge(b2_copied, g + 1)
                v.tensor_tensor(cv[:, 2:4, :], ps[:, 4:6, 0:T], cv[:, 0:2, :], ALU.add).then_inc(banks_free, 1)
                done.sync()
                v.tensor_tensor(qn[:, 4 * g:4 * g + 4, :], cg[:, :, :], spread(rsq[:, :], 4), ALU.mult).then_inc(q_ready, 1)
                dve.wait_ge(banks_free, ph.g0 + g + 1)
                v.tensor_tensor(cv[:, 2:4, :], cv[:, 2:4, :], spread(rsq[:, :], 2), ALU.mult).then_inc(rope_x, 1)
                dve.wait_ge(rope_x, g + 2)
                dve.wait_ge(rope_rot, g + 2)
                dve.wait_ge(q_ready, 2 * g + 1)
                done(v.tensor_tensor(cg[:, 2:4, :], ps[:, 6, :].rearrange("p (m t) -> p m t", m=2),
                                     spread(sin[:, :], 2), ALU.mult))
                v.tensor_tensor(cg[:, 0:2, :], cv[:, 2:4, :], spread(cos[:, :], 2), ALU.mult).then_inc(rope_read, 1)
                dve.wait_ge(rope_read, g + 2)
                if g == 0:
                    dve.wait_ge(bias_out, 16)
                v.tensor_tensor(qr[:, 2 * g:2 * g + 2, :], cg[:, 0:2, :], cg[:, 2:4, :], ALU.add).then_inc(q_ready, 1)
                dve.wait_ge(q_ready, 2 * g + 2)
                for c in range(4):
                    split(Lin(ph.c0 + AHEAD + 4 * g + c))

            ph = PH["a_kv"]

            def kv_groups(i, t=0):
                for gi in range(2):
                    k = Lin(gi + 2 * t, 2, i)
                    g = k + ph.g0
                    sum_banks(g, 2, cg[:, 0:2, :]).then_inc(banks_free, 1)
                    dve.wait_ge(banks_free, (g + 1).v)
                    v.tensor_tensor(kn[:, sl(k.times(2), 2), :], cg[:, 0:2, :], spread(rsk[:, :], 2), ALU.mult).then_inc(k_ready, 1)
                    dve.wait_ge(k_ready, (k + 1).v)

            def kv_body(i):
                kv_groups(i)
                for c in range(4):
                    split(Lin(ph.c0 + AHEAD + c, 4, i))
            repeat(dve, 0, 3, kv_body)
            kv_groups(None, 3)

            def attention(u0, units, loop_steps, masked, sinks, out_low):
                def maxes(u):
                    p, bank = u.mod(2), 2 * u.mod(2)
                    dve.wait_ge(s_done, (u + u0 + 1).v)
                    if u.i is not None or u.c >= 2:
                        dve.wait_ge(pt_done, (u + u0 - 1).v)
                    v.memset(fence[:, p:p + 1], 0.0)
                    for hh in range(2):
                        for q, cols in ((0, slice(0, P)), (1, slice(P, 384))):
                            k = 2 * hh + q
                            start = st_s[:, p, hh:hh + 1] if sinks else -3.0e38
                            done(v.tensor_tensor_reduce(out=sm[:, p, hh, cols], in0=ps[:, bank + hh, cols],
                                                        in1=masked(p, hh, q), scale=1.0, scalar=start,
                                                        op0=ALU.add, op1=ALU.max, accum_out=ri[:, p, k:k + 1]))
                    done.sync()
                    v.tensor_scalar(nm[:, p, :], ri[:, p, :], -1.0, None, ALU.mult).then_inc(m_done, 1)

                def normal(u):
                    p = u.mod(2)
                    dve.wait_ge(p_done, (u + u0 + 1).v)
                    if sinks:
                        done(v.tensor_tensor(ls[:, p, :], ls[:, p, :], es[:, p, :], ALU.add))
                        done.sync()
                    done(v.reciprocal(ri[:, p, :], ls[:, p, :]))
                    done.sync()
                    for hh in range(2):
                        for q, cols in ((0, slice(0, P)), (1, slice(P, 384))):
                            k = 2 * hh + q
                            z = v.tensor_scalar(sm[:, p, hh, cols], sm[:, p, hh, cols], ri[:, p, k:k + 1], None, ALU.mult)
                    z.then_inc(pn_done, 1)

                def low(u):
                    dve.wait_ge(att_hi, (u + u0 + 1).v)
                    out_low(u).then_inc(att_lo, 1)

                maxes(Lin(0))
                maxes(Lin(1))
                normal(Lin(0))

                def step(u, ahead=True):
                    if ahead:
                        maxes(u + 1)
                    normal(u)
                    low(u - 1)
                done.loop(0, units // 2 - 1, loop_steps, lambda i: [step(Lin(1 + k, 2, i)) for k in range(2)])
                step(Lin(units - 1), ahead=False)
                low(Lin(units - 1))

            dve.wait_ge(mask_in, 16)
            attention(0, UNITS_A, 10, lambda p, hh, q: mask[:, 0:P] if q == 0 else mask[:, P:384], False,
                      lambda u: v.tensor_tensor(oop[:, sl(u.times(2), 2), 1, :],
                                                ps[:, 6 + u.mod(2), :].rearrange("p (m t) -> p m t", m=2),
                                                oop[:, sl(u.times(2), 2), 0, :].bitcast(F32), ALU.subtract))
            for c in range(SLOTS, AHEAD):
                split(Lin(PH["a_out"].c0 + c))

            def add_residual(g, tile0):
                dve.wait_ge(b_copied, (g + 1).v)
                b0 = 4 * g.mod(2)
                hh = h[:, sl(tile0, 4), :]
                done(v.tensor_tensor(hh, hh, ps[:, b0:b0 + 4, 0:T], ALU.add))
                done.sync()
                v.tensor_tensor(hh, hh, tb[:, :, :], ALU.add).then_inc(banks_free, 1)
                dve.wait_ge(banks_free, (g + 1).v)

            def residual(ph, kts, k0, gain, static=False):
                per = kts // 2
                turns = ph.n // (2 * per)

                def body(i, t=0):
                    for j in range(2 * per):
                        split(Lin(ph.c0 + AHEAD + j + 2 * per * t, 2 * per, i))
                        gi, at = divmod(j, per)
                        tile0 = Lin(4 * gi + 8 * t, 8, i)
                        if at == per - 5:
                            add_residual(Lin(ph.g0 + gi + 2 * t, 2, i), tile0)
                        if at == per - 4 and k0 is not None:
                            gains(Lin(k0 + gi, 2, i), lambda m: h[:, sl(tile0 + m, 1), :], Lin(gain + 4 * gi, 8, i))
                        if at == per - 2 and k0 is not None:
                            operand(Lin(k0 + gi, 2, i), aop, tile0)
                if static:
                    for t in range(turns):
                        body(None, t)
                else:
                    done.loop(0, turns, 2, body)

            def conv(layer, dst, tile0):
                w = PC_CONVW + layer * 3 * CT
                for m in range(4):
                    done(v.tensor_scalar(dst[:, m, :], up[:, m, 2:T + 2], col(tile0 + (w + 2 * CT + m)),
                                         col(tile0 + (PC_CONVB + layer * CT + m)), ALU.mult, ALU.add))
                done.sync()
                for tap in (1, 0):
                    for m in range(4):
                        z = v.scalar_tensor_tensor(dst[:, m, :], up[:, m, tap:T + tap], col(tile0 + (w + tap * CT + m)),
                                                   dst[:, m, :], ALU.mult, ALU.add)
                        if tap:
                            done(z)
                    if tap:
                        done.sync()
                return z

            def ffn_in(ph, layer, k0):
                def body(i):
                    for j in range(16):
                        split(Lin(ph.c0 + AHEAD + j, 16, i))
                        gi = j // 8
                        if j in (3, 11):
                            g = Lin(ph.g0 + gi, 2, i)
                            if gi == 1:
                                dve.wait_ge(conv_ready, Lin(k0 - CONV0[k0] + 1, 1, i).v)
                            scaled(g, 4, up[:, :, 2:T + 2], rs)
                        if j == 5:
                            conv(layer, cg, Lin(0, 4, i)).then_inc(conv_ready, 1)
                        if j == 12:
                            done(conv(layer, cv, Lin(FT, 4, i)))
                            done.sync()
                        if j == 13:
                            dve.wait_ge(silu_ready, Lin(k0 - CONV0[k0] + 1, 1, i).v)
                            v.tensor_tensor(cv[:, :, :], cv[:, :, :], cg[:, :, :], ALU.mult).then_inc(t_ready, 1)
                        if j == 15:
                            operand(Lin(k0, 1, i), gop, Lin(0, 4, i))
                            dve.wait_ge(op_lo, Lin(k0 + 1, 1, i).v)
                done.loop(0, 11, 19, body)

            residual(PH["a_out"], KT, OP0["a_out"], PC_FFN)
            inverse(3, [rs[:, :]])
            dve.wait_ge(op_lo, OP0["a_out"] + 4)
            dve.wait_ge(const_set, 2)
            ffn_in(PH["f0_in"], 0, OP0["f0_in"])
            residual(PH["f0_out"], FT, OP0["f0_out"], PC_MIX + KT)
            inverse(4, [rs[:, :], rs_col[:, 2:4]])

            ph = PH["b_in"]

            def b_body(i):
                for j in range(16):
                    split(Lin(ph.c0 + AHEAD + j, 16, i))
                    if j in (3, 11):
                        gi = j // 8
                        scaled(Lin(ph.g0 + gi, 2, i), 4, cg[:, :, :], rs)
                        for m in range(4):
                            done(v.tensor_scalar(qb[:, sl(Lin(4 * gi + m, 8, i), 1), :], cg[:, m, :],
                                                 col(Lin(PC_BQKV + 4 * gi + m, 8, i)), DH ** -0.5, ALU.add, ALU.mult))
                        done.sync()
            dve.wait_ge(op_lo, OP0["f0_out"] + 4)
            done.loop(0, 2, 10, b_body)
            for j in range(SLOTS):
                split(Lin(ph.c1 + j))
            scaled(Lin(ph.g0 + 4), 2, cg[:, 0:2, :], rs)
            for m in range(2):
                z = v.tensor_scalar(cv[:, m, :], cg[:, m, :], col(Lin(PC_BQKV + KT + m)), None, ALU.add)
            z.then_inc(kd_src, 1)
            b0 = 4 * ((ph.g0 + 4) % 2)
            dve.wait_ge(swa_in, 32)
            for half in range(2):
                v.scalar_tensor_tensor(vb[:, half, :], ps[:, b0 + 2 + half, 0:T], rs_col[:, 2 + half:3 + half],
                                       bvrow[:, :], ALU.mult, ALU.add).then_inc(vb_ready, 1)
            attention(UNITS_A, UNITS_B, 12,
                      lambda p, hh, q: st_b[:, p, hh, P:T] if q == 0 else st_b[:, p, hh, :],
                      True,
                      lambda u: v.tensor_tensor(oop[:, sl(u, 1), 1, :], ps[:, 6 + u.mod(2), 0:T],
                                                oop[:, sl(u, 1), 0, :].bitcast(F32), ALU.subtract))
            for c in range(SLOTS, AHEAD):
                split(Lin(PH["b_out"].c0 + c))
            residual(PH["b_out"], KT, OP0["b_out"], PC_FFN + KT)
            inverse(5, [rs[:, :]])
            dve.wait_ge(op_lo, OP0["b_out"] + 4)
            ffn_in(PH["f1_in"], 1, OP0["f1_in"])
            residual(PH["f1_out"], FT, None, None, static=True)

            dve.wait_ge(sq_done, NORM_SQ[6])
            for m in range(KT):
                z = v.tensor_scalar(h[:, m, :], h[:, m, :], col(Lin(PC_FIN + m)), None, ALU.mult)
                if m % 4 == 3:
                    z.then_inc(y_scaled, 1)
            dve.wait_ge(ss_read, 7)
            v.reciprocal(rs_col[:, 4:6], rs_col[:, 4:6]).then_inc(sqrt_done, 1)

        @block.gpsimd
        def _(pool):
            g_ = nc.gpsimd
            done = Steps(pool, pool_done)
            g_.memset(ones[:, :], 1.0)
            g_.memset(eps[:, 0:1], EPS)
            g_.memset(sqa[:, :], 0.0)
            g_.memset(eps[:, 1:2], EPS * (NOPE + ROPE)).then_inc(const_set, 1)

            def squares(src, tmp, acc, k):
                done(g_.tensor_tensor(tmp, src, src, ALU.mult))
                done.sync()
                for j in range(4):
                    z = g_.tensor_tensor(acc[:, :], acc[:, :], tmp[:, j, :], ALU.add)
                    if j < 3:
                        done(z)
                        done.sync()
                z.then_inc(sq_done, 1)

            pool.wait_ge(h_in, 8)
            pool.wait_ge(const_set, 1)
            for q in range(4):
                squares(h[:, 4 * q:4 * q + 4, :], up[:, :, 0:T], sqa, q)
                pool.wait_ge(sq_done, q + 1)
            pool.wait_ge(ss_ready, 1)
            done(g_.memset(sqa[:, :], 0.0))
            done(g_.memset(sqb[:, :], 0.0))
            done.sync()
            for g in range(2):
                pool.wait_ge(lat_ready, g + 1)
                squares(cg[:, :, :], up[:, :, 0:T], (sqa, sqb)[g], 4 + g)
                pool.wait_ge(sq_done, 5 + g)
            pool.wait_ge(rope_in, 5 * 16)
            g_.memset(relb[BUCKETS:BUCKETS + 1, :], 1.0).then_inc(brow_ready, 1)
            pool.wait_ge(brow_ready, 2)
            pool.dma_start(bias_dram, bass.AP(brow[:, :].tensor, brow[:, :].offset,
                                              [list(brow[:, :].ap[0]), [0, P], [1, 384]])).then_inc(bias_out, 16)
            pool.wait_ge(ss_ready, 3)
            pool.wait_ge(chunk_used, PH["a_in"].c1)
            done(g_.memset(sqa[:, :], 0.0))
            pool.dma_start(mask[:, :], c_mask).then_inc(mask_in, 16)

            pool.wait_ge(q_ready, 8)
            pool.wait_ge(v_ready, 2 * PH["a_kv"].ng)

            def stage(u, u0, copies_q, copies_v):
                p = u.mod(2)
                if u.i is not None or u.c >= 2:
                    pool.wait_ge(s_done, (u + u0 - 1).v)
                    if u0:
                        pool.wait_ge(p_done, (u + u0 - 1).v)
                    g_.tensor_tensor(fence[:, 2 + p:3 + p], ones[:, 0:1], ones[:, 0:1], ALU.mult)
                copies_q(u, p).then_inc(stq, 1)
                if u.i is not None or u.c >= 2:
                    pool.wait_ge(pv_done, (u + u0 - 1).v)
                    g_.tensor_tensor(fence[:, 4 + p:5 + p], ones[:, 0:1], ones[:, 0:1], ALU.mult)
                copies_v(u, p).then_inc(stv, 1)

            def q_a(u, p):
                g_.tensor_copy(st_q[:, p, :, :], qn[:, sl(u.times(2), 2), :])
                return g_.tensor_copy(st_r[:, p, :], qr[:, sl(u, 1), :])

            def v_a(u, p):
                return g_.tensor_copy(st_v[:, p, :, :], va[:, :, sl(u.times(T), T)])
            stage(Lin(0), 0, q_a, v_a)
            stage(Lin(1), 0, q_a, v_a)
            repeat(pool, 1, UNITS_A // 2, lambda i: [stage(Lin(k, 2, i), 0, q_a, v_a) for k in range(2)])

            def residual_squares(ph, sq0):
                def body(i):
                    for gi in range(2):
                        pool.wait_ge(banks_free, Lin(ph.g0 + gi + 1, 2, i).v)
                        squares(h[:, sl(Lin(4 * gi, 8, i), 4), :], cg[:, :, :], sqa, None)
                        pool.wait_ge(sq_done, Lin(sq0 + gi + 1, 2, i).v)
                done.loop(0, 2, 8, body)
            residual_squares(PH["a_out"], SQ0["a_out"])
            pool.wait_ge(ss_ready, 4)
            done(g_.memset(sqa[:, :], 0.0))
            g_.memset(up[:, :, 0:2], 0.0).then_inc(const_set, 1)
            done.sync()
            residual_squares(PH["f0_out"], SQ0["f0_out"])
            pool.wait_ge(ss_ready, 5)
            done(g_.memset(sqa[:, :], 0.0))
            done.sync()

            pool.wait_ge(chunk_used, PH["f0_out"].c1)
            pool.wait_ge(bias_out, 16)
            bias_toeplitz = bass.AP(bias_dram.tensor, P - 1, [[383, P], [P * 384, HEADS_B], [1, T]])
            pool.dma_start(bt[:, :, :], bias_toeplitz).then_inc(bt_in, 16)
            pool.wait_ge(chunk_used, PH["b_in"].c1)
            pool.dma_start(sinkc[:, :], bass.AP(swa_sinks.tensor, 0, [[0, P], [1, HEADS_B]])).then_inc(swa_in, 16)
            pool.dma_start(bvrow[:, :], bass.AP(swa_b_qkv.tensor, QKV_B - T, [[0, P], [1, T]])).then_inc(swa_in, 16)

            pool.wait_ge(bt_in, 16)
            pool.wait_ge(swa_in, 32)
            pool.wait_ge(kd_ready, 1)
            pool.wait_ge(vb_ready, 2)

            def stage_b(kv):
                for k in range(4):
                    u = Lin(4 * 0 + k, 4, kv) if not isinstance(kv, int) else Lin(4 * kv + k)
                    one = Lin(0, 1, kv) if not isinstance(kv, int) else Lin(kv)

                    def q_b(u, p):
                        g_.tensor_copy(st_q[:, p, 0, :], qb[:, sl(u, 1), :])
                        g_.tensor_copy(st_b[:, p, :, :], bt[:, sl(u.times(2), 2), :])
                        g_.tensor_copy(st_s[:, p, :], sinkc[:, sl(u.times(2), 2)])
                        return g_.tensor_copy(st_q[:, p, 1, :], kd[:, sl(one, 1), :])

                    def v_b(u, p):
                        return g_.tensor_copy(st_vb[:, p, :, :], vb[:, :, sl(one.times(DH), DH)])
                    stage(u, UNITS_A, q_b, v_b)
            stage_b(0)
            repeat(pool, 1, KV_B, stage_b)
            residual_squares(PH["b_out"], SQ0["b_out"])
            pool.wait_ge(ss_ready, 6)
            done(g_.memset(sqa[:, :], 0.0))
            done.sync()
            residual_squares(PH["f1_out"], SQ0["f1_out"])


CONV0 = {OP0["f0_in"]: OP0["f0_in"], OP0["f1_in"]: OP0["f1_in"] - 11}


def tables():
    ident = np.eye(P, dtype=np.float32)
    rot = np.zeros((P, P), np.float32)
    half = ROPE // 2
    for m in range(P):
        b, r = divmod(m, ROPE)
        if r < half:
            rot[b * ROPE + r + half, m] = -1.0
        else:
            rot[b * ROPE + r - half, m] = 1.0
    invf = (np.float32(THETA) ** (-np.arange(half, dtype=np.float32) / half)).astype(np.float32)
    invf = np.tile(invf, P // half).reshape(P, 1)
    tri = np.where(np.arange(P)[None, :] <= np.arange(P)[:, None], 0.0, NEG).astype(np.float32)
    mask = np.concatenate([tri, np.zeros((P, P), np.float32), tri], axis=1)
    dist = 255 - np.arange(384)
    n = np.clip(dist, 0, WINDOW - 1)
    exact = BUCKETS // 2
    big = exact + (np.log(np.maximum(n, 1) / exact) / math.log(MAX_DIST / exact) * (BUCKETS - exact)).astype(np.int32)
    bucket = np.where(n < exact, n, np.minimum(big, BUCKETS - 1))
    valid = (dist >= 0) & (dist <= WINDOW - 1)
    onehot = np.zeros((BUCKETS + 1, 384), np.float32)
    onehot[bucket[valid], np.nonzero(valid)[0]] = 1.0
    onehot[BUCKETS, ~valid] = NEG
    return {"c_ident": ident, "c_rot": rot, "c_invf": invf, "c_mask": mask, "c_onehot": onehot}


def kernel(**inputs):
    import concourse.bacc as bacc
    from concourse.bass_utils import run_bass_kernel_spmd as run

    shape = {
        "x": (T, D), "positions": (1, T), "rel_bias": (BUCKETS, HEADS_B), "norm_mix": (2 * KT, P),
        "norm_ffn": (2 * KT, P), "mla_w_in": (D, 2 * RANK + ROPE), "mla_g_q": (4, P), "mla_g_kv": (4, P),
        "mla_w_qb": (RANK, HEADS_A * (NOPE + ROPE)), "mla_w_kvb": (RANK, HEADS_A * (NOPE + VDIM)),
        "mla_w_o": (HEADS_A * VDIM, D), "swa_w_qkv": (D, QKV_B), "swa_b_qkv": (QKV_B // P, P),
        "swa_sinks": (1, HEADS_B), "swa_w_o": (HEADS_B * DH, D), "swa_b_o": (KT, P),
        "ffn_w_in": (2, D, 2 * FF), "ffn_conv_w": (2 * 3 * CT, P), "ffn_conv_b": (2 * CT, P),
        "ffn_w_out": (2, FF, D), "final_norm": (KT, P),
    }
    nc = bacc.Bacc("TRN2", target_bir_lowering=False, num_devices=1)
    arrays, args = {}, []
    for name, s in shape.items():
        arrays[name] = np.ascontiguousarray(inputs[name]).reshape(s)
    arrays.update(tables())
    for name, a in arrays.items():
        args.append(nc.dram_tensor(name, a.shape, mybir.dt.from_np(a.dtype), kind="ExternalInput").ap())
    y = nc.dram_tensor("y", (T, D), F32, kind="ExternalOutput").ap()
    build(nc, *args, y)
    r = run(nc, [arrays], core_ids=[0])
    return r.results[0]["y"].reshape(1, T, D)
```

```python
import math
from contextlib import ExitStack

import numpy as np
import concourse.bass as bass
from concourse import mybir

F32 = mybir.dt.float32
F32R = mybir.dt.float32r
I32 = mybir.dt.int32
ALU = mybir.AluOpType
ACT = mybir.ActivationFunctionType

P = 128
T = 256
D = 2048
KT = D // P
FF = 5632
FT = FF // P
RANK = 512
HEADS_A, NOPE, ROPE, VDIM = 16, 128, 64, 128
HEADS_B, KV_B, DH = 32, 4, 64
QKV_B = (HEADS_B + 2 * KV_B) * DH
EPS = 1e-6
NEG = -1e30
THETA = 10000.0
BUCKETS, MAX_DIST, WINDOW = 32, 2048, 128

SLOTS = 4
CH = 1024
EARLY = 2
AHEAD = 8
COLS = 512
DMAS = 2

PC_MIX, PC_FFN, PC_FIN, PC_GQ, PC_GKV, PC_BQKV, PC_BO = 0, 32, 64, 80, 84, 88, 108
PC_END0 = 124
PC_CONVW = 128
CT = 2 * FT
PC_CONVB = PC_CONVW + 2 * 3 * CT
PC_END = PC_CONVB + 2 * CT


class Phase:
    def __init__(self, chunk0, chunks, group0, groups):
        self.c0, self.n, self.g0, self.ng = chunk0, chunks, group0, groups
        self.c1, self.g1 = chunk0 + chunks, group0 + groups


def phases():
    out, c, g = {}, 0, 0
    for name, n, m in (("a_in", 18, 3), ("a_q", 16, 4), ("a_kv", 16, 8), ("a_out", 32, 4),
                       ("f0_in", 176, 22), ("f0_out", 88, 4), ("b_in", 40, 5), ("b_out", 32, 4),
                       ("f1_in", 176, 22), ("f1_out", 88, 4)):
        out[name] = Phase(c, n, g, m)
        c, g = c + n, g + m
    return out, c


PH, CHUNKS = phases()
OP0 = {"x": 0, "lat": 4, "a_out": 6, "f0_in": 10, "f0_out": 21, "b_out": 25, "f1_in": 29}
SQ0 = {"x": 0, "lat": 4, "a_out": 6, "f0_out": 10, "b_out": 14, "f1_out": 18}
NORMS = ["x", "cq", "ckv", "f0", "b", "f1", "out"]
NORM_SQ = [4, 5, 6, 10, 14, 18, 22]
UNITS_A, UNITS_B = HEADS_A // 2, HEADS_B // 2


def attention_banks(ph_out):
    scores = 4 * (ph_out.g0 % 2)
    return scores, 4 - scores, 6 - scores


class Lin:
    def __init__(self, c, k=0, i=None):
        self.c, self.k, self.i = c, k, i

    def __add__(self, d):
        return Lin(self.c + d, self.k, self.i)

    def __sub__(self, d):
        return self + (-d)

    def times(self, m):
        return Lin(self.c * m, self.k * m, self.i)

    def over(self, d):
        assert self.i is None or self.k % d == 0
        return Lin(self.c // d, self.k // d, self.i)

    def mod(self, d):
        assert self.i is None or self.k % d == 0
        return self.c % d

    @property
    def v(self):
        return self.c if self.i is None else self.i * self.k + self.c


def sl(n, size):
    return slice(n.v, n.v + size) if n.i is None else bass.ds(n.v, size)


def repeat(eng, start, end, body):
    if end > start:
        with eng.Fori(start, end) as i:
            body(i)


class Steps:
    def __init__(self, eng, sem):
        self.eng, self.sem, self.n, self.at = eng, sem, 0, None

    def __call__(self, ins):
        ins.then_inc(self.sem, 1)
        self.n += 1
        return ins

    def sync(self):
        self.eng.wait_ge(self.sem, Lin(self.n, *(self.at or ())).v)

    def loop(self, start, end, per, body):
        n0 = self.n

        def inner(i):
            self.n, self.at = n0 - start * per, (per, i)
            body(i)
            assert self.n == n0 - start * per + per, f"steps in the loop: {self.n - n0 + start * per}"
        if end > start:
            repeat(self.eng, start, end, inner)
        self.n, self.at = n0 + (end - start) * per, None


def build(nc, x, positions, rel_bias, norm_mix, norm_ffn, mla_w_in, mla_g_q, mla_g_kv, mla_w_qb,
          mla_w_kvb, mla_w_o, swa_w_qkv, swa_b_qkv, swa_sinks, swa_w_o, swa_b_o, ffn_w_in,
          ffn_conv_w, ffn_conv_b, ffn_w_out, final_norm, c_ident, c_rot, c_invf, c_mask,
          c_onehot, out):
    bias_dram = nc.dram_tensor("bias_rows", [HEADS_B, P, 384], F32, kind="Internal").ap()

    top = [(nc.sbuf_base + 63) // 64 * 64]

    def region(nbytes):
        at = top[0]
        top[0] += (nbytes + 31) // 32 * 32
        assert top[0] <= nc.sbuf_usable_end, (top[0], nc.sbuf_usable_end)
        return at

    def place(name, shape, dt, at):
        return nc.alloc_sbuf_tensor_at(name, shape, dt, offset=at)

    def new(name, shape, dt=F32):
        return place(name, shape, dt, region(int(np.prod(shape[1:])) * 4))

    raw = [new(f"raw{s}", [P, CH]) for s in range(SLOTS)]
    w_hi = [new(f"w_hi{s}", [P, CH], F32R) for s in range(SLOTS)]
    w_lo = [new(f"w_lo{s}", [P, CH], F32R) for s in range(SLOTS)]
    h = new("h", [P, KT, T])
    r_tb = region(4 * T * 4)
    tb = place("tb", [P, 4, T], F32, r_tb)
    up = new("up", [P, 4, T + 2])
    r_cg = region(4 * T * 4)
    cg = place("cg", [P, 4, T], F32, r_cg)
    cv = new("cv", [P, 4, T])
    par = new("par", [P, 7 * P])
    ident = new("ident", [P, P])
    ones = new("ones", [P, P])
    rs = new("rs", [P, T])
    sqa = new("sqa", [P, T])
    eps = new("eps", [P, 2])
    rs_col = new("rs_col", [P, 6])
    nm = new("nm", [P, 2, 4])
    ls = new("ls", [P, 2, 4])
    es = new("es", [P, 2, 4])
    ri = new("ri", [P, 2, 4])
    fence = new("fence", [P, 10])

    sinkc = new("sinkc", [P, HEADS_B])
    nsink = new("nsink", [P, HEADS_B])
    pn = [place("pn0", [P, 2, 384], F32, r_cg), place("pn1", [P, 2, 384], F32, r_tb)]

    ra = region(KT * 2 * T * 4)
    aop = place("aop", [P, KT, 2, T], F32R, ra)
    pts = [place("pts0", [P, 2, 384], F32, ra), place("pts1", [P, 2, 384], F32, ra + 29312)]
    sm = place("sm", [P, 2, 2, 384], F32, ra + 3072)
    st_q = place("st_q", [P, 2, 2, T], F32, ra + 9216)
    st_r = place("st_r", [P, 2, T], F32, ra + 13312)
    st_v = place("st_v", [P, 2, 2, T], F32, ra + 15360)
    mask = place("mask", [P, 384], F32, ra + 19456)
    kr = place("kr", [P, T], F32, ra + 20992)
    kd = place("kd", [P, KV_B, T], F32, ra + 22016)
    yt = place("yt", [P, 2, D], F32, ra)

    rg = region(FT * 2 * T * 4)
    gop = place("gop", [P, FT, 2, T], F32R, rg)
    qn = place("qn", [P, HEADS_A, T], F32, rg)
    qr = place("qr", [P, UNITS_A, T], F32, rg + 16384)
    kn = place("kn", [P, HEADS_A, T], F32, rg + 24576)
    va = place("va", [P, 2, HEADS_A * VDIM], F32, rg + 40960)
    r_o = rg + 57344
    oop = place("oop", [P, KT, 2, T], F32R, r_o)
    cop = place("cop", [P, 8, 2, T], F32R, r_o)
    cos = place("cos", [P, T], F32, r_o + 16384)
    sin = place("sin", [P, T], F32, r_o + 17408)
    rot = place("rot", [P, P], F32, r_o + 18432)
    rsq = place("rsq", [P, T], F32, r_o + 18944)
    rsk = place("rsk", [P, T], F32, r_o + 19968)
    sqb = place("sqb", [P, T], F32, r_o + 20992)
    ang = place("ang", [P, T], F32, r_o + 22016)
    turn = place("turn", [P, T], F32, r_o + 23040)
    posi = place("posi", [P, T], I32, r_o + 24064)
    invf = place("invf", [P, 1], F32, r_o + 25088)
    xin = place("xin", [P, 2, D], F32, rg)
    bvrow = up[:, 0, 2:T + 2]
    vb = cv[:, 2:4, :]
    praw = place("praw", [P, 7, P], F32, rg + 16384)
    onehot = place("onehot", [BUCKETS + 1, 384], F32, rg + 20480)
    relb = place("relb", [BUCKETS + 1, HEADS_B], F32, rg + 22016)
    brow = place("brow", [HEADS_B, 384], F32, rg + 22528)
    qb = place("qb", [P, KT, T], F32, rg)
    bt = place("bt", [P, HEADS_B, T], F32, rg + 24576)
    st_vb = place("st_vb", [P, 2, 2, DH], F32, ra + 15360)
    st_b = place("st_b", [P, 2, 2, T], F32, ra + 16384)
    st_k = place("st_k", [P, 2, T], F32, ra + 11264)
    st_qb = place("st_qb", [P, 2, T], F32, ra + 9216)

    ctx = ExitStack()
    with ctx:
        ps = ctx.enter_context(nc.psum_tensor("ps", [P, 8, 512], F32))

        def sem(name):
            return ctx.enter_context(nc.semaphore(name))

        par_in, x_in, c_in, rope_in = sem("par_in"), sem("x_in"), sem("c_in"), sem("rope_in")
        mask_in, bias_out, bt_in, swa_in = sem("mask_in"), sem("bias_out"), sem("bt_in"), sem("swa_in")
        const_set, par_t, par_ready, x_t, h_in = sem("const_set"), sem("par_t"), sem("par_ready"), sem("x_t"), sem("h_in")
        brow_t, brow_ready = sem("brow_t"), sem("brow_ready")
        raw_full = [sem(f"raw_full{s}") for s in range(SLOTS)]
        hi_ready, lo_ready, chunk_used = sem("hi_ready"), sem("lo_ready"), sem("chunk_used")
        b_copied, banks_free = sem("b_copied"), sem("banks_free")
        t_ready, op_hi, op_lo = sem("t_ready"), sem("op_hi"), sem("op_lo")
        sq_done, ss_ready, ss_read, sqrt_done = sem("sq_done"), sem("ss_ready"), sem("ss_read"), sem("sqrt_done")
        dve_done, act_done, pool_done = sem("dve_done"), sem("act_done"), sem("pool_done")
        lat_ready, angle_ready, trig_ready = sem("lat_ready"), sem("angle_ready"), sem("trig_ready")
        ckv_cols, vb_ready = sem("ckv_cols"), sem("vb_ready")
        b2_copied, rope_x, rope_rot, rope_read = sem("b2_copied"), sem("rope_x"), sem("rope_rot"), sem("rope_read")
        q_ready, k_ready, v_ready, kd_ready, kd_src = (sem("q_ready"), sem("k_ready"), sem("v_ready"), sem("kd_ready"),
                                                        sem("kd_src"))
        conv_ready, silu_ready = sem("conv_ready"), sem("silu_ready")
        stq, stv, s_done, m_done, p_done = sem("stq"), sem("stv"), sem("s_done"), sem("m_done"), sem("p_done")
        bias_staged, nsink_ready = sem("bias_staged"), sem("nsink_ready")
        pn_done, pt_done, ptc, pv_done, att_hi, att_lo = (sem("pn_done"), sem("pt_done"), sem("ptc"),
                                                         sem("pv_done"), sem("att_hi"), sem("att_lo"))
        y_scaled, y_t, y_read, stored = sem("y_scaled"), sem("y_t"), sem("y_read"), sem("stored")

        block = ctx.enter_context(nc.Block())

        @block.sync
        def _(sp):
            sp.dma_start(ident[:, :], c_ident).then_inc(c_in, 16)
            rows = [(norm_mix, 2 * KT), (norm_ffn, 2 * KT), (final_norm, KT), (mla_g_q, 4), (mla_g_kv, 4),
                    (swa_b_qkv, QKV_B // P), (swa_b_o, KT)]
            at = 0
            for a, n in rows:
                sp.dma_start(praw[at:at + n, 0, :], a).then_inc(par_in, 16)
                at += n
            assert at == PC_END0
            for half in range(2):
                sp.dma_start(xin[:, half, :], x[half * P:(half + 1) * P, :]).then_inc(x_in, 16)
            sp.dma_start(praw[:, 1:5, :], ffn_conv_w[0:512, :].rearrange("(b r) c -> r b c", b=4)).then_inc(par_in, 16)
            sp.dma_start(praw[0:16, 5, :], ffn_conv_w[512:528, :]).then_inc(par_in, 16)
            sp.dma_start(praw[16:128, 5, :], ffn_conv_b[0:112, :]).then_inc(par_in, 16)
            sp.dma_start(praw[0:64, 6, :], ffn_conv_b[112:176, :]).then_inc(par_in, 16)

            def load(n, parts):
                s = n.mod(SLOTS)
                if n.i is not None or n.c >= SLOTS:
                    sp.wait_ge(lo_ready, (n - (SLOTS - 1)).v)
                for dst, src in parts(raw[s]):
                    sp.dma_start(dst, src).then_inc(raw_full[s], 16)

            def rows_cols(w, row, col):
                def parts(r):
                    return [(r[:, k * COLS:(k + 1) * COLS], w[row + k * P:row + (k + 1) * P, sl(col, COLS)])
                            for k in range(2)]
                return parts

            def stream(ph, w, kts, cols):
                per = kts // 2
                turn_chunks = per * len(cols(None))
                turns = ph.n // turn_chunks

                def turn_body(i):
                    for gi, col in enumerate(cols(i)):
                        for c in range(per):
                            load(Lin(ph.c0 + gi * per + c, turn_chunks, i), rows_cols(w, c * 2 * P, col))
                repeat(sp, 0, turns, turn_body)

            ph = PH["a_in"]
            for g in range(2):
                for c in range(8):
                    load(Lin(ph.c0 + g * 8 + c), rows_cols(mla_w_in, c * 2 * P, Lin(g * COLS)))
                    if g == 0 and c == 3:
                        sp.dma_start(rot[:, :], c_rot).then_inc(rope_in, 16)
                        sp.dma_start(invf[:, :], c_invf).then_inc(rope_in, 16)
                        sp.dma_start(posi[:, :], bass.AP(positions.tensor, 0, [[0, P], [1, T]])).then_inc(rope_in, 16)
                        sp.dma_start(onehot[:, :], c_onehot).then_inc(rope_in, 16)
                        sp.dma_start(relb[0:BUCKETS, :], rel_bias).then_inc(rope_in, 16)
            for c in range(2):
                def rope_parts(r, c=c):
                    v = r[:, :].rearrange("p (k d c) -> p k d c", k=8, d=2)
                    src = mla_w_in[c * 8 * P:(c + 1) * 8 * P, 2 * RANK:2 * RANK + ROPE].rearrange("(k p) c -> p k c", p=P)
                    return [(v[:, :, d, :], src) for d in range(2)]
                load(Lin(ph.c0 + 16 + c), rope_parts)
            ph = PH["a_q"]

            def q_body(i):
                for k in range(4):
                    def q_parts(r, k=k):
                        src = mla_w_qb[k * P:(k + 1) * P, sl(Lin(0, 4 * 192, i), 4 * 192)].rearrange("p (h c) -> p h c", h=4)
                        return [(r[:, 0:512].rearrange("p (h c) -> p h c", h=4), src[:, :, 0:NOPE]),
                                (r[:, 512:768].rearrange("p (h c) -> p h c", h=4), src[:, :, NOPE:192])]
                    load(Lin(ph.c0 + k, 4, i), q_parts)
            repeat(sp, 0, 4, q_body)
            stream(PH["a_kv"], mla_w_kvb, 4, lambda i: [Lin(0, 1024, i), Lin(512, 1024, i)])
            two_groups = lambda i: [Lin(0, 1024, i), Lin(COLS, 1024, i)]
            gate_val = lambda i: [Lin(0, COLS, i), Lin(FF, COLS, i)]
            stream(PH["a_out"], mla_w_o, KT, two_groups)
            stream(PH["f0_in"], ffn_w_in[0], KT, gate_val)
            stream(PH["f0_out"], ffn_w_out[0], FT, two_groups)
            ph = PH["b_in"]
            for c in range(8):
                load(Lin(ph.c0 + c), rows_cols(swa_w_qkv, c * 2 * P, Lin(4 * COLS)))
            stream(Phase(ph.c0 + 8, 32, ph.g0 + 1, 4), swa_w_qkv, KT, two_groups)
            stream(PH["b_out"], swa_w_o, KT, two_groups)
            stream(PH["f1_in"], ffn_w_in[1], KT, gate_val)
            stream(PH["f1_out"], ffn_w_out[1], FT, two_groups)
            for half in range(2):
                sp.wait_ge(y_read, 4 * (half + 1))
                sp.dma_start(out[half * P:(half + 1) * P, :], yt[:, half, :]).then_inc(stored, 16)
            sp.wait_ge(stored, 32)
            sp.wait_ge(bias_out, 16)

        @block.tensor
        def _(pe):
            mm = nc.tensor.matmul

            def feature_tile(bank, whi, wlo, op, start, stop, cols=T):
                def high():
                    return mm(ps[:, bank, 0:2 * T], whi, op, start=start, stop=stop)

                def low():
                    return mm(ps[:, bank, 0:T], wlo, op[:, 0, :], start=False, stop=False)
                if stop:
                    low()
                    return high()
                high()
                return low()

            def w_chunk(n, op, kt0, first, last, b0, tiles=(0, 1, 2, 3)):
                s = n.mod(SLOTS)
                pe.wait_ge(lo_ready, (n + 1).v)
                for j, m in enumerate(tiles):
                    for k in range(2):
                        c = k * COLS + m * P
                        z = feature_tile(b0 + j, w_hi[s][:, c:c + P], w_lo[s][:, c:c + P],
                                         op[:, kt0 + k, :, :], first and k == 0, last and k == 1)
                return z

            def token_chunk(n, op, kt0, first, last, bank, wcols):
                s = n.mod(SLOTS)
                for half in range(2):
                    t0 = half * P
                    for k in range(2):
                        hi, lo = op[:, kt0 + k, 0, t0:t0 + P], op[:, kt0 + k, 1, t0:t0 + P]
                        o = ps[:, bank + half, 0:T]
                        mm(o, hi, wcols(w_hi[s], k), start=first and k == 0, stop=False)
                        mm(o, hi, wcols(w_lo[s], k), start=False, stop=False)
                        z = mm(o, lo, wcols(w_hi[s], k), start=False, stop=last and k == 1)
                return z

            def banks_of(g):
                if g.i is not None or g.c >= 2:
                    pe.wait_ge(banks_free, (g - 1).v)
                return 4 * g.mod(2)

            def sum_squares(norm, src, bank, cols=False):
                pe.wait_ge(sq_done, NORM_SQ[norm])
                z = mm(ps[:, bank, 0:T], ones[:, :], src[:, :], start=True, stop=True)
                if cols:
                    for half in range(2):
                        z = mm(ps[:, bank, T + half:T + half + 1], src[:, half * P:(half + 1) * P],
                               ones[:, 0:1], start=True, stop=True)
                z.then_inc(ss_ready, 1)

            pe.wait_ge(c_in, 16)
            pe.wait_ge(par_in, 11 * 16)
            for b in range(7):
                n = (PC_END0, P, P, P, P, P, 64)[b]
                z = nc.tensor.transpose(ps[:, b // 4, (b % 4) * P:(b % 4) * P + n], praw[0:n, b, :], ident[0:n, 0:n])
            z.then_inc(par_t, 1)
            pe.wait_ge(x_in, 32)
            for j in (2, 3, 4, 5, 6, 7, 0, 1):
                if j == 0:
                    pe.wait_ge(par_ready, 1)
                for m in range(2):
                    for half in range(2):
                        z = nc.tensor.transpose(ps[:, j, m * T + half * P:m * T + (half + 1) * P],
                                                xin[:, half, (2 * j + m) * P:(2 * j + m + 1) * P], ident[:, :])
                z.then_inc(x_t, 1)

            ph = PH["a_in"]
            pe.wait_ge(h_in, 8)
            for g in range(2):
                for c in range(8):
                    if g == 0 and c % 2 == 0:
                        pe.wait_ge(op_lo, OP0["x"] + c // 2 + 1)
                    if g == 1 and c == 0:
                        pe.wait_ge(ss_read, 1)
                    w_chunk(Lin(ph.c0 + g * 8 + c), aop, 2 * c, c == 0, c == 7,
                            banks_of(Lin(g)) if c == 0 else 4 * (g % 2)).then_inc(chunk_used, 1)
                    if g == 0 and c == 5:
                        sum_squares(0, sqa, 4)
            banks_of(Lin(2))
            for c in range(2):
                n = Lin(ph.c0 + 16 + c)
                pe.wait_ge(lo_ready, (n + 1).v)
                for k in range(8):
                    z = feature_tile(0, w_hi[n.mod(SLOTS)][:, k * P:(k + 1) * P], w_lo[n.mod(SLOTS)][:, k * P:(k + 1) * P],
                                     aop[:, 8 * c + k, :, :], c == 0 and k == 0, c == 1 and k == 7)
                z.then_inc(chunk_used, 1)
            pe.wait_ge(brow_ready, 1)
            mm(ps[0:HEADS_B, 1, 0:384], relb[:, :], onehot[:, :], start=True, stop=True).then_inc(brow_t, 1)
            sum_squares(1, sqa, 2)
            sum_squares(2, sqb, 3, cols=True)
            pe.wait_ge(rope_in, 5 * 16)

            def rotate(k, bank, src):
                pe.wait_ge(rope_x, k + 1)
                mm(ps[:, bank, 0:T if k == 0 else 2 * T], rot[:, :], src,
                   start=True, stop=True).then_inc(rope_rot, 1)
            rotate(0, 6, cv[:, 2, :])

            ph = PH["a_q"]
            for g in range(4):
                pe.wait_ge(banks_free, ph.g0 + g)
                if g == 0:
                    pe.wait_ge(op_lo, OP0["lat"] + 1)
                    pe.wait_ge(ss_read, 3)
                    pe.wait_ge(brow_ready, 2)
                for c in range(4):
                    n = Lin(ph.c0 + 4 * g + c)
                    s = n.mod(SLOTS)
                    pe.wait_ge(lo_ready, (n + 1).v)
                    for m in range(6):
                        z = feature_tile(m, w_hi[s][:, m * P:(m + 1) * P], w_lo[s][:, m * P:(m + 1) * P],
                                         cop[:, c, :, :], c == 0, c == 3)
                    z.then_inc(chunk_used, 1)
                pe.wait_ge(rope_read, g + 1)
                rotate(1 + g, 6, cv[:, 2:4, :])

            ph = PH["a_kv"]
            pe.wait_ge(op_lo, OP0["lat"] + 2)
            pe.wait_ge(banks_free, ph.g0)
            pe.wait_ge(rope_read, 5)

            def kv_body(i):
                for gi in range(2):
                    g = Lin(ph.g0 + gi, 2, i)
                    b0 = banks_of(g)
                    for c in range(2):
                        n = Lin(ph.c0 + 2 * gi + c, 4, i)
                        w_chunk(n, cop, 4 + 2 * c, c == 0, c == 1, b0, tiles=(0, 2))
                        token_chunk(n, cop, 4 + 2 * c, c == 0, c == 1, b0 + 2,
                                    lambda w, k: w[:, k * COLS:(k + 1) * COLS].rearrange("p (h c) -> p h c", h=2)[:, :, P:2 * P]
                                    ).then_inc(chunk_used, 1)
            repeat(pe, 0, 4, kv_body)

            def attention(u0, units, scores, values, banks, inputs, early):
                def score(u):
                    pe.wait_ge(stq, (u + u0 + 1).v)
                    if u.i is not None or u.c >= 2:
                        pe.wait_ge(m_done, (u + u0 - 1).v)
                    if u.i is None and u.c == units - 1 and not u0:
                        pe.wait_ge(k_ready, PH["a_kv"].ng)
                    scores(u, banks[0] + 2 * u.mod(2)).then_inc(s_done, 1)

                def turn_p(u):
                    pe.wait_ge(pn_done, (u + u0 + 1).v)
                    if u.i is not None or u.c + u0 >= 1:
                        pe.wait_ge(ptc, (u + u0).v)
                    for hh in range(2):
                        for blk in range(3):
                            z = nc.tensor.transpose(ps[:, banks[1] + hh, blk * P:(blk + 1) * P],
                                                    pn[u.mod(2)][:, hh, blk * P:(blk + 1) * P], ident[:, :])
                    z.then_inc(pt_done, 1)

                def value(u):
                    pe.wait_ge(ptc, (u + u0 + 1).v)
                    pe.wait_ge(stv, (u + u0 + 1).v)
                    if u.i is not None or u.c >= 2:
                        pe.wait_ge(att_lo, (u + u0 - 1).v)
                    values(u, banks[2] + u.mod(2)).then_inc(pv_done, 1)

                def step(u, ahead=True):
                    if ahead:
                        score(u + 2)
                    turn_p(u)
                    value(u - 1)
                pe.wait_ge(banks_free, inputs.g1 - 1)
                score(Lin(0))
                score(Lin(1))
                score(Lin(2))
                pe.wait_ge(banks_free, inputs.g1)
                turn_p(Lin(0))
                step(Lin(1))
                repeat(pe, 1, units // 2 - 1, lambda i: [step(Lin(k, 2, i)) for k in range(2)])
                step(Lin(units - 2), ahead=False)
                pe.wait_ge(m_done, units + u0)
                early(0)
                step(Lin(units - 1), ahead=False)
                early(1)
                value(Lin(units - 1))

            def scores_a(u, bank):
                p = u.mod(2)
                for hh in range(2):
                    r = slice(64 * hh, 64 * hh + 64)
                    for q0, keys, o in ((0, P, 0), (P, T, P)):
                        o = ps[:, bank + hh, o:o + keys]
                        mm(o, st_q[:, p, hh, q0:q0 + P], kn[:, sl(u.times(2) + hh, 1), 0:keys], start=True, stop=False)
                        z = mm(o, st_r[r, p, q0:q0 + P], kr[r, 0:keys], start=False, stop=True)
                return z

            def values_a(u, bank):
                p = u.mod(2)
                for hh in range(2):
                    v = slice(hh * VDIM, (hh + 1) * VDIM)
                    mm(ps[:, bank, hh * T:(hh + 1) * T], st_v[:, p, 0, v], pts[p][:, hh, 0:T], start=True, stop=False)
                    z = mm(ps[:, bank, hh * T + P:(hh + 1) * T], st_v[:, p, 1, v], pts[p][:, hh, T:384],
                           start=False, stop=True)
                return z

            def early_chunk(ph, per_unit, u0):
                def chunk(c):
                    pe.wait_ge(att_lo, u0 + per_unit * (c + 1))
                    w_chunk(Lin(ph.c0 + c), oop, 2 * c, c == 0, False, 4 * (ph.g0 % 2)).then_inc(chunk_used, 1)
                return chunk

            def groups(ph, op, kts, first_wait, norm=None, rs_cols=False, start=0, end=None):
                per = kts // 2
                turns = (ph.n // (2 * per)) if end is None else end

                def body(i, first=False):
                    for gi in range(2):
                        g = Lin(ph.g0 + gi, 2, i)
                        if first and gi == 1 and norm is not None:
                            pe.wait_ge(ss_read, norm + 1)
                        b0 = banks_of(g)
                        for c in range(start if first and gi == 0 else 0, per):
                            if first and gi == 0:
                                first_wait(c)
                            w_chunk(Lin(ph.c0 + gi * per + c, 2 * per, i), op, 2 * c, c == 0, c == per - 1,
                                    b0).then_inc(chunk_used, 1)
                            if first and gi == 0 and c == 4 and norm is not None:
                                pe.wait_ge(banks_free, ph.g0)
                                sum_squares(norm, sqa, 4 - b0, rs_cols)
                body(None, True)
                repeat(pe, 1, turns, body)

            def plain_groups(g, n, op, per):
                for gi in range(2):
                    b0 = banks_of(g + gi)
                    for c in range(per):
                        w_chunk(n + (gi * per + c), op, 2 * c, c == 0, c == per - 1, b0).then_inc(chunk_used, 1)

            def att_wait(done):
                return lambda c: pe.wait_ge(att_lo, done) if c == EARLY else None

            def op_wait(base):
                return lambda c: pe.wait_ge(op_lo, base + c // 2 + 1) if c % 2 == 0 else None

            pe.wait_ge(k_ready, PH["a_kv"].ng - 1)
            attention(0, UNITS_A, scores_a, values_a, attention_banks(PH["a_out"]), PH["a_kv"], early_chunk(PH["a_out"], 1, 0))
            groups(PH["a_out"], oop, KT, att_wait(UNITS_A), start=EARLY)
            groups(PH["f0_in"], aop, KT, op_wait(OP0["a_out"]), norm=3)
            groups(PH["f0_out"], gop, FT, op_wait(OP0["f0_in"]))

            ph = PH["b_in"]
            b0 = banks_of(Lin(ph.g0))
            for c in range(8):
                n = Lin(ph.c0 + c)
                op_wait(OP0["f0_out"])(c)
                w_chunk(n, aop, 2 * c, c == 0, c == 7, b0, tiles=(0, 1))
                token_chunk(n, aop, 2 * c, c == 0, c == 7, b0 + 2,
                            lambda w, k: w[:, k * COLS + T:(k + 1) * COLS]).then_inc(chunk_used, 1)
                if c == 4:
                    pe.wait_ge(banks_free, ph.g0)
                    sum_squares(4, sqa, 4 - b0, True)
            pe.wait_ge(ss_read, 5)
            repeat(pe, 0, 2, lambda i: plain_groups(Lin(ph.g0 + 1, 2, i), Lin(ph.c0 + 8, 16, i), aop, 8))

            def scores_b(u, bank):
                p = u.mod(2)
                for hh in range(2):
                    r = slice(64 * hh, 64 * hh + 64)
                    for q0, keys, o in ((0, P, 0), (P, T, P)):
                        z = mm(ps[:, bank + hh, o:o + keys], st_qb[r, p, q0:q0 + P], st_k[r, p, 0:keys],
                               start=True, stop=True)
                return z

            def values_b(u, bank):
                p = u.mod(2)
                for hh in range(2):
                    r = slice(64 * hh, 64 * hh + 64)
                    mm(ps[r, bank, 0:T], st_vb[:, p, 0, :], pts[p][:, hh, 0:T], start=True, stop=False)
                    z = mm(ps[r, bank, P:T], st_vb[:, p, 1, :], pts[p][:, hh, T:384], start=False, stop=True)
                return z

            attention(UNITS_A, UNITS_B, scores_b, values_b, attention_banks(PH["b_out"]), ph, early_chunk(PH["b_out"], 2, UNITS_A))
            groups(PH["b_out"], oop, KT, att_wait(UNITS_A + UNITS_B), start=EARLY)
            groups(PH["f1_in"], aop, KT, op_wait(OP0["b_out"]), norm=5)
            groups(PH["f1_out"], gop, FT, op_wait(OP0["f1_in"]))

            pe.wait_ge(banks_free, PH["f1_out"].g1)
            pe.wait_ge(sq_done, NORM_SQ[6])
            for half in range(2):
                z = mm(ps[:, 0, T + half:T + half + 1], sqa[:, half * P:(half + 1) * P], ones[:, 0:1],
                       start=True, stop=True)
            z.then_inc(ss_ready, 1)
            for half in range(2):
                for q in range(4):
                    if half == 0:
                        pe.wait_ge(y_scaled, q + 1)
                    if q == 0:
                        pe.wait_ge(y_read, 4 * half) if half else pe.wait_ge(ss_read, 7)
                    for j in range(4):
                        z = nc.tensor.transpose(ps[:, 4 * (1 - half) + q, j * P:(j + 1) * P],
                                                h[:, 4 * q + j, half * P:(half + 1) * P], ident[:, :])
                    z.then_inc(y_t, 1)

        @block.scalar
        def _(act):
            f = nc.scalar.activation
            done = Steps(act, act_done)

            def split(n):
                if n.i is None and n.c >= CHUNKS:
                    return
                s = n.mod(SLOTS)
                act.wait_ge(raw_full[s], (n.over(SLOTS).times(16 * DMAS) + 16 * DMAS).v)
                if n.i is not None or n.c >= SLOTS:
                    act.wait_ge(chunk_used, (n - (SLOTS - 1)).v)
                f(w_hi[s][:, :], raw[s][:, :], ACT.Copy).then_inc(hi_ready, 1)

            def b_half(g, last_chunk, tiles=4, bias=None):
                act.wait_ge(chunk_used, (last_chunk + 1).v)
                if g.i is not None or g.c >= 1:
                    act.wait_ge(banks_free, g.v)
                b0 = 4 * g.mod(2)
                if bias is None:
                    f(tb[:, 0:tiles, :], ps[:, b0:b0 + tiles, T:2 * T], ACT.Copy).then_inc(b_copied, 1)
                    return
                for j in range(tiles):
                    z = f(tb[:, j, :], ps[:, b0 + j, T:2 * T], ACT.Identity, bias=bias(j))
                z.then_inc(b_copied, 1)

            def op_high(k, dst):
                act.wait_ge(t_ready, (k + 1).v)
                f(dst, cv[:, :, :], ACT.Copy).then_inc(op_hi, 1)

            def norm_root(norm, dst, bank, width, scale=1.0, cols=None):
                act.wait_ge(ss_ready, norm + 1)
                act.wait_ge(const_set, 1)
                z = f(dst, ps[:, bank, 0:T], ACT.Sqrt, bias=eps[:, 1:2] if scale != 1.0 else eps[:, 0:1],
                      scale=1.0 / width / scale ** 2)
                if cols is not None:
                    z = f(rs_col[:, cols:cols + 2], ps[:, bank, T:T + 2], ACT.Sqrt, bias=eps[:, 0:1], scale=1.0 / width)
                z.then_inc(ss_read, 1)

            act.wait_ge(par_t, 1)
            f(par[:, 0:PC_END0], ps[:, 0, 0:PC_END0], ACT.Copy)
            f(par[:, P:512], ps[:, 0, P:512], ACT.Copy)
            f(par[:, 512:PC_END], ps[:, 1, 0:PC_END - 512], ACT.Copy).then_inc(par_ready, 1)
            order = (2, 3, 4, 5, 6, 7, 0, 1)
            for n, j in enumerate(order):
                act.wait_ge(x_t, n + 1)
                f(h[:, 2 * j:2 * j + 2, :], ps[:, j, :].rearrange("p (m t) -> p m t", m=2), ACT.Copy).then_inc(h_in, 1)
            for c in range(SLOTS):
                split(Lin(c))
            for q in range(4):
                op_high(Lin(OP0["x"] + q), aop[:, 4 * q:4 * q + 4, 0, :])
            for c in range(SLOTS, AHEAD):
                split(Lin(c))
            norm_root(0, rs[:, :], 4, D)

            ph = PH["a_in"]
            for c in range(AHEAD, ph.n + AHEAD):
                split(Lin(c))
                if c == AHEAD + 1:
                    act.wait_ge(angle_ready, 1)
                    f(sin[:, :], sin[:, :], ACT.Sin)
                    f(cos[:, :], cos[:, :], ACT.Sin).then_inc(trig_ready, 1)
                if c in (11, 19):
                    g = (c - 11) // 8
                    b_half(Lin(g), Lin(8 * g + 7))
                    op_high(Lin(OP0["lat"] + g), cop[:, 4 * g:4 * g + 4, 0, :])
                if c == 21:
                    b_half(Lin(2), Lin(17), tiles=1)
                    act.wait_ge(brow_t, 1)
                    f(brow[:, :], ps[0:HEADS_B, 1, 0:384], ACT.Copy).then_inc(brow_ready, 1)
                    act.wait_ge(ss_ready, 2)
                    norm_root(1, rsq[:, :], 2, RANK, scale=(NOPE + ROPE) ** -0.5)
                    norm_root(2, rsk[:, :], 3, RANK, cols=0)

            ph = PH["a_q"]

            for g in range(4):
                act.wait_ge(rope_read, g + 1)
                act.wait_ge(chunk_used, ph.c0 + 4 * g + 4)
                act.wait_ge(banks_free, ph.g0 + g)
                f(tb[:, 0:4, :], ps[:, 0:4, T:2 * T], ACT.Copy).then_inc(b_copied, 1)
                f(cv[:, 0:2, :], ps[:, 4:6, T:2 * T], ACT.Copy).then_inc(b2_copied, 1)
                for c in range(4):
                    split(Lin(ph.c0 + AHEAD + 4 * g + c))

            ph = PH["a_kv"]

            def kv_body(i):
                for gi in range(2):
                    g = Lin(ph.g0 + gi, 2, i)
                    b0 = 4 * g.mod(2)
                    act.wait_ge(chunk_used, Lin(ph.c0 + 2 * gi + 2, 4, i).v)
                    act.wait_ge(ckv_cols, 1)
                    for half in range(2):
                        f(va[:, half, sl(Lin(T * gi, 2 * T, i), T)], ps[:, b0 + 2 + half, 0:T], ACT.Copy,
                          scale=rs_col[:, half:half + 1]).then_inc(v_ready, 1)
                    b_half(g, Lin(ph.c0 + 2 * gi + 1, 4, i), tiles=2)
                for c in range(4):
                    split(Lin(ph.c0 + AHEAD + c, 4, i))
            repeat(act, 0, 3, kv_body)
            for gi in range(2):
                g = Lin(ph.g0 + 6 + gi)
                b0 = 4 * g.mod(2)
                act.wait_ge(chunk_used, ph.c0 + 14 + 2 * gi)
                for half in range(2):
                    f(va[:, half, T * (6 + gi):T * (7 + gi)], ps[:, b0 + 2 + half, 0:T], ACT.Copy,
                      scale=rs_col[:, half:half + 1]).then_inc(v_ready, 1)
                b_half(g, Lin(ph.c0 + 13 + 2 * gi), tiles=2)

            def attention(u0, units, banks, sinks, out_high):
                def exps(u):
                    p = u.mod(2)
                    act.wait_ge(m_done, (u + u0 + 1).v)
                    for hh in range(2):
                        for q, cols in ((0, slice(0, P)), (1, slice(P, 384))):
                            k = 2 * hh + q
                            z = f(sm[:, p, hh, cols], sm[:, p, hh, cols], ACT.Exp, bias=nm[:, p, k:k + 1],
                                  accum_out=ls[:, p, k:k + 1])
                    if sinks:
                        for hh in range(2):
                            z = f(es[:, p, 2 * hh:2 * hh + 2], nm[:, p, 2 * hh:2 * hh + 2], ACT.Exp,
                                  bias=sinkc[:, sl(u.times(2) + hh, 1)])
                    z.then_inc(p_done, 1)

                def pt_copy(u):
                    act.wait_ge(pt_done, (u + u0 + 1).v)
                    if u.i is not None or u.c >= 2:
                        act.wait_ge(pv_done, (u + u0 - 1).v)
                    f(pts[u.mod(2)][:, :, :], ps[:, banks[1]:banks[1] + 2, 0:384], ACT.Copy).then_inc(ptc, 1)

                def o_high(u):
                    act.wait_ge(pv_done, (u + u0 + 1).v)
                    out_high(u).then_inc(att_hi, 1)

                def step(u, ahead=True):
                    if ahead:
                        exps(u + 1)
                    if u.i is not None or u.c >= 2:
                        o_high(u - 2)
                    pt_copy(u)
                exps(Lin(0))
                step(Lin(0))
                step(Lin(1))
                repeat(act, 1, units // 2 - 1, lambda i: [step(Lin(k, 2, i)) for k in range(2)])
                step(Lin(units - 2))
                step(Lin(units - 1), ahead=False)
                o_high(Lin(units - 2))
                o_high(Lin(units - 1))

            banks = attention_banks(PH["a_out"])
            attention(0, UNITS_A, banks, False,
                      lambda u, o=banks[2]: f(oop[:, sl(u.times(2), 2), 0, :],
                                  ps[:, o + u.mod(2), :].rearrange("p (m t) -> p m t", m=2), ACT.Copy))
            for c in range(SLOTS, AHEAD):
                split(Lin(PH["a_out"].c0 + c))

            def residual(ph, kts, k0, norm_next, bias=None, last=False):
                per = kts // 2
                turns = ph.n // (2 * per)

                def body(i):
                    for j in range(2 * per):
                        split(Lin(ph.c0 + AHEAD + j, 2 * per, i))
                        gi, at = divmod(j, per)
                        if at == per - 5:
                            b_half(Lin(ph.g0 + gi, 2, i), Lin(ph.c0 + gi * per + per - 1, 2 * per, i),
                                   bias=bias and (lambda t: par[:, sl(Lin(bias + 4 * gi + t, 8, i), 1)]))
                        if at == per - 3 and k0 is not None:
                            op_high(Lin(k0 + gi, 2, i), aop[:, sl(Lin(4 * gi, 8, i), 4), 0, :])
                if last:
                    for t in range(turns):
                        body_static(ph, per, t, k0, bias)
                else:
                    repeat(act, 0, turns, body)

            def body_static(ph, per, t, k0, bias):
                for j in range(2 * per):
                    split(Lin(ph.c0 + AHEAD + j + 2 * per * t))
                    gi, at = divmod(j, per)
                    if at == per - 5:
                        b_half(Lin(ph.g0 + gi + 2 * t), Lin(ph.c0 + gi * per + per - 1 + 2 * per * t))

            def ffn_in(ph, k0):
                def body(i):
                    for j in range(16):
                        split(Lin(ph.c0 + AHEAD + j, 16, i))
                        if j in (3, 11):
                            gi = j // 8
                            b_half(Lin(ph.g0 + gi, 2, i), Lin(ph.c0 + 8 * gi + 7, 16, i))
                        if j == 8:
                            act.wait_ge(conv_ready, Lin(k0 - CONV0[k0] + 1, 1, i).v)
                            f(cg[:, :, :], cg[:, :, :], ACT.Silu).then_inc(silu_ready, 1)
                        if j == 14:
                            op_high(Lin(k0, 1, i), gop[:, sl(Lin(0, 4, i), 4), 0, :])
                repeat(act, 0, 11, body)

            residual(PH["a_out"], KT, OP0["a_out"], 3)
            norm_root(3, rs[:, :], 4 - 4 * (PH["f0_in"].g0 % 2), D)
            ffn_in(PH["f0_in"], OP0["f0_in"])
            residual(PH["f0_out"], FT, OP0["f0_out"], 4)
            norm_root(4, rs[:, :], 4 - 4 * (PH["b_in"].g0 % 2), D, cols=2)

            ph = PH["b_in"]

            for j in range(SLOTS):
                split(Lin(ph.c0 + AHEAD + j))
            b_half(Lin(ph.g0), Lin(ph.c0 + 7), tiles=2)

            def b_body(i):
                for j in range(16):
                    split(Lin(ph.c0 + AHEAD + SLOTS + j, 16, i))
                    if j in (7, 15):
                        b_half(Lin(ph.g0 + (j + 1) // 8, 2, i), Lin(ph.c0 + 8 + j, 16, i))
            repeat(act, 0, 2, b_body)
            act.wait_ge(kd_src, 1)
            for kv in range(KV_B):
                for d in range(2):
                    z = f(kd[64 * d:64 * d + 64, kv, :], cv[64 * (kv % 2):64 * (kv % 2) + 64, kv // 2, :], ACT.Copy)
                if kv in (0, KV_B - 1):
                    z.then_inc(kd_ready, 1)
            banks = attention_banks(PH["b_out"])
            attention(UNITS_A, UNITS_B, banks, True,
                      lambda u, o=banks[2]: f(oop[:, sl(u, 1), 0, :], ps[:, o + u.mod(2), 0:T], ACT.Copy))
            for c in range(SLOTS, AHEAD):
                split(Lin(PH["b_out"].c0 + c))
            residual(PH["b_out"], KT, OP0["b_out"], 5, bias=PC_BO)
            norm_root(5, rs[:, :], 4 - 4 * (PH["f1_in"].g0 % 2), D)
            ffn_in(PH["f1_in"], OP0["f1_in"])
            residual(PH["f1_out"], FT, None, 6, last=True)

            act.wait_ge(ss_ready, 7)
            f(rs_col[:, 4:6], ps[:, 0, T:T + 2], ACT.Sqrt, bias=eps[:, 0:1], scale=1.0 / D).then_inc(ss_read, 1)
            act.wait_ge(sqrt_done, 1)
            for half in range(2):
                for q in range(4):
                    act.wait_ge(y_t, 4 * half + q + 1)
                    f(yt[:, half, q * 512:(q + 1) * 512], ps[:, 4 * (1 - half) + q, :], ACT.Copy,
                      scale=rs_col[:, 4 + half:5 + half]).then_inc(y_read, 1)

        @block.vector
        def _(dve):
            v = nc.vector
            done = Steps(dve, dve_done)

            def split(n):
                if n.i is None and n.c >= CHUNKS:
                    return
                s = n.mod(SLOTS)
                dve.wait_ge(hi_ready, (n + 1).v)
                v.tensor_tensor(w_lo[s][:, :], raw[s][:, :], w_hi[s][:, :].bitcast(F32), ALU.subtract).then_inc(lo_ready, 1)

            def spread(a, tiles):
                return bass.AP(a.tensor, a.offset, [list(a.ap[0]), [0, tiles], [1, T]])

            def col(n):
                return par[:, sl(n, 1)]

            def gains(k, src, gain, tiles=4):
                if k.i is not None or k.c >= 1:
                    dve.wait_ge(op_lo, k.v)
                for j in range(tiles):
                    z = v.tensor_scalar(cv[:, j, :], src(j), col(gain + j), None, ALU.mult)
                z.then_inc(t_ready, 1)

            def op_low(k, dst, hi):
                dve.wait_ge(op_hi, (k + 1).v)
                v.tensor_tensor(dst, cv[:, :, :], hi.bitcast(F32), ALU.subtract).then_inc(op_lo, 1)

            def operand(k, op, tile0):
                op_low(k, op[:, sl(tile0, 4), 1, :], op[:, sl(tile0, 4), 0, :])

            dve.wait_ge(par_ready, 1)
            dve.wait_ge(h_in, 8)
            for q in range(4):
                if q == 0:
                    gains(Lin(0), lambda j: h[:, j, :], Lin(PC_MIX))
                    for c in range(SLOTS):
                        split(Lin(c))
                else:
                    gains(Lin(q), lambda j: h[:, 4 * q + j, :], Lin(PC_MIX + 4 * q))
                operand(Lin(q), aop, Lin(4 * q))
            for c in range(SLOTS, AHEAD):
                split(Lin(c))

            def inverse(norm, dst):
                dve.wait_ge(ss_read, norm + 1)
                for d in dst:
                    done(v.reciprocal(d, d))
                done.sync()
            inverse(0, [rs[:, :]])

            def angles():
                dve.wait_ge(rope_in, 5 * 16)
                done(v.tensor_copy(turn[:, :], posi[:, :]))
                done.sync()
                done(v.tensor_scalar(ang[:, :], turn[:, :], invf[:, 0:1], None, ALU.mult))
                done.sync()
                magic = 1.5 * 2.0 ** 23
                done(v.tensor_scalar(turn[:, :], ang[:, :], 1.0 / (2 * math.pi), magic, ALU.mult, ALU.add))
                done.sync()
                done(v.tensor_scalar(turn[:, :], turn[:, :], magic, None, ALU.subtract))
                done.sync()
                c1 = 6.28125
                c2 = float(np.float32(np.round((2 * math.pi - c1) * 2 ** 20) / 2 ** 20))
                c3 = 2 * math.pi - c1 - c2
                for c in (c1, c2, c3):
                    done(v.scalar_tensor_tensor(ang[:, :], turn[:, :], -c, ang[:, :], ALU.mult, ALU.add))
                    done.sync()
                lim = 3.1415925
                done(v.tensor_scalar(sin[:, :], ang[:, :], lim, -lim, ALU.min, ALU.max))
                done(v.tensor_scalar(cos[:, :], ang[:, :], math.pi / 2, None, ALU.add))
                done.sync()
                done(v.tensor_scalar(turn[:, :], cos[:, :], math.pi, -2 * math.pi, ALU.is_gt, ALU.mult))
                done.sync()
                done(v.tensor_tensor(cos[:, :], cos[:, :], turn[:, :], ALU.add))
                done.sync()
                v.tensor_scalar(cos[:, :], cos[:, :], lim, -lim, ALU.min, ALU.max).then_inc(angle_ready, 1)

            def sum_banks(g, tiles, dst, src=None):
                dve.wait_ge(b_copied, (g + 1).v)
                b0 = 4 * g.mod(2)
                return v.tensor_tensor(dst, ps[:, b0:b0 + tiles, 0:T], tb[:, 0:tiles, :], ALU.add)

            def over_rms(g, tiles, dst, r):
                sum_banks(g, tiles, dst).then_inc(banks_free, 1)
                dve.wait_ge(banks_free, (g + 1).v)
                return v.tensor_tensor(dst, dst, spread(r[:, :], tiles), ALU.mult)

            def scaled(g, tiles, dst, r):
                done(over_rms(g, tiles, dst, r))
                done.sync()

            ph = PH["a_in"]
            for c in range(AHEAD, ph.n + AHEAD):
                split(Lin(c))
                if c == AHEAD:
                    angles()
                if c in (11, 19):
                    g = (c - 11) // 8
                    if g == 1:
                        dve.wait_ge(sq_done, SQ0["lat"] + 1)
                    over_rms(Lin(g), 4, cg[:, :, :], rs).then_inc(lat_ready, 1)
                    dve.wait_ge(lat_ready, g + 1)
                    gains(Lin(OP0["lat"] + g), lambda j: cg[:, j, :], Lin(PC_GQ if g == 0 else PC_GKV))
                    operand(Lin(OP0["lat"] + g), cop, Lin(4 * g))
                if c == 21:
                    dve.wait_ge(trig_ready, 1)
                    dve.wait_ge(op_lo, OP0["lat"] + 2)
                    g = Lin(2)
                    sum_banks(g, 1, cv[:, 2:3, :]).then_inc(banks_free, 1)
                    dve.wait_ge(banks_free, 3)
                    v.tensor_tensor(cv[:, 2, :], cv[:, 2, :], rs[:, :], ALU.mult).then_inc(rope_x, 1)
                    dve.wait_ge(rope_x, 1)
                    inverse(1, [rsq[:, :]])
                    inverse(2, [rsk[:, :]])
                    v.reciprocal(rs_col[:, 0:2], rs_col[:, 0:2]).then_inc(ckv_cols, 1)
                    dve.wait_ge(rope_rot, 1)
                    done(v.tensor_tensor(tb[:, 3, :], ps[:, 6, 0:T], sin[:, :], ALU.mult))
                    done(v.tensor_tensor(cv[:, 2, :], cv[:, 2, :], cos[:, :], ALU.mult))
                    done.sync()
                    v.tensor_tensor(kr[:, :], cv[:, 2, :], tb[:, 3, :], ALU.add).then_inc(rope_read, 1)

            ph = PH["a_q"]
            for g in range(4):
                dve.wait_ge(b_copied, ph.g0 + g + 1)
                done(v.tensor_tensor(cg[:, :, :], ps[:, 0:4, 0:T], tb[:, :, :], ALU.add))
                dve.wait_ge(b2_copied, g + 1)
                v.tensor_tensor(cv[:, 2:4, :], ps[:, 4:6, 0:T], cv[:, 0:2, :], ALU.add).then_inc(banks_free, 1)
                done.sync()
                v.tensor_tensor(qn[:, 4 * g:4 * g + 4, :], cg[:, :, :], spread(rsq[:, :], 4), ALU.mult).then_inc(q_ready, 1)
                dve.wait_ge(banks_free, ph.g0 + g + 1)
                v.tensor_tensor(cv[:, 2:4, :], cv[:, 2:4, :], spread(rsq[:, :], 2), ALU.mult).then_inc(rope_x, 1)
                dve.wait_ge(rope_x, g + 2)
                dve.wait_ge(rope_rot, g + 2)
                dve.wait_ge(q_ready, 2 * g + 1)
                done(v.tensor_tensor(cg[:, 2:4, :], ps[:, 6, :].rearrange("p (m t) -> p m t", m=2),
                                     spread(sin[:, :], 2), ALU.mult))
                v.tensor_tensor(cg[:, 0:2, :], cv[:, 2:4, :], spread(cos[:, :], 2), ALU.mult).then_inc(rope_read, 1)
                dve.wait_ge(rope_read, g + 2)
                if g == 0:
                    dve.wait_ge(bias_out, 16)
                v.tensor_tensor(qr[:, 2 * g:2 * g + 2, :], cg[:, 0:2, :], cg[:, 2:4, :], ALU.add).then_inc(q_ready, 1)
                dve.wait_ge(q_ready, 2 * g + 2)
                for c in range(4):
                    split(Lin(ph.c0 + AHEAD + 4 * g + c))

            ph = PH["a_kv"]

            def kv_groups(i, t=0):
                for gi in range(2):
                    k = Lin(gi + 2 * t, 2, i)
                    g = k + ph.g0
                    sum_banks(g, 2, cg[:, 0:2, :]).then_inc(banks_free, 1)
                    dve.wait_ge(banks_free, (g + 1).v)
                    v.tensor_tensor(kn[:, sl(k.times(2), 2), :], cg[:, 0:2, :], spread(rsk[:, :], 2), ALU.mult).then_inc(k_ready, 1)
                    dve.wait_ge(k_ready, (k + 1).v)

            def kv_body(i):
                kv_groups(i)
                for c in range(4):
                    split(Lin(ph.c0 + AHEAD + c, 4, i))
            repeat(dve, 0, 3, kv_body)
            kv_groups(None, 3)

            def attention(u0, units, banks, loop_steps, masked, sinks, out_low):
                def maxes(u):
                    p, bank = u.mod(2), banks[0] + 2 * u.mod(2)
                    dve.wait_ge(s_done, (u + u0 + 1).v)
                    if u.i is not None or u.c >= 2:
                        dve.wait_ge(pn_done, (u + u0 - 1).v)
                    if sinks:
                        dve.wait_ge(bias_staged, (u + 1).v)
                    v.memset(fence[:, p:p + 1], 0.0)
                    for hh in range(2):
                        for q, cols in ((0, slice(0, P)), (1, slice(P, 384))):
                            k = 2 * hh + q
                            done(v.tensor_tensor_reduce(out=sm[:, p, hh, cols], in0=ps[:, bank + hh, cols],
                                                        in1=masked(p, hh, q), scale=1.0, scalar=-3.0e38,
                                                        op0=ALU.add, op1=ALU.max, accum_out=ri[:, p, k:k + 1]))
                    done.sync()
                    if sinks:
                        a = nsink[:, sl(u.times(2), 2)]
                        z = v.scalar_tensor_tensor(nm[:, p, :].rearrange("p (h q) -> p h q", h=2),
                                                   ri[:, p, :].rearrange("p (h q) -> p h q", h=2), -1.0,
                                                   bass.AP(a.tensor, a.offset, list(a.ap) + [[0, 2]]),
                                                   ALU.mult, ALU.min)
                    else:
                        z = v.tensor_scalar(nm[:, p, :], ri[:, p, :], -1.0, None, ALU.mult)
                    z.then_inc(m_done, 1)

                def normal(u):
                    p = u.mod(2)
                    dve.wait_ge(p_done, (u + u0 + 1).v)
                    if sinks:
                        done(v.tensor_tensor(ls[:, p, :], ls[:, p, :], es[:, p, :], ALU.add))
                        done.sync()
                    done(v.reciprocal(ri[:, p, :], ls[:, p, :]))
                    done.sync()
                    if u.i is not None or u.c >= 2:
                        dve.wait_ge(pt_done, (u + u0 - 1).v)
                    for hh in range(2):
                        for q, cols in ((0, slice(0, P)), (1, slice(P, 384))):
                            k = 2 * hh + q
                            z = v.tensor_scalar(pn[p][:, hh, cols], sm[:, p, hh, cols], ri[:, p, k:k + 1], None, ALU.mult)
                    z.then_inc(pn_done, 1)

                def low(u):
                    dve.wait_ge(att_hi, (u + u0 + 1).v)
                    out_low(u).then_inc(att_lo, 1)

                def step(u, ahead=True):
                    if ahead:
                        maxes(u + 1)
                    normal(u)
                    if u.i is not None or u.c >= 2:
                        low(u - 2)
                maxes(Lin(0))
                step(Lin(0))
                step(Lin(1))
                done.loop(1, units // 2 - 1, loop_steps, lambda i: [step(Lin(k, 2, i)) for k in range(2)])
                step(Lin(units - 2))
                step(Lin(units - 1), ahead=False)
                low(Lin(units - 2))
                low(Lin(units - 1))

            dve.wait_ge(mask_in, 16)
            banks = attention_banks(PH["a_out"])
            attention(0, UNITS_A, banks, 10, lambda p, hh, q: mask[:, 0:P] if q == 0 else mask[:, P:384], False,
                      lambda u, o=banks[2]: v.tensor_tensor(oop[:, sl(u.times(2), 2), 1, :],
                                                ps[:, o + u.mod(2), :].rearrange("p (m t) -> p m t", m=2),
                                                oop[:, sl(u.times(2), 2), 0, :].bitcast(F32), ALU.subtract))
            for c in range(SLOTS, AHEAD):
                split(Lin(PH["a_out"].c0 + c))

            def add_residual(g, tile0):
                dve.wait_ge(b_copied, (g + 1).v)
                b0 = 4 * g.mod(2)
                hh = h[:, sl(tile0, 4), :]
                done(v.tensor_tensor(hh, hh, ps[:, b0:b0 + 4, 0:T], ALU.add))
                done.sync()
                v.tensor_tensor(hh, hh, tb[:, :, :], ALU.add).then_inc(banks_free, 1)
                dve.wait_ge(banks_free, (g + 1).v)

            def residual(ph, kts, k0, gain, static=False):
                per = kts // 2
                turns = ph.n // (2 * per)

                def body(i, t=0):
                    for j in range(2 * per):
                        split(Lin(ph.c0 + AHEAD + j + 2 * per * t, 2 * per, i))
                        gi, at = divmod(j, per)
                        tile0 = Lin(4 * gi + 8 * t, 8, i)
                        if at == per - 5:
                            add_residual(Lin(ph.g0 + gi + 2 * t, 2, i), tile0)
                        if at == per - 4 and k0 is not None:
                            gains(Lin(k0 + gi, 2, i), lambda m: h[:, sl(tile0 + m, 1), :], Lin(gain + 4 * gi, 8, i))
                        if at == per - 2 and k0 is not None:
                            operand(Lin(k0 + gi, 2, i), aop, tile0)
                if static:
                    for t in range(turns):
                        body(None, t)
                else:
                    done.loop(0, turns, 2, body)

            def conv(layer, dst, tile0):
                w = PC_CONVW + layer * 3 * CT
                for m in range(4):
                    done(v.tensor_scalar(dst[:, m, :], up[:, m, 2:T + 2], col(tile0 + (w + 2 * CT + m)),
                                         col(tile0 + (PC_CONVB + layer * CT + m)), ALU.mult, ALU.add))
                done.sync()
                for tap in (1, 0):
                    for m in range(4):
                        z = v.scalar_tensor_tensor(dst[:, m, :], up[:, m, tap:T + tap], col(tile0 + (w + tap * CT + m)),
                                                   dst[:, m, :], ALU.mult, ALU.add)
                        if tap:
                            done(z)
                    if tap:
                        done.sync()
                return z

            def ffn_in(ph, layer, k0):
                def body(i):
                    for j in range(16):
                        split(Lin(ph.c0 + AHEAD + j, 16, i))
                        gi = j // 8
                        if j in (3, 11):
                            g = Lin(ph.g0 + gi, 2, i)
                            if gi == 1:
                                dve.wait_ge(conv_ready, Lin(k0 - CONV0[k0] + 1, 1, i).v)
                            scaled(g, 4, up[:, :, 2:T + 2], rs)
                        if j == 5:
                            conv(layer, cg, Lin(0, 4, i)).then_inc(conv_ready, 1)
                        if j == 12:
                            done(conv(layer, cv, Lin(FT, 4, i)))
                            done.sync()
                        if j == 13:
                            dve.wait_ge(silu_ready, Lin(k0 - CONV0[k0] + 1, 1, i).v)
                            v.tensor_tensor(cv[:, :, :], cv[:, :, :], cg[:, :, :], ALU.mult).then_inc(t_ready, 1)
                        if j == 15:
                            operand(Lin(k0, 1, i), gop, Lin(0, 4, i))
                            dve.wait_ge(op_lo, Lin(k0 + 1, 1, i).v)
                done.loop(0, 11, 19, body)

            residual(PH["a_out"], KT, OP0["a_out"], PC_FFN)
            inverse(3, [rs[:, :]])
            dve.wait_ge(op_lo, OP0["a_out"] + 4)
            dve.wait_ge(const_set, 2)
            ffn_in(PH["f0_in"], 0, OP0["f0_in"])
            residual(PH["f0_out"], FT, OP0["f0_out"], PC_MIX + KT)
            inverse(4, [rs[:, :], rs_col[:, 2:4]])

            ph = PH["b_in"]

            dve.wait_ge(op_lo, OP0["f0_out"] + 4)
            for j in range(SLOTS):
                split(Lin(ph.c0 + AHEAD + j))
            scaled(Lin(ph.g0), 2, cg[:, 0:2, :], rs)
            for m in range(2):
                z = v.tensor_scalar(cv[:, m, :], cg[:, m, :], col(Lin(PC_BQKV + KT + m)), None, ALU.add)
            z.then_inc(kd_src, 1)
            b0 = 4 * (ph.g0 % 2)
            dve.wait_ge(swa_in, 32)
            for half in range(2):
                v.scalar_tensor_tensor(vb[:, half, :], ps[:, b0 + 2 + half, 0:T], rs_col[:, 2 + half:3 + half],
                                       bvrow, ALU.mult, ALU.add).then_inc(vb_ready, 1)

            def b_body(i):
                for j in range(16):
                    split(Lin(ph.c0 + AHEAD + SLOTS + j, 16, i))
                    if j in (7, 15):
                        gi = j // 8
                        scaled(Lin(ph.g0 + 1 + gi, 2, i), 4, cg[:, :, :], rs)
                        for m in range(4):
                            done(v.tensor_scalar(qb[:, sl(Lin(4 * gi + m, 8, i), 1), :], cg[:, m, :],
                                                 col(Lin(PC_BQKV + 4 * gi + m, 8, i)), DH ** -0.5, ALU.add, ALU.mult))
                        done.sync()
            done.loop(0, 2, 10, b_body)
            v.tensor_scalar(nsink[:, :], sinkc[:, :], -1.0, None, ALU.mult).then_inc(nsink_ready, 1)
            dve.wait_ge(nsink_ready, 1)
            banks = attention_banks(PH["b_out"])
            attention(UNITS_A, UNITS_B, banks, 12,
                      lambda p, hh, q: st_b[:, p, hh, P:T] if q == 0 else st_b[:, p, hh, :],
                      True,
                      lambda u, o=banks[2]: v.tensor_tensor(oop[:, sl(u, 1), 1, :], ps[:, o + u.mod(2), 0:T],
                                                oop[:, sl(u, 1), 0, :].bitcast(F32), ALU.subtract))
            for c in range(SLOTS, AHEAD):
                split(Lin(PH["b_out"].c0 + c))
            residual(PH["b_out"], KT, OP0["b_out"], PC_FFN + KT)
            inverse(5, [rs[:, :]])
            dve.wait_ge(op_lo, OP0["b_out"] + 4)
            ffn_in(PH["f1_in"], 1, OP0["f1_in"])
            residual(PH["f1_out"], FT, None, None, static=True)

            dve.wait_ge(sq_done, NORM_SQ[6])
            for m in range(KT):
                z = v.tensor_scalar(h[:, m, :], h[:, m, :], col(Lin(PC_FIN + m)), None, ALU.mult)
                if m % 4 == 3:
                    z.then_inc(y_scaled, 1)
            dve.wait_ge(ss_read, 7)
            v.reciprocal(rs_col[:, 4:6], rs_col[:, 4:6]).then_inc(sqrt_done, 1)

        @block.gpsimd
        def _(pool):
            g_ = nc.gpsimd
            done = Steps(pool, pool_done)
            g_.memset(ones[:, :], 1.0)
            g_.memset(eps[:, 0:1], EPS)
            g_.memset(sqa[:, :], 0.0)
            g_.memset(eps[:, 1:2], EPS * (NOPE + ROPE)).then_inc(const_set, 1)

            def squares(src, tmp, acc, k):
                done(g_.tensor_tensor(tmp, src, src, ALU.mult))
                done.sync()
                for j in range(4):
                    z = g_.tensor_tensor(acc[:, :], acc[:, :], tmp[:, j, :], ALU.add)
                    if j < 3:
                        done(z)
                        done.sync()
                z.then_inc(sq_done, 1)

            pool.wait_ge(h_in, 8)
            pool.wait_ge(const_set, 1)
            for q in range(4):
                squares(h[:, 4 * q:4 * q + 4, :], up[:, :, 0:T], sqa, q)
                pool.wait_ge(sq_done, q + 1)
            pool.wait_ge(ss_ready, 1)
            done(g_.memset(sqa[:, :], 0.0))
            done(g_.memset(sqb[:, :], 0.0))
            done.sync()
            for g in range(2):
                pool.wait_ge(lat_ready, g + 1)
                squares(cg[:, :, :], up[:, :, 0:T], (sqa, sqb)[g], 4 + g)
                pool.wait_ge(sq_done, 5 + g)
            pool.wait_ge(rope_in, 5 * 16)
            g_.memset(relb[BUCKETS:BUCKETS + 1, :], 1.0).then_inc(brow_ready, 1)
            pool.wait_ge(brow_ready, 2)
            pool.dma_start(bias_dram, bass.AP(brow[:, :].tensor, brow[:, :].offset,
                                              [list(brow[:, :].ap[0]), [0, P], [1, 384]])).then_inc(bias_out, 16)
            pool.wait_ge(ss_ready, 3)
            pool.wait_ge(chunk_used, PH["a_in"].c1)
            done(g_.memset(sqa[:, :], 0.0))
            pool.dma_start(mask[:, :], c_mask).then_inc(mask_in, 16)

            pool.wait_ge(q_ready, 8)
            pool.wait_ge(v_ready, 2 * PH["a_kv"].ng)

            def stage(u, u0, copies, read, staged, place):
                if u.i is not None or u.c >= 2:
                    pool.wait_ge(read, (u + u0 - 1).v)
                    g_.tensor_tensor(fence[:, place:place + 1], ones[:, 0:1], ones[:, 0:1], ALU.mult)
                copies(u, u.mod(2)).then_inc(staged, 1)

            def q_a(u):
                def copies(u, p):
                    g_.tensor_copy(st_q[:, p, :, :], qn[:, sl(u.times(2), 2), :])
                    return g_.tensor_copy(st_r[:, p, :], qr[:, sl(u, 1), :])
                stage(u, 0, copies, s_done, stq, 2 + u.mod(2))

            def v_a(u):
                def copies(u, p):
                    return g_.tensor_copy(st_v[:, p, :, :], va[:, :, sl(u.times(T), T)])
                stage(u, 0, copies, pv_done, stv, 4 + u.mod(2))

            def step_a(u):
                q_a(u + 2)
                v_a(u)
            q_a(Lin(0))
            q_a(Lin(1))
            step_a(Lin(0))
            step_a(Lin(1))
            repeat(pool, 1, UNITS_A // 2 - 1, lambda i: [step_a(Lin(k, 2, i)) for k in range(2)])
            v_a(Lin(UNITS_A - 2))
            v_a(Lin(UNITS_A - 1))

            def residual_squares(ph, sq0):
                def body(i):
                    for gi in range(2):
                        pool.wait_ge(banks_free, Lin(ph.g0 + gi + 1, 2, i).v)
                        squares(h[:, sl(Lin(4 * gi, 8, i), 4), :], cg[:, :, :], sqa, None)
                        pool.wait_ge(sq_done, Lin(sq0 + gi + 1, 2, i).v)
                done.loop(0, 2, 8, body)
            residual_squares(PH["a_out"], SQ0["a_out"])
            pool.wait_ge(ss_ready, 4)
            done(g_.memset(sqa[:, :], 0.0))
            g_.memset(up[:, :, 0:2], 0.0).then_inc(const_set, 1)
            done.sync()
            residual_squares(PH["f0_out"], SQ0["f0_out"])
            pool.wait_ge(ss_ready, 5)
            done(g_.memset(sqa[:, :], 0.0))
            done.sync()

            pool.wait_ge(chunk_used, PH["f0_out"].c1)
            pool.wait_ge(bias_out, 16)
            bias_toeplitz = bass.AP(bias_dram.tensor, P - 1, [[383, P], [P * 384, HEADS_B], [1, T]])
            pool.dma_start(bt[:, :, :], bias_toeplitz).then_inc(bt_in, 16)
            pool.dma_start(sinkc[:, :], bass.AP(swa_sinks.tensor, 0, [[0, P], [1, HEADS_B]])).then_inc(swa_in, 16)
            pool.dma_start(bvrow, bass.AP(swa_b_qkv.tensor, QKV_B - T, [[0, P], [1, T]])).then_inc(swa_in, 16)

            pool.wait_ge(bt_in, 16)
            pool.wait_ge(vb_ready, 2)
            pool.wait_ge(chunk_used, PH["b_in"].c1)

            def q_b(u, kv):
                def queries(u, p):
                    z = g_.tensor_copy(st_qb[:, p, :], qb[:, sl(u, 1), :])
                    if kv is not None:
                        pool.wait_ge(kd_ready, 1 if kv.i is None and kv.c == 0 else 2)
                        z = g_.tensor_copy(st_k[:, p, :], kd[:, sl(kv, 1), :])
                    return z

                def biases(u, p):
                    return g_.tensor_copy(st_b[:, p, :, :], bt[:, sl(u.times(2), 2), :])
                stage(u, UNITS_A, queries, s_done, stq, 2 + u.mod(2))
                stage(u, UNITS_A, biases, m_done, bias_staged, 6 + u.mod(2))

            def v_b(u, kv):
                def copies(u, p):
                    if kv is None:
                        return g_.tensor_tensor(fence[:, 8 + p:9 + p], ones[:, 0:1], ones[:, 0:1], ALU.mult)
                    return g_.tensor_copy(st_vb[:, p, :, :], vb[:, :, sl(kv.times(DH), DH)])
                stage(u, UNITS_A, copies, pv_done, stv, 4 + u.mod(2))

            def turn_b(i, t=0, last=False):
                for k in range(4):
                    if not (last and k >= 2):
                        q_b(Lin(k + 2 + 4 * t, 4, i), Lin(t + 1, 1, i) if k >= 2 else None)
                    v_b(Lin(k + 4 * t, 4, i), Lin(t, 1, i) if k < 2 else None)
            for k in range(2):
                q_b(Lin(k), Lin(0))
            turn_b(None)
            repeat(pool, 1, KV_B - 1, turn_b)
            turn_b(None, KV_B - 1, last=True)
            residual_squares(PH["b_out"], SQ0["b_out"])
            pool.wait_ge(ss_ready, 6)
            done(g_.memset(sqa[:, :], 0.0))
            done.sync()
            residual_squares(PH["f1_out"], SQ0["f1_out"])


CONV0 = {OP0["f0_in"]: OP0["f0_in"], OP0["f1_in"]: OP0["f1_in"] - 11}


def tables():
    ident = np.eye(P, dtype=np.float32)
    rot = np.zeros((P, P), np.float32)
    half = ROPE // 2
    for m in range(P):
        b, r = divmod(m, ROPE)
        if r < half:
            rot[b * ROPE + r + half, m] = -1.0
        else:
            rot[b * ROPE + r - half, m] = 1.0
    invf = (np.float32(THETA) ** (-np.arange(half, dtype=np.float32) / half)).astype(np.float32)
    invf = np.tile(invf, P // half).reshape(P, 1)
    tri = np.where(np.arange(P)[None, :] <= np.arange(P)[:, None], 0.0, NEG).astype(np.float32)
    mask = np.concatenate([tri, np.zeros((P, P), np.float32), tri], axis=1)
    dist = 255 - np.arange(384)
    n = np.clip(dist, 0, WINDOW - 1)
    exact = BUCKETS // 2
    big = exact + (np.log(np.maximum(n, 1) / exact) / math.log(MAX_DIST / exact) * (BUCKETS - exact)).astype(np.int32)
    bucket = np.where(n < exact, n, np.minimum(big, BUCKETS - 1))
    valid = (dist >= 0) & (dist <= WINDOW - 1)
    onehot = np.zeros((BUCKETS + 1, 384), np.float32)
    onehot[bucket[valid], np.nonzero(valid)[0]] = 1.0
    onehot[BUCKETS, ~valid] = NEG
    return {"c_ident": ident, "c_rot": rot, "c_invf": invf, "c_mask": mask, "c_onehot": onehot}


def kernel(**inputs):
    import concourse.bacc as bacc
    from concourse.bass_utils import run_bass_kernel_spmd as run

    shape = {
        "x": (T, D), "positions": (1, T), "rel_bias": (BUCKETS, HEADS_B), "norm_mix": (2 * KT, P),
        "norm_ffn": (2 * KT, P), "mla_w_in": (D, 2 * RANK + ROPE), "mla_g_q": (4, P), "mla_g_kv": (4, P),
        "mla_w_qb": (RANK, HEADS_A * (NOPE + ROPE)), "mla_w_kvb": (RANK, HEADS_A * (NOPE + VDIM)),
        "mla_w_o": (HEADS_A * VDIM, D), "swa_w_qkv": (D, QKV_B), "swa_b_qkv": (QKV_B // P, P),
        "swa_sinks": (1, HEADS_B), "swa_w_o": (HEADS_B * DH, D), "swa_b_o": (KT, P),
        "ffn_w_in": (2, D, 2 * FF), "ffn_conv_w": (2 * 3 * CT, P), "ffn_conv_b": (2 * CT, P),
        "ffn_w_out": (2, FF, D), "final_norm": (KT, P),
    }
    nc = bacc.Bacc("TRN2", target_bir_lowering=False, num_devices=1)
    arrays, args = {}, []
    for name, s in shape.items():
        arrays[name] = np.ascontiguousarray(inputs[name]).reshape(s)
    arrays.update(tables())
    for name, a in arrays.items():
        args.append(nc.dram_tensor(name, a.shape, mybir.dt.from_np(a.dtype), kind="ExternalInput").ap())
    y = nc.dram_tensor("y", (T, D), F32, kind="ExternalOutput").ap()
    build(nc, *args, y)
    r = run(nc, [arrays], core_ids=[0])
    return r.results[0]["y"].reshape(1, T, D)
```

```python
import math
from contextlib import ExitStack

import numpy as np
import concourse.bass as bass
from concourse import mybir

F32 = mybir.dt.float32
F32R = mybir.dt.float32r
I32 = mybir.dt.int32
ALU = mybir.AluOpType
ACT = mybir.ActivationFunctionType

P = 128
T = 256
D = 2048
KT = D // P
FF = 5632
FT = FF // P
RANK = 512
HEADS_A, NOPE, ROPE, VDIM = 16, 128, 64, 128
HEADS_B, KV_B, DH = 32, 4, 64
QKV_B = (HEADS_B + 2 * KV_B) * DH
EPS = 1e-6
NEG = -1e30
THETA = 10000.0
BUCKETS, MAX_DIST, WINDOW = 32, 2048, 128

SLOTS = 4
CH = 1024
EARLY = 2
AHEAD = 8
AHEAD_2 = 6
QCOLS = 2 * (NOPE + ROPE)
COLS = 512

PC_MIX, PC_FFN, PC_FIN, PC_GQ, PC_GKV, PC_BQKV, PC_BO = 0, 32, 64, 80, 84, 88, 108
PC_END0 = 124
PC_CONVW = 128
CT = 2 * FT
FFN_TURNS = FT // 4
PC_CONVB = PC_CONVW + 2 * 3 * CT
PC_END = PC_CONVB + 2 * CT


class Phase:
    def __init__(self, chunk0, chunks, group0, groups):
        self.c0, self.n, self.g0, self.ng = chunk0, chunks, group0, groups
        self.c1, self.g1 = chunk0 + chunks, group0 + groups


def phases():
    out, c, g = {}, 0, 0
    for name, n, m in (("a_in", 18, 3), ("a_q", 16, 8), ("a_kv", 16, 8), ("a_out", 32, 4),
                       ("f0_in", 176, 22), ("f0_out", 88, 4), ("b_in", 40, 5), ("b_out", 32, 4),
                       ("f1_in", 176, 22), ("f1_out", 88, 4)):
        out[name] = Phase(c, n, g, m)
        c, g = c + n, g + m
    return out, c


PH, CHUNKS = phases()
OP0 = {"x": 0, "lat": 4, "a_out": 6, "f0_in": 10, "f0_out": 21, "b_out": 25, "f1_in": 29}
SQ0 = {"x": 0, "lat": 4, "a_out": 6, "f0_out": 10, "b_out": 14, "f1_out": 18}
NORM_SQ = [4, 5, 6, 10, 14, 18, 21]
UNITS_A, UNITS_B = HEADS_A // 2, HEADS_B // 2


def attention_banks(ph_out):
    scores = 4 * (ph_out.g0 % 2)
    return scores, 4 - scores, 6 - scores


OUT_BANKS = [(4 * (PH["f1_out"].g1 % 2) + 2 * k) % 8 for k in range(4)]


class Lin:
    def __init__(self, c, k=0, i=None):
        self.c, self.k, self.i = c, k, i

    def __add__(self, d):
        return Lin(self.c + d, self.k, self.i)

    def __sub__(self, d):
        return self + (-d)

    def times(self, m):
        return Lin(self.c * m, self.k * m, self.i)

    def over(self, d):
        assert self.i is None or self.k % d == 0
        return Lin(self.c // d, self.k // d, self.i)

    def mod(self, d):
        assert self.i is None or self.k % d == 0
        return self.c % d

    @property
    def v(self):
        return self.c if self.i is None else self.i * self.k + self.c


def sl(n, size):
    return slice(n.v, n.v + size) if n.i is None else bass.ds(n.v, size)


def repeat(eng, start, end, body):
    if end > start:
        with eng.Fori(start, end) as i:
            body(i)


class Steps:
    def __init__(self, eng, sem):
        self.eng, self.sem, self.n, self.at = eng, sem, 0, None

    def __call__(self, ins):
        ins.then_inc(self.sem, 1)
        self.n += 1
        return ins

    def sync(self):
        self.eng.wait_ge(self.sem, Lin(self.n, *(self.at or ())).v)

    def loop(self, start, end, per, body):
        n0 = self.n

        def inner(i):
            self.n, self.at = n0 - start * per, (per, i)
            body(i)
            assert self.n == n0 - start * per + per, f"steps in the loop: {self.n - n0 + start * per}"
        if end > start:
            repeat(self.eng, start, end, inner)
        self.n, self.at = n0 + (end - start) * per, None


def build(nc, x, positions, rel_bias, small, conv_par, mla_w_in, mla_w_qb, mla_w_kvb, mla_w_o,
          swa_w_qkv, swa_b_v, swa_sinks, swa_w_o, ffn_w_in, ffn_w_out, c_ident, c_rot, c_invf, c_mask,
          c_onehot, out):
    bias_dram = nc.dram_tensor("bias_rows", [HEADS_B, P, 384], F32, kind="Internal").ap()

    top = [(nc.sbuf_base + 63) // 64 * 64]

    def region(nbytes):
        at = top[0]
        top[0] += (nbytes + 31) // 32 * 32
        assert top[0] <= nc.sbuf_usable_end, (top[0], nc.sbuf_usable_end)
        return at

    def place(name, shape, dt, at):
        return nc.alloc_sbuf_tensor_at(name, shape, dt, offset=at)

    def new(name, shape, dt=F32):
        return place(name, shape, dt, region(int(np.prod(shape[1:])) * 4))

    raw = [new(f"raw{s}", [P, CH]) for s in range(SLOTS)]
    w_hi = [new(f"w_hi{s}", [P, CH], F32R) for s in range(SLOTS)]
    w_lo = [new(f"w_lo{s}", [P, CH], F32R) for s in range(SLOTS)]
    h = new("h", [P, KT, T])
    r_half_b, r_cg = region(4 * T * 4), region(4 * T * 4)
    half_b = place("half_b", [P, 4, T], F32, r_half_b)
    cg = place("cg", [P, 4, T], F32, r_cg)
    cv = new("cv", [P, 4, T])
    up = new("up", [P, 4, T + 2])
    par = new("par", [P, 7 * P])
    ident = new("ident", [P, P])
    ones = new("ones", [P, P])
    inv_rms = new("inv_rms", [P, T])
    rs_col = new("rs_col", [P, 6])
    sqa = new("sqa", [P, T])
    eps = new("eps", [P, 2])
    neg_max = new("neg_max", [P, 2, 4])
    exp_sums = new("exp_sums", [P, 2, 4])
    sink_exps = new("sink_exps", [P, 2, 4])
    ri = new("ri", [P, 2, 4])
    sinkc = new("sinkc", [P, HEADS_B])
    nsink = new("nsink", [P, HEADS_B])
    fence = new("fence", [P, 12])
    probs = [place("probs0", [P, 2, 384], F32, r_cg), place("probs1", [P, 2, 384], F32, r_half_b)]

    ra = region(KT * 2 * T * 4)
    op_in = place("op_in", [P, KT, 2, T], F32R, ra)
    yt = place("yt", [P, 2, D], F32, ra)
    probs_t = [place("probs_t0", [P, 2, 384], F32, ra), place("probs_t1", [P, 2, 384], F32, ra + 29312)]
    scores_sb = place("scores_sb", [P, 2, 2, 384], F32, ra + 3072)
    st_q = place("st_q", [P, 2, 2, T], F32, ra + 9216)
    st_r = place("st_r", [P, 2, T], F32, ra + 13312)
    st_v = place("st_v", [P, 2, 2, T], F32, ra + 15360)
    mask = place("mask", [P, 384], F32, ra + 19456)
    k_rope = place("k_rope", [P, T], F32, ra + 20992)
    xr = place("xr", [P, 2, T], F32, ra + 22016)
    xt = place("xt", [P, 2, T], F32, ra + 24064)
    xk = place("xk", [P, T], F32, ra + 26112)
    brow = place("brow", [HEADS_B, 384], F32, ra + 27136)
    st_qb = place("st_qb", [P, 2, T], F32, ra + 9216)
    st_k = place("st_k", [P, 2, T], F32, ra + 11264)
    st_vb = place("st_vb", [P, 2, 2, DH], F32, ra + 15360)
    st_b = place("st_b", [P, 2, 2, T], F32, ra + 16384)
    k_both = place("k_both", [P, KV_B, T], F32, ra + 22016)

    rg = region(FT * 2 * T * 4)
    r_o = rg + 57344
    op_ffn = place("op_ffn", [P, FT, 2, T], F32R, rg)
    op_att = place("op_att", [P, KT, 2, T], F32R, r_o)
    op_lat = place("op_lat", [P, 8, 2, T], F32R, r_o)
    xin = place("xin", [P, 2, D], F32, rg)
    praw = place("praw", [P, 7, P], F32, rg + 16384)
    onehot = place("onehot", [BUCKETS + 1, 384], F32, rg + 20480)
    relb = place("relb", [BUCKETS + 1, HEADS_B], F32, rg + 22016)
    q_nope = place("q_nope", [P, HEADS_A, T], F32, rg)
    q_rope = place("q_rope", [P, UNITS_A, T], F32, rg + 16384)
    k_nope = place("k_nope", [P, HEADS_A, T], F32, rg + 24576)
    v_mla = place("v_mla", [P, 2, HEADS_A * VDIM], F32, rg + 40960)
    cos = place("cos", [P, T], F32, r_o + 16384)
    sin = place("sin", [P, T], F32, r_o + 17408)
    rot = place("rot", [P, P], F32, r_o + 18432)
    rsq = place("rsq", [P, T], F32, r_o + 18944)
    rsk = place("rsk", [P, T], F32, r_o + 19968)
    sqb = place("sqb", [P, T], F32, r_o + 20992)
    ang = place("ang", [P, T], F32, r_o + 22016)
    turn = place("turn", [P, T], F32, r_o + 23040)
    posi = place("posi", [P, T], I32, r_o + 24064)
    invf = place("invf", [P, 1], F32, r_o + 25088)
    q_win = place("q_win", [P, KT, T], F32, rg)
    win_bias = place("win_bias", [P, HEADS_B, T], F32, rg + 24576)
    v_win = cv[:, 2:4, :]
    bvrow = up[:, 0, 2:T + 2]

    ctx = ExitStack()
    with ctx:
        ps = ctx.enter_context(nc.psum_tensor("ps", [P, 8, 512], F32))

        def sem(name):
            return ctx.enter_context(nc.semaphore(name))

        x_in = [sem(f"x_in{q}") for q in range(4)]
        c_in = sem("c_in")
        par_in = sem("par_in")
        conv_in = sem("conv_in")
        rope_in = sem("rope_in")
        mask_in = sem("mask_in")
        bias_out = sem("bias_out")
        win_bias_in = sem("win_bias_in")
        sinks_in = sem("sinks_in")
        stored = sem("stored")
        const_set = sem("const_set")
        par_transposed = sem("par_transposed")
        par_ready = sem("par_ready")
        x_transposed = sem("x_transposed")
        h_in = sem("h_in")
        bias_row_product = sem("bias_row_product")
        brow_ready = sem("brow_ready")
        raw_full = [sem(f"raw_full{s}") for s in range(SLOTS)]
        hi_ready = sem("hi_ready")
        lo_ready = sem("lo_ready")
        chunk_used = sem("chunk_used")
        b_copied = sem("b_copied")
        banks_free = sem("banks_free")
        operand_in_cv = sem("operand_in_cv")
        operand_hi = sem("operand_hi")
        operand_lo = sem("operand_lo")
        squares_added = sem("squares_added")
        norm_sum = sem("norm_sum")
        norm_root_taken = sem("norm_root_taken")
        sqrt_done = sem("sqrt_done")
        dve_done = sem("dve_done")
        pool_done = sem("pool_done")
        lat_ready = sem("lat_ready")
        angle_ready = sem("angle_ready")
        trig_ready = sem("trig_ready")
        k_rope_ready = sem("k_rope_ready")
        rope_rotated = sem("rope_rotated")
        rope_read = sem("rope_read")
        q_ready = sem("q_ready")
        q_rope_ready = sem("q_rope_ready")
        v_ready = sem("v_ready")
        v_win_ready = sem("v_win_ready")
        k_ready = sem("k_ready")
        k_both_ready = sem("k_both_ready")
        nsink_ready = sem("nsink_ready")
        bias_staged = sem("bias_staged")
        q_placed = sem("q_placed")
        conv_ready = sem("conv_ready")
        silu_ready = sem("silu_ready")
        queries_staged = sem("queries_staged")
        values_staged = sem("values_staged")
        scores_done = sem("scores_done")
        maxima_done = sem("maxima_done")
        exps_done = sem("exps_done")
        probs_ready = sem("probs_ready")
        probs_transposed = sem("probs_transposed")
        probs_t_copied = sem("probs_t_copied")
        outputs_done = sem("outputs_done")
        outputs_hi = sem("outputs_hi")
        outputs_lo = sem("outputs_lo")
        y_scaled = sem("y_scaled")
        last_squares = sem("last_squares")
        y_transposed = sem("y_transposed")
        y_act = sem("y_act")
        y_dve = sem("y_dve")

        block = ctx.enter_context(nc.Block())

        @block.sync
        def _(sp):
            sp.dma_start(ident[:, :], c_ident).then_inc(c_in, 16)
            sp.dma_start(praw[0:PC_END0, 0, :], small).then_inc(par_in, 16)

            def load(n, w, row, col, tiles=2, cols=COLS):
                s = n.mod(SLOTS)
                if n.i is not None or n.c >= SLOTS:
                    sp.wait_ge(lo_ready, (n - (SLOTS - 1)).v)
                sp.dma_start(raw[s][:, 0:tiles * cols].rearrange("p (k c) -> p k c", k=tiles),
                             w[row:row + tiles * P, sl(col, cols)].rearrange("(k p) c -> p k c", p=P)
                             ).then_inc(raw_full[s], 16)

            def stream(ph, w, kts, cols):
                per = kts // 2
                turn_chunks = per * len(cols(None))
                turns = ph.n // turn_chunks

                def turn_body(i):
                    for gi, col in enumerate(cols(i)):
                        for c in range(per):
                            load(Lin(ph.c0 + gi * per + c, turn_chunks, i), w, c * 2 * P, col)
                repeat(sp, 0, turns, turn_body)

            ph = PH["a_in"]
            for g in range(2):
                for c in range(8):
                    if g == 0 and c < 4:
                        sp.dma_start(xin[:, :, c * 512:(c + 1) * 512],
                                     x[:, c * 512:(c + 1) * 512].rearrange("(h p) c -> p h c", h=2)).then_inc(x_in[c], 16)
                    load(Lin(ph.c0 + g * 8 + c), mla_w_in, c * 2 * P, Lin(g * COLS))
                    if g == 0 and c == 3:
                        sp.dma_start(praw[:, 1:6, :], conv_par[0:5 * P, :].rearrange("(b r) c -> r b c", b=5)
                                     ).then_inc(conv_in, 16)
                        sp.dma_start(praw[0:64, 6, :], conv_par[5 * P:5 * P + 64, :]).then_inc(conv_in, 16)
                        sp.dma_start(rot[:, :], c_rot).then_inc(rope_in, 16)
                        sp.dma_start(invf[:, :], c_invf).then_inc(rope_in, 16)
                        sp.dma_start(posi[:, :], bass.AP(positions.tensor, 0, [[0, P], [1, T]])).then_inc(rope_in, 16)
                        sp.dma_start(onehot[:, :], c_onehot).then_inc(rope_in, 16)
                        sp.dma_start(relb[0:BUCKETS, :], rel_bias).then_inc(rope_in, 16)
            for c in range(2):
                load(Lin(ph.c0 + 16 + c), mla_w_in, c * 8 * P, Lin(2 * RANK), 8, 2 * ROPE)
            ph = PH["a_q"]

            def q_body(i):
                for gi in range(2):
                    for c in range(2):
                        load(Lin(ph.c0 + 2 * gi + c, 4, i), mla_w_qb, 2 * c * P, Lin(gi * QCOLS, 2 * QCOLS, i),
                             2, QCOLS)
            repeat(sp, 0, 4, q_body)
            stream(PH["a_kv"], mla_w_kvb, 4, lambda i: [Lin(0, 1024, i), Lin(512, 1024, i)])
            two_groups = lambda i: [Lin(0, 1024, i), Lin(COLS, 1024, i)]
            gate_val = lambda i: [Lin(0, COLS, i), Lin(FF, COLS, i)]
            stream(PH["a_out"], mla_w_o, KT, two_groups)
            stream(PH["f0_in"], ffn_w_in[0], KT, gate_val)
            stream(PH["f0_out"], ffn_w_out[0], FT, two_groups)
            ph = PH["b_in"]
            for c in range(8):
                load(Lin(ph.c0 + c), swa_w_qkv, c * 2 * P, Lin(4 * COLS))
            stream(Phase(ph.c0 + 8, 32, ph.g0 + 1, 4), swa_w_qkv, KT, two_groups)
            stream(PH["b_out"], swa_w_o, KT, two_groups)
            stream(PH["f1_in"], ffn_w_in[1], KT, gate_val)
            stream(PH["f1_out"], ffn_w_out[1], FT, two_groups)
            for k in range(4):
                half, cols = k // 2, slice(k % 2 * (D // 2), (k % 2 + 1) * (D // 2))
                sp.wait_ge(y_act, k + 1)
                sp.wait_ge(y_dve, k + 1)
                sp.dma_start(out[half * P:(half + 1) * P, cols], yt[:, half, cols]).then_inc(stored, 16)
            sp.wait_ge(stored, 64)
            sp.wait_ge(bias_out, 16)

        @block.tensor
        def _(pe):
            mm = nc.tensor.matmul

            def feature_tile(bank, whi, wlo, op, start, stop, cols=T):
                def high():
                    return mm(ps[:, bank, 0:2 * T], whi, op, start=start, stop=stop)

                def low():
                    return mm(ps[:, bank, 0:T], wlo, op[:, 0, :], start=False, stop=False)
                if stop:
                    low()
                    return high()
                high()
                return low()

            def w_chunk(n, op, kt0, first, last, b0, tiles=(0, 1, 2, 3)):
                s = n.mod(SLOTS)
                pe.wait_ge(lo_ready, (n + 1).v)
                for j, m in enumerate(tiles):
                    for k in range(2):
                        c = k * COLS + m * P
                        z = feature_tile(b0 + j, w_hi[s][:, c:c + P], w_lo[s][:, c:c + P],
                                         op[:, kt0 + k, :, :], first and k == 0, last and k == 1)
                return z

            def token_chunk(n, op, kt0, first, last, bank, wcols):
                s = n.mod(SLOTS)
                for half in range(2):
                    t0 = half * P
                    for k in range(2):
                        hi, lo = op[:, kt0 + k, 0, t0:t0 + P], op[:, kt0 + k, 1, t0:t0 + P]
                        o = ps[:, bank + half, 0:T]
                        mm(o, hi, wcols(w_hi[s], k), start=first and k == 0, stop=False)
                        mm(o, hi, wcols(w_lo[s], k), start=False, stop=False)
                        z = mm(o, lo, wcols(w_hi[s], k), start=False, stop=last and k == 1)
                return z

            def banks_of(g):
                if g.i is not None or g.c >= 2:
                    pe.wait_ge(banks_free, (g - 1).v)
                return 4 * g.mod(2)

            def sum_squares(norm, src, bank, cols=False):
                pe.wait_ge(squares_added, NORM_SQ[norm])
                z = mm(ps[:, bank, 0:T], ones[:, :], src[:, :], start=True, stop=True)
                if cols:
                    for half in range(2):
                        z = mm(ps[:, bank, T + half:T + half + 1], src[:, half * P:(half + 1) * P],
                               ones[:, 0:1], start=True, stop=True)
                z.then_inc(norm_sum, 1)

            pe.wait_ge(c_in, 16)
            pe.wait_ge(par_in, 16)
            nc.tensor.transpose(ps[:, 0, 0:PC_END0], praw[0:PC_END0, 0, :], ident[0:PC_END0, 0:PC_END0]
                                ).then_inc(par_transposed, 1)
            for q in range(4):
                pe.wait_ge(x_in[q], 16)
                if q >= 2:
                    pe.wait_ge(h_in, 2 * (q - 1))
                for j in range(2):
                    for m in range(2):
                        for half in range(2):
                            z = nc.tensor.transpose(ps[:, 4 + 2 * (q % 2) + j, m * T + half * P:m * T + (half + 1) * P],
                                                    xin[:, half, (4 * q + 2 * j + m) * P:(4 * q + 2 * j + m + 1) * P],
                                                    ident[:, :])
                    z.then_inc(x_transposed, 1)

            def conv_parameters():
                pe.wait_ge(conv_in, 32)
                pe.wait_ge(h_in, 8)
                for b in range(1, 7):
                    n = 64 if b == 6 else P
                    z = nc.tensor.transpose(ps[:, 5 + (b - 1) // 4, (b - 1) % 4 * P:(b - 1) % 4 * P + n],
                                            praw[0:n, b, :], ident[0:n, 0:n])
                z.then_inc(par_transposed, 1)

            ph = PH["a_in"]
            pe.wait_ge(par_ready, 1)
            for g in range(2):
                for c in range(8):
                    if g == 0 and c % 2 == 0:
                        pe.wait_ge(operand_lo, OP0["x"] + c // 2 + 1)
                    if g == 1 and c == 0:
                        pe.wait_ge(norm_root_taken, 1)
                        pe.wait_ge(par_ready, 2)
                    w_chunk(Lin(ph.c0 + g * 8 + c), op_in, 2 * c, c == 0, c == 7,
                            banks_of(Lin(g)) if c == 0 else 4 * (g % 2)).then_inc(chunk_used, 1)
                    if g == 0 and c == 5:
                        conv_parameters()
                    if g == 0 and c == 6:
                        sum_squares(0, sqa, 4)
                    if g == 1 and c == 3:
                        sum_squares(1, sqa, 2)
            banks_of(Lin(2))
            for c in range(2):
                n = Lin(ph.c0 + 16 + c)
                pe.wait_ge(lo_ready, (n + 1).v)
                for k in range(8):
                    w = slice(k * P, (k + 1) * P)
                    z = feature_tile(0, w_hi[n.mod(SLOTS)][:, w], w_lo[n.mod(SLOTS)][:, w],
                                     op_in[:, 8 * c + k, :, :], c == 0 and k == 0, c == 1 and k == 7)
                z.then_inc(chunk_used, 1)
            pe.wait_ge(brow_ready, 1)
            pe.wait_ge(banks_free, 2)
            mm(ps[0:HEADS_B, 6, 0:384], relb[:, :], onehot[:, :], start=True, stop=True).then_inc(bias_row_product, 1)

            ph = PH["a_q"]

            def rotate(r, bank, src):
                if r.i is not None or r.c >= 1:
                    pe.wait_ge(banks_free, (r + PH["a_q"].g0).v)
                    pe.wait_ge(rope_read, r.v)
                else:
                    pe.wait_ge(k_rope_ready, 1)
                mm(ps[:, bank, 0:T], rot[:, :], src, start=True, stop=True).then_inc(rope_rotated, 1)

            def q_group(k):
                b0 = 3 * (k + 1).mod(2)
                pe.wait_ge(banks_free, (k + (ph.g0 - 1)).v)
                for c in range(2):
                    n = k.times(2) + (ph.c0 + c)
                    s = n.mod(SLOTS)
                    pe.wait_ge(lo_ready, (n + 1).v)
                    for m in range(3):
                        for kt in range(2):
                            w = slice(kt * QCOLS + m * P, kt * QCOLS + (m + 1) * P)
                            z = feature_tile(b0 + m, w_hi[s][:, w], w_lo[s][:, w], op_lat[:, 2 * c + kt, :, :],
                                             c == 0 and kt == 0, c == 1 and kt == 1)
                    z.then_inc(chunk_used, 1)
            pe.wait_ge(operand_lo, OP0["lat"] + 1)
            q_group(Lin(0))
            pe.wait_ge(rope_in, 5 * 16)
            pe.wait_ge(brow_ready, 2)
            rotate(Lin(0), 6, xk[:, :])
            sum_squares(2, sqb, 7)
            q_group(Lin(1))
            rotate(Lin(1), 6, xr[:, 0, :])

            def q_turn(i):
                for gi in range(2):
                    q_group(Lin(gi, 2, i))
                    rotate(Lin(gi, 2, i), 6, xr[:, (gi + 1) % 2, :])
            repeat(pe, 1, 3, q_turn)
            q_group(Lin(6))
            rotate(Lin(6), 6, xr[:, 1, :])
            q_group(Lin(7))
            rotate(Lin(7), 3, xr[:, 0, :])

            ph = PH["a_kv"]
            pe.wait_ge(operand_lo, OP0["lat"] + 2)
            pe.wait_ge(rope_read, 7)
            pe.wait_ge(norm_root_taken, 3)

            def value_columns(w, k):
                return w[:, k * COLS:(k + 1) * COLS].rearrange("p (h c) -> p h c", h=2)[:, :, P:2 * P]

            def kv_turn(i, first=False):
                for gi in range(2):
                    g = Lin(ph.g0 + gi, 2, i)
                    if first and gi == 1:
                        pe.wait_ge(rope_read, 9)
                    b0 = banks_of(g)
                    for c in range(2):
                        n = Lin(ph.c0 + 2 * gi + c, 4, i)
                        w_chunk(n, op_lat, 4 + 2 * c, c == 0, c == 1, b0, tiles=(0, 2))
                        token_chunk(n, op_lat, 4 + 2 * c, c == 0, c == 1, b0 + 2,
                                    value_columns).then_inc(chunk_used, 1)
                        if first and gi == 0 and c == 0:
                            rotate(Lin(8), 3, xr[:, 1, :])
            kv_turn(None, True)
            repeat(pe, 1, 4, kv_turn)

            def attention(u0, units, scores, values, banks, inputs, early):
                def score(u):
                    pe.wait_ge(queries_staged, (u + u0 + 1).v)
                    if u.i is not None or u.c >= 2:
                        pe.wait_ge(maxima_done, (u + u0 - 1).v)
                    scores(u, banks[0] + 2 * u.mod(2)).then_inc(scores_done, 1)

                def turn_p(u):
                    pe.wait_ge(probs_ready, (u + u0 + 1).v)
                    if u.i is not None or u.c + u0 >= 1:
                        pe.wait_ge(probs_t_copied, (u + u0).v)
                    for hh in range(2):
                        for blk in range(3):
                            z = nc.tensor.transpose(ps[:, banks[1] + hh, blk * P:(blk + 1) * P],
                                                    probs[u.mod(2)][:, hh, blk * P:(blk + 1) * P], ident[:, :])
                    z.then_inc(probs_transposed, 1)

                def value(u):
                    pe.wait_ge(probs_t_copied, (u + u0 + 1).v)
                    pe.wait_ge(values_staged, (u + u0 + 1).v)
                    if u.i is not None or u.c >= 2:
                        pe.wait_ge(outputs_lo, (u + u0 - 1).v)
                    values(u, banks[2] + u.mod(2)).then_inc(outputs_done, 1)

                def step(u, ahead=True):
                    if ahead:
                        score(u + 2)
                    turn_p(u)
                    value(u - 1)
                pe.wait_ge(banks_free, inputs.g1 - 1)
                score(Lin(0))
                score(Lin(1))
                score(Lin(2))
                pe.wait_ge(banks_free, inputs.g1)
                turn_p(Lin(0))
                step(Lin(1))
                repeat(pe, 1, units // 2 - 1, lambda i: [step(Lin(k, 2, i)) for k in range(2)])
                step(Lin(units - 2), ahead=False)
                pe.wait_ge(maxima_done, units + u0)
                early(0)
                step(Lin(units - 1), ahead=False)
                early(1)
                value(Lin(units - 1))

            def scores_a(u, bank):
                p = u.mod(2)
                for hh in range(2):
                    r = slice(64 * hh, 64 * hh + 64)
                    for q0, keys, o in ((0, P, 0), (P, T, P)):
                        o = ps[:, bank + hh, o:o + keys]
                        mm(o, st_q[:, p, hh, q0:q0 + P], k_nope[:, sl(u.times(2) + hh, 1), 0:keys],
                           start=True, stop=False)
                        z = mm(o, st_r[r, p, q0:q0 + P], k_rope[r, 0:keys], start=False, stop=True)
                return z

            def values_a(u, bank):
                p = u.mod(2)
                for hh in range(2):
                    v = slice(hh * VDIM, (hh + 1) * VDIM)
                    mm(ps[:, bank, hh * T:(hh + 1) * T], st_v[:, p, 0, v], probs_t[p][:, hh, 0:T],
                       start=True, stop=False)
                    z = mm(ps[:, bank, hh * T + P:(hh + 1) * T], st_v[:, p, 1, v], probs_t[p][:, hh, T:384],
                           start=False, stop=True)
                return z

            def early_chunk(ph, per_unit, u0):
                def chunk(c):
                    pe.wait_ge(outputs_lo, u0 + per_unit * (c + 1))
                    w_chunk(Lin(ph.c0 + c), op_att, 2 * c, c == 0, False, 4 * (ph.g0 % 2)).then_inc(chunk_used, 1)
                return chunk

            def groups(ph, op, kts, first_wait, norm=None, rs_cols=False, start=0, end=None):
                per = kts // 2
                turns = (ph.n // (2 * per)) if end is None else end

                def body(i, first=False):
                    for gi in range(2):
                        g = Lin(ph.g0 + gi, 2, i)
                        if first and gi == 1 and norm is not None:
                            pe.wait_ge(norm_root_taken, norm + 1)
                        b0 = banks_of(g)
                        for c in range(start if first and gi == 0 else 0, per):
                            if first and gi == 0:
                                first_wait(c)
                            w_chunk(Lin(ph.c0 + gi * per + c, 2 * per, i), op, 2 * c, c == 0, c == per - 1,
                                    b0).then_inc(chunk_used, 1)
                            if first and gi == 0 and c == 4 and norm is not None:
                                pe.wait_ge(banks_free, ph.g0)
                                sum_squares(norm, sqa, 4 - b0, rs_cols)
                body(None, True)
                repeat(pe, 1, turns, body)

            def plain_groups(g, n, op, per):
                for gi in range(2):
                    b0 = banks_of(g + gi)
                    for c in range(per):
                        w_chunk(n + (gi * per + c), op, 2 * c, c == 0, c == per - 1, b0).then_inc(chunk_used, 1)

            def att_wait(done):
                return lambda c: pe.wait_ge(outputs_lo, done) if c == EARLY else None

            def op_wait(base):
                return lambda c: pe.wait_ge(operand_lo, base + c // 2 + 1) if c % 2 == 0 else None

            attention(0, UNITS_A, scores_a, values_a, attention_banks(PH["a_out"]), PH["a_kv"],
                      early_chunk(PH["a_out"], 1, 0))
            groups(PH["a_out"], op_att, KT, att_wait(UNITS_A), start=EARLY)
            groups(PH["f0_in"], op_in, KT, op_wait(OP0["a_out"]), norm=3)
            groups(PH["f0_out"], op_ffn, FT, op_wait(OP0["f0_in"]))

            ph = PH["b_in"]
            b0 = banks_of(Lin(ph.g0))
            for c in range(8):
                n = Lin(ph.c0 + c)
                op_wait(OP0["f0_out"])(c)
                w_chunk(n, op_in, 2 * c, c == 0, c == 7, b0, tiles=(0, 1))
                token_chunk(n, op_in, 2 * c, c == 0, c == 7, b0 + 2,
                            lambda w, k: w[:, k * COLS + T:(k + 1) * COLS]).then_inc(chunk_used, 1)
                if c == 4:
                    pe.wait_ge(banks_free, ph.g0)
                    sum_squares(4, sqa, 4 - b0, True)
            pe.wait_ge(norm_root_taken, 5)
            repeat(pe, 0, 2, lambda i: plain_groups(Lin(ph.g0 + 1, 2, i), Lin(ph.c0 + 8, 16, i), op_in, 8))

            def scores_b(u, bank):
                p = u.mod(2)
                if u.i is None and u.c < 2:
                    pe.wait_ge(k_both_ready, u.c + 1)
                pe.wait_ge(q_placed, (u + 1).v)
                for hh in range(2):
                    r = slice(64 * hh, 64 * hh + 64)
                    for q0, keys, o in ((0, P, 0), (P, T, P)):
                        z = mm(ps[:, bank + hh, o:o + keys], st_qb[r, p, q0:q0 + P], st_k[r, p, 0:keys],
                               start=True, stop=True)
                return z

            def values_b(u, bank):
                p = u.mod(2)
                for hh in range(2):
                    r = slice(64 * hh, 64 * hh + 64)
                    mm(ps[r, bank, 0:T], st_vb[:, p, 0, :], probs_t[p][:, hh, 0:T], start=True, stop=False)
                    z = mm(ps[r, bank, P:T], st_vb[:, p, 1, :], probs_t[p][:, hh, T:384], start=False, stop=True)
                return z

            attention(UNITS_A, UNITS_B, scores_b, values_b, attention_banks(PH["b_out"]), ph,
                      early_chunk(PH["b_out"], 2, UNITS_A))
            groups(PH["b_out"], op_att, KT, att_wait(UNITS_A + UNITS_B), start=EARLY)
            groups(PH["f1_in"], op_in, KT, op_wait(OP0["b_out"]), norm=5)
            groups(PH["f1_out"], op_ffn, FT, op_wait(OP0["f1_in"]))

            def transposes(q, src, bank):
                pe.wait_ge(y_scaled, q + 1)
                for half in range(2):
                    if q == 3 and half == 1:
                        pe.wait_ge(norm_root_taken, 7)
                    for j in range(4):
                        z = nc.tensor.transpose(ps[:, bank + half, j * P:(j + 1) * P],
                                                src(j)[:, half * P:(half + 1) * P], ident[:, :])
                    z.then_inc(y_transposed, 1)
            yb = OUT_BANKS
            pe.wait_ge(banks_free, PH["f1_out"].g1 - 1)
            transposes(0, lambda j: h[:, j, :], yb[0])
            transposes(1, lambda j: h[:, 4 + j, :], yb[1])
            pe.wait_ge(banks_free, PH["f1_out"].g1)
            transposes(2, lambda j: h[:, 8 + j, :], yb[2])
            pe.wait_ge(squares_added, NORM_SQ[6])
            pe.wait_ge(last_squares, 1)
            for half in range(2):
                tokens = slice(half * P, (half + 1) * P)
                o = ps[:, yb[3] + 1, half:half + 1]
                mm(o, sqa[:, tokens], ones[:, 0:1], start=True, stop=False)
                for j in range(4):
                    z = mm(o, cg[:, j, tokens], ones[:, 0:1], start=False, stop=j == 3)
            z.then_inc(norm_sum, 1)
            transposes(3, lambda j: cv[:, j, :], yb[3])

        @block.scalar
        def _(act):
            f = nc.scalar.activation

            def split(n, cols=CH):
                if n.i is None and n.c >= CHUNKS:
                    return
                s = n.mod(SLOTS)
                act.wait_ge(raw_full[s], (n.over(SLOTS).times(16) + 16).v)
                if n.i is not None or n.c >= SLOTS:
                    act.wait_ge(chunk_used, (n - (SLOTS - 1)).v)
                f(w_hi[s][:, 0:cols], raw[s][:, 0:cols], ACT.Copy).then_inc(hi_ready, 1)

            def b_half(g, last_chunk, tiles=4, bias=None):
                act.wait_ge(chunk_used, (last_chunk + 1).v)
                if g.i is not None or g.c >= 1:
                    act.wait_ge(banks_free, g.v)
                b0 = 4 * g.mod(2)
                if bias is None:
                    f(half_b[:, 0:tiles, :], ps[:, b0:b0 + tiles, T:2 * T], ACT.Copy).then_inc(b_copied, 1)
                    return
                for j in range(tiles):
                    z = f(half_b[:, j, :], ps[:, b0 + j, T:2 * T], ACT.Identity, bias=bias(j))
                z.then_inc(b_copied, 1)

            def op_high(k, dst):
                act.wait_ge(operand_in_cv, (k + 1).v)
                f(dst, cv[:, :, :], ACT.Copy).then_inc(operand_hi, 1)

            def norm_root(norm, dst, bank, width, scale=1.0, cols=None):
                act.wait_ge(norm_sum, norm + 1)
                act.wait_ge(const_set, 1)
                z = f(dst, ps[:, bank, 0:T], ACT.Sqrt, bias=eps[:, 1:2] if scale != 1.0 else eps[:, 0:1],
                      scale=1.0 / width / scale ** 2)
                if cols is not None:
                    z = f(rs_col[:, cols:cols + 2], ps[:, bank, T:T + 2], ACT.Sqrt, bias=eps[:, 0:1], scale=1.0 / width)
                z.then_inc(norm_root_taken, 1)

            act.wait_ge(par_transposed, 1)
            f(par[:, 0:PC_END0], ps[:, 0, 0:PC_END0], ACT.Copy).then_inc(par_ready, 1)
            for q in range(4):
                for j in range(2):
                    act.wait_ge(x_transposed, 2 * q + j + 1)
                    f(h[:, 4 * q + 2 * j:4 * q + 2 * j + 2, :],
                      ps[:, 4 + 2 * (q % 2) + j, :].rearrange("p (m t) -> p m t", m=2), ACT.Copy).then_inc(h_in, 1)
                split(Lin(q))
                op_high(Lin(OP0["x"] + q), op_in[:, 4 * q:4 * q + 4, 0, :])
            for c in range(SLOTS, AHEAD):
                split(Lin(c))

            ph = PH["a_in"]
            for c in range(AHEAD, ph.n + AHEAD_2):
                split(Lin(c), CH if c < ph.n else 2 * QCOLS)
                if c == 9:
                    act.wait_ge(par_transposed, 2)
                    f(par[:, P:5 * P], ps[:, 5, :], ACT.Copy)
                    f(par[:, 5 * P:PC_END], ps[:, 6, 0:PC_END - 5 * P], ACT.Copy).then_inc(par_ready, 1)
                if c == 10:
                    norm_root(0, inv_rms[:, :], 4, D)
                if c == AHEAD + 1:
                    act.wait_ge(angle_ready, 1)
                    f(sin[:, :], sin[:, :], ACT.Sin)
                    f(cos[:, :], cos[:, :], ACT.Sin).then_inc(trig_ready, 1)
                if c == 11:
                    b_half(Lin(0), Lin(7))
                if c == 15:
                    norm_root(1, rsq[:, :], 2, RANK, scale=(NOPE + ROPE) ** -0.5)
                    op_high(Lin(OP0["lat"]), op_lat[:, 0:4, 0, :])
                if c == 19:
                    b_half(Lin(1), Lin(15))
                if c == 21:
                    b_half(Lin(2), Lin(17), tiles=1)
                    act.wait_ge(bias_row_product, 1)
                    f(brow[:, :], ps[0:HEADS_B, 6, 0:384], ACT.Copy).then_inc(brow_ready, 1)

            ph = PH["a_q"]

            def q_group(k, cols):
                act.wait_ge(chunk_used, (k.times(2) + (ph.c0 + 2)).v)
                act.wait_ge(banks_free, (k + ph.g0).v)
                b0 = 3 * (k + 1).mod(2)
                f(half_b[:, 0:3, :], ps[:, b0:b0 + 3, T:2 * T], ACT.Copy).then_inc(b_copied, 1)
                for c in range(2):
                    split(k.times(2) + (ph.c0 + AHEAD_2 + c), cols)
                    if c == 0 and k.i is None and k.c == 1:
                        op_high(Lin(OP0["lat"] + 1), op_lat[:, 4:8, 0, :])
            q_group(Lin(0), 2 * QCOLS)
            norm_root(2, rsk[:, :], 7, RANK)
            q_group(Lin(1), 2 * QCOLS)
            repeat(act, 1, 3, lambda i: [q_group(Lin(k, 2, i), (2 * QCOLS, CH)[k]) for k in range(2)])
            q_group(Lin(6), CH)
            q_group(Lin(7), CH)

            ph = PH["a_kv"]

            def kv_group(k, splits=True):
                g = k + ph.g0
                b0 = 4 * g.mod(2)
                act.wait_ge(chunk_used, (k.times(2) + (ph.c0 + 2)).v)
                f(v_mla[:, :, sl(k.times(T), T)], ps[:, b0 + 2:b0 + 4, 0:T], ACT.Copy).then_inc(v_ready, 1)
                b_half(g, k.times(2) + (ph.c0 + 1), tiles=2)
                if splits:
                    for c in range(2):
                        split(k.times(2) + (ph.c0 + AHEAD_2 + c))
            repeat(act, 0, 3, lambda i: [kv_group(Lin(k, 2, i)) for k in range(2)])
            kv_group(Lin(6))
            kv_group(Lin(7), False)

            def attention(u0, units, banks, sinks, out_high, place_q=None):
                def exps(u):
                    p = u.mod(2)
                    act.wait_ge(maxima_done, (u + u0 + 1).v)
                    for hh in range(2):
                        for q, cols in ((0, slice(0, P)), (1, slice(P, 384))):
                            k = 2 * hh + q
                            z = f(scores_sb[:, p, hh, cols], scores_sb[:, p, hh, cols], ACT.Exp,
                                  bias=neg_max[:, p, k:k + 1], accum_out=exp_sums[:, p, k:k + 1])
                    if sinks:
                        for hh in range(2):
                            z = f(sink_exps[:, p, 2 * hh:2 * hh + 2], neg_max[:, p, 2 * hh:2 * hh + 2], ACT.Exp,
                                  bias=sinkc[:, sl(u.times(2) + hh, 1)])
                    z.then_inc(exps_done, 1)

                def pt_copy(u):
                    act.wait_ge(probs_transposed, (u + u0 + 1).v)
                    if u.i is not None or u.c >= 2:
                        act.wait_ge(outputs_done, (u + u0 - 1).v)
                    f(probs_t[u.mod(2)][:, :, :], ps[:, banks[1]:banks[1] + 2, 0:384],
                      ACT.Copy).then_inc(probs_t_copied, 1)

                def o_high(u):
                    act.wait_ge(outputs_done, (u + u0 + 1).v)
                    out_high(u).then_inc(outputs_hi, 1)

                def step(u, ahead=True):
                    if u.i is not None or u.c >= 2:
                        o_high(u - 2)
                    if ahead:
                        exps(u + 1)
                    if place_q and (u.i is not None or u.c < units - 3):
                        place_q(u + 3)
                    pt_copy(u)
                exps(Lin(0))
                if place_q:
                    place_q(Lin(2))
                step(Lin(0))
                step(Lin(1))
                repeat(act, 1, units // 2 - 2, lambda i: [step(Lin(k, 2, i)) for k in range(2)])
                for k in range(4, 1, -1):
                    step(Lin(units - k))
                step(Lin(units - 1), ahead=False)
                o_high(Lin(units - 2))
                o_high(Lin(units - 1))

            banks = attention_banks(PH["a_out"])
            attention(0, UNITS_A, banks, False,
                      lambda u, o=banks[2]: f(op_att[:, sl(u.times(2), 2), 0, :],
                                  ps[:, o + u.mod(2), :].rearrange("p (m t) -> p m t", m=2), ACT.Copy))
            for c in range(SLOTS, AHEAD):
                split(Lin(PH["a_out"].c0 + c))

            def residual(ph, kts, k0, bias=None):
                per = kts // 2

                def body(i, t=0):
                    for j in range(2 * per):
                        split(Lin(ph.c0 + AHEAD + j + 2 * per * t, 2 * per, i))
                        gi, at = divmod(j, per)
                        if at == per - 5:
                            b_half(Lin(ph.g0 + gi + 2 * t, 2, i), Lin(ph.c0 + (gi + 1) * per - 1 + 2 * per * t, 2 * per, i),
                                   bias=bias and (lambda m: par[:, sl(Lin(bias + 4 * gi + m, 8, i), 1)]))
                        if at == per - 3 and k0 is not None:
                            op_high(Lin(k0 + gi, 2, i), op_in[:, sl(Lin(4 * gi, 8, i), 4), 0, :])
                if k0 is not None:
                    repeat(act, 0, 2, body)
                else:
                    body(None, 0)
                    body(None, 1)

            def ffn_in(ph, layer, k0):
                def body(i):
                    for j in range(16):
                        split(Lin(ph.c0 + AHEAD + j, 16, i))
                        if j in (3, 11):
                            gi = j // 8
                            b_half(Lin(ph.g0 + gi, 2, i), Lin(ph.c0 + 8 * gi + 7, 16, i))
                        if j == 8:
                            act.wait_ge(conv_ready, Lin(FFN_TURNS * layer + 1, 1, i).v)
                            f(cg[:, :, :], cg[:, :, :], ACT.Silu).then_inc(silu_ready, 1)
                        if j == 14:
                            op_high(Lin(k0, 1, i), op_ffn[:, sl(Lin(0, 4, i), 4), 0, :])
                repeat(act, 0, FFN_TURNS, body)

            act.wait_ge(bias_out, 16)
            residual(PH["a_out"], KT, OP0["a_out"])
            norm_root(3, inv_rms[:, :], 4 - 4 * (PH["f0_in"].g0 % 2), D)
            ffn_in(PH["f0_in"], 0, OP0["f0_in"])
            residual(PH["f0_out"], FT, OP0["f0_out"])
            norm_root(4, inv_rms[:, :], 4 - 4 * (PH["b_in"].g0 % 2), D, cols=2)

            ph = PH["b_in"]

            for j in range(SLOTS):
                split(Lin(ph.c0 + AHEAD + j))
            b_half(Lin(ph.g0), Lin(ph.c0 + 7), tiles=2)

            def b_body(i):
                for j in range(16):
                    split(Lin(ph.c0 + AHEAD + SLOTS + j, 16, i))
                    if j in (7, 15):
                        b_half(Lin(ph.g0 + (j + 1) // 8, 2, i), Lin(ph.c0 + 8 + j, 16, i))
            repeat(act, 0, 2, b_body)
            banks = attention_banks(PH["b_out"])

            def place_q(u):
                if u.i is not None or u.c >= 2:
                    act.wait_ge(scores_done, (u + UNITS_A - 1).v)
                if u.i is None and u.c == 0:
                    act.wait_ge(banks_free, ph.g1 - 1)
                f(st_qb[:, u.mod(2), :], q_win[:, sl(u, 1), :], ACT.Copy).then_inc(q_placed, 1)

            def both_halves(dst, kv):
                for d in range(2):
                    z = f(dst[64 * d:64 * d + 64, :], cv[64 * (kv % 2):64 * (kv % 2) + 64, kv // 2, :], ACT.Copy)
                z.then_inc(k_both_ready, 1)
            act.wait_ge(k_ready, 1)
            for p in range(2):
                both_halves(st_k[:, p, :], 0)
                place_q(Lin(p))
            for kv in range(1, KV_B):
                both_halves(k_both[:, kv, :], kv)
            attention(UNITS_A, UNITS_B, banks, True,
                      lambda u, o=banks[2]: f(op_att[:, sl(u, 1), 0, :], ps[:, o + u.mod(2), 0:T], ACT.Copy), place_q)
            for c in range(SLOTS, AHEAD):
                split(Lin(PH["b_out"].c0 + c))
            residual(PH["b_out"], KT, OP0["b_out"], bias=PC_BO)
            norm_root(5, inv_rms[:, :], 4 - 4 * (PH["f1_in"].g0 % 2), D)
            ffn_in(PH["f1_in"], 1, OP0["f1_in"])
            residual(PH["f1_out"], FT, None)

            act.wait_ge(banks_free, PH["f1_out"].g1)
            f(cg[:, :, :], h[:, KT - 4:KT, :], ACT.Square).then_inc(last_squares, 1)
            act.wait_ge(norm_sum, 7)
            f(rs_col[:, 4:6], ps[:, OUT_BANKS[3] + 1, 0:2], ACT.Sqrt, bias=eps[:, 0:1],
              scale=1.0 / D).then_inc(norm_root_taken, 1)
            act.wait_ge(sqrt_done, 1)
            for half in range(2):
                for q in (0, 2):
                    act.wait_ge(y_transposed, 2 * q + half + 1)
                    f(yt[:, half, q * 512:(q + 1) * 512], ps[:, OUT_BANKS[q] + half, :], ACT.Copy,
                      scale=rs_col[:, 4 + half:5 + half]).then_inc(y_act, 1)

        @block.vector
        def _(dve):
            v = nc.vector
            done = Steps(dve, dve_done)

            def split(n, cols=CH):
                if n.i is None and n.c >= CHUNKS:
                    return
                s = n.mod(SLOTS)
                dve.wait_ge(hi_ready, (n + 1).v)
                v.tensor_tensor(w_lo[s][:, 0:cols], raw[s][:, 0:cols], w_hi[s][:, 0:cols].bitcast(F32),
                                ALU.subtract).then_inc(lo_ready, 1)

            def spread(a, tiles):
                return bass.AP(a.tensor, a.offset, [list(a.ap[0]), [0, tiles], [1, T]])

            def col(n):
                return par[:, sl(n, 1)]

            def gains(k, src, gain, tiles=4):
                if k.i is not None or k.c >= 1:
                    dve.wait_ge(operand_lo, k.v)
                for j in range(tiles):
                    z = v.tensor_scalar(cv[:, j, :], src(j), col(gain + j), None, ALU.mult)
                z.then_inc(operand_in_cv, 1)

            def op_low(k, dst, hi):
                dve.wait_ge(operand_hi, (k + 1).v)
                v.tensor_tensor(dst, cv[:, :, :], hi.bitcast(F32), ALU.subtract).then_inc(operand_lo, 1)

            def operand(k, op, tile0):
                op_low(k, op[:, sl(tile0, 4), 1, :], op[:, sl(tile0, 4), 0, :])

            dve.wait_ge(par_ready, 1)
            for q in range(4):
                dve.wait_ge(h_in, 2 * q + 2)
                gains(Lin(q), lambda j: h[:, 4 * q + j, :], Lin(PC_MIX + 4 * q))
                split(Lin(q))
                operand(Lin(q), op_in, Lin(4 * q))
            for c in range(SLOTS, AHEAD):
                split(Lin(c))

            def inverse(norm, dst):
                dve.wait_ge(norm_root_taken, norm + 1)
                for d in dst:
                    done(v.reciprocal(d, d))
                done.sync()
            def angles():
                dve.wait_ge(rope_in, 5 * 16)
                done(v.tensor_copy(turn[:, :], posi[:, :]))
                done.sync()
                done(v.tensor_scalar(ang[:, :], turn[:, :], invf[:, 0:1], None, ALU.mult))
                done.sync()
                magic = 1.5 * 2.0 ** 23
                done(v.tensor_scalar(turn[:, :], ang[:, :], 1.0 / (2 * math.pi), magic, ALU.mult, ALU.add))
                done.sync()
                done(v.tensor_scalar(turn[:, :], turn[:, :], magic, None, ALU.subtract))
                done.sync()
                c1 = 6.28125
                c2 = float(np.float32(np.round((2 * math.pi - c1) * 2 ** 20) / 2 ** 20))
                c3 = 2 * math.pi - c1 - c2
                for c in (c1, c2, c3):
                    done(v.scalar_tensor_tensor(ang[:, :], turn[:, :], -c, ang[:, :], ALU.mult, ALU.add))
                    done.sync()
                lim = 3.1415925
                done(v.tensor_scalar(sin[:, :], ang[:, :], lim, -lim, ALU.min, ALU.max))
                done(v.tensor_scalar(cos[:, :], ang[:, :], math.pi / 2, None, ALU.add))
                done.sync()
                done(v.tensor_scalar(turn[:, :], cos[:, :], math.pi, -2 * math.pi, ALU.is_gt, ALU.mult))
                done.sync()
                done(v.tensor_tensor(cos[:, :], cos[:, :], turn[:, :], ALU.add))
                done.sync()
                v.tensor_scalar(cos[:, :], cos[:, :], lim, -lim, ALU.min, ALU.max).then_inc(angle_ready, 1)

            def sum_banks(g, tiles, dst, src=None):
                dve.wait_ge(b_copied, (g + 1).v)
                b0 = 4 * g.mod(2)
                return v.tensor_tensor(dst, ps[:, b0:b0 + tiles, 0:T], half_b[:, 0:tiles, :], ALU.add)

            def over_rms(g, tiles, dst, r):
                sum_banks(g, tiles, dst).then_inc(banks_free, 1)
                dve.wait_ge(banks_free, (g + 1).v)
                return v.tensor_tensor(dst, dst, spread(r[:, :], tiles), ALU.mult)

            def scaled(g, tiles, dst, r):
                done(over_rms(g, tiles, dst, r))
                done.sync()

            def latent(g, r, gain):
                dve.wait_ge(operand_lo, OP0["lat"] + g)
                for j in range(4):
                    z = v.scalar_tensor_tensor(cv[:, j, :], cg[:, j, :], col(Lin(gain + j)), r[:, :], ALU.mult, ALU.mult)
                z.then_inc(operand_in_cv, 1)

            ph = PH["a_in"]
            for c in range(AHEAD, ph.n + AHEAD_2):
                split(Lin(c), CH if c < ph.n else 2 * QCOLS)
                if c == AHEAD:
                    angles()
                if c == 10:
                    inverse(0, [inv_rms[:, :]])
                if c == 11:
                    over_rms(Lin(0), 4, cg[:, :, :], inv_rms).then_inc(lat_ready, 1)
                    dve.wait_ge(lat_ready, 1)
                if c == 15:
                    inverse(1, [rsq[:, :]])
                    latent(0, rsq, PC_GQ)
                    operand(Lin(OP0["lat"]), op_lat, Lin(0))
                if c == 19:
                    dve.wait_ge(operand_in_cv, OP0["lat"] + 1)
                    over_rms(Lin(1), 4, cg[:, :, :], inv_rms).then_inc(lat_ready, 1)
                    dve.wait_ge(lat_ready, 2)
                if c == 21:
                    sum_banks(Lin(2), 1, xk[:, :]).then_inc(banks_free, 1)
                    dve.wait_ge(banks_free, 3)
                    v.tensor_tensor(xk[:, :], xk[:, :], inv_rms[:, :], ALU.mult).then_inc(k_rope_ready, 1)
            dve.wait_ge(k_rope_ready, 1)
            dve.wait_ge(trig_ready, 1)

            ph = PH["a_q"]

            def rope_finish(r, bank, x, dst):
                done(v.tensor_tensor(xt[:, 0, :], x, cos[:, :], ALU.mult))
                dve.wait_ge(rope_rotated, (r + 1).v)
                v.tensor_tensor(xt[:, 1, :], ps[:, bank, 0:T], sin[:, :], ALU.mult).then_inc(rope_read, 1)
                done.sync()
                dve.wait_ge(rope_read, (r + 1).v)
                v.tensor_tensor(dst, xt[:, 0, :], xt[:, 1, :], ALU.add).then_inc(q_rope_ready, 1)
                dve.wait_ge(q_rope_ready, (r + 1).v)

            def q_group(k, cols, last=False):
                dve.wait_ge(b_copied, (k + (ph.g0 + 1)).v)
                b0 = 3 * (k + 1).mod(2)
                v.tensor_tensor(q_nope[:, sl(k.times(2), 2), :], ps[:, b0:b0 + 2, 0:T], half_b[:, 0:2, :],
                                ALU.add).then_inc(q_ready, 1)
                v.tensor_tensor(xr[:, k.mod(2), :], ps[:, b0 + 2, 0:T], half_b[:, 2, :],
                                ALU.add).then_inc(banks_free, 1)
                dve.wait_ge(banks_free, (k + (ph.g0 + 1)).v)
                if k.i is None and k.c == 0:
                    rope_finish(k, 6, xk[:, :], k_rope[:, :])
                else:
                    rope_finish(k, 3 if last else 6, xr[:, (k + 1).mod(2), :], q_rope[:, sl(k - 1, 1), :])
                if k.i is None and k.c == 1:
                    latent(1, rsk, PC_GKV)
                for c in range(2):
                    if k.i is None and k.c == 1 and c == 1:
                        operand(Lin(OP0["lat"] + 1), op_lat, Lin(4))
                    if last and c == 1:
                        rope_finish(Lin(8), 3, xr[:, 1, :], q_rope[:, UNITS_A - 1:UNITS_A, :])
                    split(k.times(2) + (ph.c0 + AHEAD_2 + c), cols)
            q_group(Lin(0), 2 * QCOLS)
            inverse(2, [rsk[:, :]])
            q_group(Lin(1), 2 * QCOLS)
            done.loop(1, 3, 2, lambda i: [q_group(Lin(k, 2, i), (2 * QCOLS, CH)[k]) for k in range(2)])
            q_group(Lin(6), CH)
            q_group(Lin(7), CH, last=True)

            ph = PH["a_kv"]

            def kv_group(k, splits=True):
                g = k + ph.g0
                sum_banks(g, 2, k_nope[:, sl(k.times(2), 2), :]).then_inc(banks_free, 1)
                if splits:
                    for c in range(2):
                        split(k.times(2) + (ph.c0 + AHEAD_2 + c))
            repeat(dve, 0, 3, lambda i: [kv_group(Lin(k, 2, i)) for k in range(2)])
            kv_group(Lin(6))
            kv_group(Lin(7), False)

            def attention(u0, units, banks, loop_steps, masked, sinks, out_low):
                def maxes(u):
                    p, bank = u.mod(2), banks[0] + 2 * u.mod(2)
                    dve.wait_ge(scores_done, (u + u0 + 1).v)
                    if u.i is not None or u.c >= 2:
                        dve.wait_ge(probs_ready, (u + u0 - 1).v)
                    if sinks:
                        dve.wait_ge(bias_staged, (u + 1).v)
                    v.memset(fence[:, p:p + 1], 0.0)
                    for hh in range(2):
                        for q, cols in ((0, slice(0, P)), (1, slice(P, 384))):
                            k = 2 * hh + q
                            done(v.tensor_tensor_reduce(out=scores_sb[:, p, hh, cols], in0=ps[:, bank + hh, cols],
                                                        in1=masked(p, hh, q), scale=1.0, scalar=-3.0e38,
                                                        op0=ALU.add, op1=ALU.max, accum_out=ri[:, p, k:k + 1]))
                    done.sync()
                    if sinks:
                        a = nsink[:, sl(u.times(2), 2)]
                        z = v.scalar_tensor_tensor(neg_max[:, p, :].rearrange("p (h q) -> p h q", h=2),
                                                   ri[:, p, :].rearrange("p (h q) -> p h q", h=2), -1.0,
                                                   bass.AP(a.tensor, a.offset, list(a.ap) + [[0, 2]]),
                                                   ALU.mult, ALU.min)
                    else:
                        z = v.tensor_scalar(neg_max[:, p, :], ri[:, p, :], -1.0, None, ALU.mult)
                    z.then_inc(maxima_done, 1)

                def normal(u):
                    p = u.mod(2)
                    dve.wait_ge(exps_done, (u + u0 + 1).v)
                    if sinks:
                        done(v.tensor_tensor(exp_sums[:, p, :], exp_sums[:, p, :], sink_exps[:, p, :], ALU.add))
                        done.sync()
                    done(v.reciprocal(ri[:, p, :], exp_sums[:, p, :]))
                    done.sync()
                    if u.i is not None or u.c >= 2:
                        dve.wait_ge(probs_transposed, (u + u0 - 1).v)
                    for hh in range(2):
                        for q, cols in ((0, slice(0, P)), (1, slice(P, 384))):
                            k = 2 * hh + q
                            z = v.tensor_scalar(probs[p][:, hh, cols], scores_sb[:, p, hh, cols], ri[:, p, k:k + 1],
                                                None, ALU.mult)
                    z.then_inc(probs_ready, 1)

                def low(u):
                    dve.wait_ge(outputs_hi, (u + u0 + 1).v)
                    out_low(u).then_inc(outputs_lo, 1)

                def step(u, ahead=True):
                    if ahead:
                        maxes(u + 1)
                    normal(u)
                    if u.i is not None or u.c >= 2:
                        low(u - 2)
                maxes(Lin(0))
                step(Lin(0))
                step(Lin(1))
                done.loop(1, units // 2 - 1, loop_steps, lambda i: [step(Lin(k, 2, i)) for k in range(2)])
                step(Lin(units - 2))
                step(Lin(units - 1), ahead=False)
                low(Lin(units - 2))
                low(Lin(units - 1))

            dve.wait_ge(mask_in, 16)
            banks = attention_banks(PH["a_out"])
            attention(0, UNITS_A, banks, 10, lambda p, hh, q: mask[:, 0:P] if q == 0 else mask[:, P:384], False,
                      lambda u, o=banks[2]: v.tensor_tensor(op_att[:, sl(u.times(2), 2), 1, :],
                                                ps[:, o + u.mod(2), :].rearrange("p (m t) -> p m t", m=2),
                                                op_att[:, sl(u.times(2), 2), 0, :].bitcast(F32), ALU.subtract))
            for c in range(SLOTS, AHEAD):
                split(Lin(PH["a_out"].c0 + c))

            def add_residual(g, tile0):
                dve.wait_ge(b_copied, (g + 1).v)
                b0 = 4 * g.mod(2)
                hh = h[:, sl(tile0, 4), :]
                done(v.tensor_tensor(hh, hh, ps[:, b0:b0 + 4, 0:T], ALU.add))
                done.sync()
                v.tensor_tensor(hh, hh, half_b[:, :, :], ALU.add).then_inc(banks_free, 1)
                dve.wait_ge(banks_free, (g + 1).v)

            def residual(ph, kts, k0, gain, static=False):
                per = kts // 2
                turns = ph.n // (2 * per)

                def body(i, t=0):
                    for j in range(2 * per):
                        split(Lin(ph.c0 + AHEAD + j + 2 * per * t, 2 * per, i))
                        gi, at = divmod(j, per)
                        tile0 = Lin(4 * gi + 8 * t, 8, i)
                        if static and t == turns - 1 and gi == 1 and 6 <= at < 9:
                            if at == 6:
                                dve.wait_ge(squares_added, NORM_SQ[6])
                            for m in range(4 * (at - 6), 4 * (at - 5)):
                                z = v.tensor_scalar(h[:, m, :], h[:, m, :], col(Lin(PC_FIN + m)), None, ALU.mult)
                            z.then_inc(y_scaled, 1)
                        if at == per - 5:
                            add_residual(Lin(ph.g0 + gi + 2 * t, 2, i), tile0)
                        if at == per - 4 and k0 is not None:
                            gains(Lin(k0 + gi, 2, i), lambda m: h[:, sl(tile0 + m, 1), :], Lin(gain + 4 * gi, 8, i))
                        if at == per - 2 and k0 is not None:
                            operand(Lin(k0 + gi, 2, i), op_in, tile0)
                if static:
                    for t in range(turns):
                        body(None, t)
                else:
                    done.loop(0, turns, 2, body)

            def conv(layer, dst, tile0):
                w = PC_CONVW + layer * 3 * CT
                for m in range(4):
                    done(v.tensor_scalar(dst[:, m, :], up[:, m, 2:T + 2], col(tile0 + (w + 2 * CT + m)),
                                         col(tile0 + (PC_CONVB + layer * CT + m)), ALU.mult, ALU.add))
                done.sync()
                for tap in (1, 0):
                    for m in range(4):
                        z = v.scalar_tensor_tensor(dst[:, m, :], up[:, m, tap:T + tap], col(tile0 + (w + tap * CT + m)),
                                                   dst[:, m, :], ALU.mult, ALU.add)
                        if tap:
                            done(z)
                    if tap:
                        done.sync()
                return z

            def ffn_in(ph, layer, k0):
                def body(i):
                    for j in range(16):
                        split(Lin(ph.c0 + AHEAD + j, 16, i))
                        gi = j // 8
                        if j in (3, 11):
                            g = Lin(ph.g0 + gi, 2, i)
                            if gi == 1:
                                dve.wait_ge(conv_ready, Lin(FFN_TURNS * layer + 1, 1, i).v)
                            scaled(g, 4, up[:, :, 2:T + 2], inv_rms)
                        if j == 5:
                            conv(layer, cg, Lin(0, 4, i)).then_inc(conv_ready, 1)
                        if j == 12:
                            done(conv(layer, cv, Lin(FT, 4, i)))
                            done.sync()
                        if j == 13:
                            dve.wait_ge(silu_ready, Lin(FFN_TURNS * layer + 1, 1, i).v)
                            v.tensor_tensor(cv[:, :, :], cv[:, :, :], cg[:, :, :], ALU.mult).then_inc(operand_in_cv, 1)
                        if j == 15:
                            operand(Lin(k0, 1, i), op_ffn, Lin(0, 4, i))
                            dve.wait_ge(operand_lo, Lin(k0 + 1, 1, i).v)
                done.loop(0, FFN_TURNS, 19, body)

            dve.wait_ge(bias_out, 16)
            residual(PH["a_out"], KT, OP0["a_out"], PC_FFN)
            inverse(3, [inv_rms[:, :]])
            dve.wait_ge(operand_lo, OP0["a_out"] + 4)
            dve.wait_ge(const_set, 2)
            dve.wait_ge(par_ready, 2)
            ffn_in(PH["f0_in"], 0, OP0["f0_in"])
            residual(PH["f0_out"], FT, OP0["f0_out"], PC_MIX + KT)
            inverse(4, [inv_rms[:, :], rs_col[:, 2:4]])

            ph = PH["b_in"]

            dve.wait_ge(operand_lo, OP0["f0_out"] + 4)
            for j in range(SLOTS):
                split(Lin(ph.c0 + AHEAD + j))
            scaled(Lin(ph.g0), 2, cg[:, 0:2, :], inv_rms)
            for m in range(2):
                z = v.tensor_scalar(cv[:, m, :], cg[:, m, :], col(Lin(PC_BQKV + KT + m)), None, ALU.add)
            z.then_inc(k_ready, 1)
            b0 = 4 * (ph.g0 % 2)
            dve.wait_ge(sinks_in, 32)
            v.tensor_scalar(nsink[:, :], sinkc[:, :], -1.0, None, ALU.mult).then_inc(nsink_ready, 1)
            dve.wait_ge(nsink_ready, 1)
            for half in range(2):
                v.scalar_tensor_tensor(v_win[:, half, :], ps[:, b0 + 2 + half, 0:T], rs_col[:, 2 + half:3 + half],
                                       bvrow, ALU.mult, ALU.add).then_inc(v_win_ready, 1)

            def b_body(i):
                for j in range(16):
                    split(Lin(ph.c0 + AHEAD + SLOTS + j, 16, i))
                    if j in (7, 15):
                        gi = j // 8
                        scaled(Lin(ph.g0 + 1 + gi, 2, i), 4, cg[:, :, :], inv_rms)
                        for m in range(4):
                            done(v.tensor_scalar(q_win[:, sl(Lin(4 * gi + m, 8, i), 1), :], cg[:, m, :],
                                                 col(Lin(PC_BQKV + 4 * gi + m, 8, i)), DH ** -0.5, ALU.add, ALU.mult))
                        done.sync()
            done.loop(0, 2, 10, b_body)
            banks = attention_banks(PH["b_out"])
            attention(UNITS_A, UNITS_B, banks, 12,
                      lambda p, hh, q: st_b[:, p, hh, P:T] if q == 0 else st_b[:, p, hh, :],
                      True,
                      lambda u, o=banks[2]: v.tensor_tensor(op_att[:, sl(u, 1), 1, :], ps[:, o + u.mod(2), 0:T],
                                                op_att[:, sl(u, 1), 0, :].bitcast(F32), ALU.subtract))
            for c in range(SLOTS, AHEAD):
                split(Lin(PH["b_out"].c0 + c))
            residual(PH["b_out"], KT, OP0["b_out"], PC_FFN + KT)
            inverse(5, [inv_rms[:, :]])
            dve.wait_ge(operand_lo, OP0["b_out"] + 4)
            ffn_in(PH["f1_in"], 1, OP0["f1_in"])
            residual(PH["f1_out"], FT, None, None, static=True)

            for m in range(4):
                z = v.tensor_scalar(cv[:, m, :], h[:, KT - 4 + m, :], col(Lin(PC_FIN + KT - 4 + m)), None, ALU.mult)
            z.then_inc(y_scaled, 1)
            dve.wait_ge(norm_root_taken, 7)
            v.reciprocal(rs_col[:, 4:6], rs_col[:, 4:6]).then_inc(sqrt_done, 1)
            dve.wait_ge(sqrt_done, 1)
            for half in range(2):
                for q in (1, 3):
                    dve.wait_ge(y_transposed, 2 * q + half + 1)
                    v.tensor_scalar(yt[:, half, q * 512:(q + 1) * 512], ps[:, OUT_BANKS[q] + half, :],
                                    rs_col[:, 4 + half:5 + half], None, ALU.mult).then_inc(y_dve, 1)

        @block.gpsimd
        def _(pool):
            g_ = nc.gpsimd
            done = Steps(pool, pool_done)
            g_.memset(ones[:, :], 1.0)
            g_.memset(eps[:, 0:1], EPS)
            g_.memset(sqa[:, :], 0.0)
            g_.memset(eps[:, 1:2], EPS * (NOPE + ROPE)).then_inc(const_set, 1)

            def squares(src, tmp, acc, k):
                done(g_.tensor_tensor(tmp, src, src, ALU.mult))
                done.sync()
                for j in range(4):
                    z = g_.tensor_tensor(acc[:, :], acc[:, :], tmp[:, j, :], ALU.add)
                    if j < 3:
                        done(z)
                        done.sync()
                z.then_inc(squares_added, 1)

            pool.wait_ge(const_set, 1)
            for q in range(4):
                pool.wait_ge(h_in, 2 * q + 2)
                squares(h[:, 4 * q:4 * q + 4, :], up[:, :, 0:T], sqa, q)
                pool.wait_ge(squares_added, q + 1)
            pool.wait_ge(norm_sum, 1)
            done(g_.memset(sqa[:, :], 0.0))
            done(g_.memset(sqb[:, :], 0.0))
            done.sync()
            pool.wait_ge(rope_in, 5 * 16)
            g_.memset(relb[BUCKETS:BUCKETS + 1, :], 1.0).then_inc(brow_ready, 1)
            pool.wait_ge(brow_ready, 1)
            for g in range(2):
                pool.wait_ge(lat_ready, g + 1)
                squares(cg[:, :, :], up[:, :, 0:T], (sqa, sqb)[g], 4 + g)
                pool.wait_ge(squares_added, 5 + g)
            pool.wait_ge(norm_sum, 3)
            pool.wait_ge(chunk_used, PH["a_in"].c1)
            done(g_.memset(sqa[:, :], 0.0))
            pool.dma_start(mask[:, :], c_mask).then_inc(mask_in, 16)

            pool.wait_ge(q_ready, UNITS_A)
            pool.wait_ge(q_rope_ready, 1 + UNITS_A)

            def stage(u, u0, copies, read, staged, place):
                if u.i is not None or u.c >= 2:
                    pool.wait_ge(read, (u + u0 - 1).v)
                    g_.tensor_tensor(fence[:, place:place + 1], ones[:, 0:1], ones[:, 0:1], ALU.mult)
                copies(u, u.mod(2)).then_inc(staged, 1)

            def q_a(u):
                def copies(u, p):
                    g_.tensor_copy(st_q[:, p, :, :], q_nope[:, sl(u.times(2), 2), :])
                    return g_.tensor_copy(st_r[:, p, :], q_rope[:, sl(u, 1), :])
                stage(u, 0, copies, scores_done, queries_staged, 2 + u.mod(2))

            def v_a(u):
                def copies(u, p):
                    return g_.tensor_copy(st_v[:, p, :, :], v_mla[:, :, sl(u.times(T), T)])
                stage(u, 0, copies, outputs_done, values_staged, 4 + u.mod(2))

            def step_a(u):
                q_a(u + 2)
                v_a(u)
            q_a(Lin(0))
            q_a(Lin(1))
            pool.wait_ge(brow_ready, 2)
            pool.wait_ge(v_ready, PH["a_kv"].ng - 1)
            pool.dma_start(bias_dram, bass.AP(brow[:, :].tensor, brow[:, :].offset,
                                              [list(brow[:, :].ap[0]), [0, P], [1, 384]])).then_inc(bias_out, 16)
            pool.wait_ge(v_ready, PH["a_kv"].ng)
            v_a(Lin(0))
            q_a(Lin(2))
            step_a(Lin(1))
            repeat(pool, 1, UNITS_A // 2 - 1, lambda i: [step_a(Lin(k, 2, i)) for k in range(2)])
            v_a(Lin(UNITS_A - 2))
            v_a(Lin(UNITS_A - 1))

            def residual_squares(ph, sq0):
                def body(i):
                    for gi in range(2):
                        pool.wait_ge(banks_free, Lin(ph.g0 + gi + 1, 2, i).v)
                        squares(h[:, sl(Lin(4 * gi, 8, i), 4), :], cg[:, :, :], sqa, None)
                        pool.wait_ge(squares_added, Lin(sq0 + gi + 1, 2, i).v)
                done.loop(0, 2, 8, body)
            residual_squares(PH["a_out"], SQ0["a_out"])
            pool.wait_ge(norm_sum, 4)
            done(g_.memset(sqa[:, :], 0.0))
            g_.memset(up[:, :, 0:2], 0.0).then_inc(const_set, 1)
            done.sync()
            residual_squares(PH["f0_out"], SQ0["f0_out"])
            pool.wait_ge(norm_sum, 5)
            done(g_.memset(sqa[:, :], 0.0))
            done.sync()

            pool.wait_ge(chunk_used, PH["f0_out"].c1)
            pool.wait_ge(bias_out, 16)
            pool.dma_start(sinkc[:, :], bass.AP(swa_sinks.tensor, 0, [[0, P], [1, HEADS_B]])).then_inc(sinks_in, 16)
            pool.dma_start(bvrow, bass.AP(swa_b_v.tensor, 0, [[0, P], [1, T]])).then_inc(sinks_in, 16)

            for k in range(4):
                pool.wait_ge(chunk_used, PH["b_in"].c0 + 6 * k)
                heads = bass.AP(bias_dram.tensor, P - 1 + 8 * k * P * 384, [[383, P], [P * 384, 8], [1, T]])
                pool.dma_start(win_bias[:, 8 * k:8 * k + 8, :], heads).then_inc(win_bias_in, 16)
            pool.wait_ge(win_bias_in, 64)
            pool.wait_ge(v_win_ready, 2)
            pool.wait_ge(chunk_used, PH["b_in"].c1)

            def q_b(u, kv):
                def keys(u, p):
                    if kv is None:
                        return g_.tensor_tensor(fence[:, 10 + p:11 + p], ones[:, 0:1], ones[:, 0:1], ALU.mult)
                    pool.wait_ge(k_both_ready, KV_B + 1)
                    return g_.tensor_copy(st_k[:, p, :], k_both[:, sl(kv, 1), :])

                def biases(u, p):
                    return g_.tensor_copy(st_b[:, p, :, :], win_bias[:, sl(u.times(2), 2), :])
                stage(u, UNITS_A, keys, scores_done, queries_staged, 2 + u.mod(2))
                stage(u, UNITS_A, biases, maxima_done, bias_staged, 6 + u.mod(2))

            def v_b(u, kv):
                def copies(u, p):
                    if kv is None:
                        return g_.tensor_tensor(fence[:, 8 + p:9 + p], ones[:, 0:1], ones[:, 0:1], ALU.mult)
                    return g_.tensor_copy(st_vb[:, p, :, :], v_win[:, :, sl(kv.times(DH), DH)])
                stage(u, UNITS_A, copies, outputs_done, values_staged, 4 + u.mod(2))

            def turn_b(i, t=0, last=False):
                for k in range(4):
                    if not (last and k >= 2):
                        q_b(Lin(k + 2 + 4 * t, 4, i), Lin(t + 1, 1, i) if k >= 2 else None)
                    v_b(Lin(k + 4 * t, 4, i), Lin(t, 1, i) if k < 2 else None)
            for k in range(2):
                q_b(Lin(k), None)
            turn_b(None)
            repeat(pool, 1, KV_B - 1, turn_b)
            turn_b(None, KV_B - 1, last=True)
            residual_squares(PH["b_out"], SQ0["b_out"])
            pool.wait_ge(norm_sum, 6)
            done(g_.memset(sqa[:, :], 0.0))
            done.sync()
            for gi in range(3):
                pool.wait_ge(banks_free, PH["f1_out"].g0 + gi + 1)
                squares(h[:, 4 * gi:4 * gi + 4, :], cg[:, :, :], sqa, None)
                pool.wait_ge(squares_added, SQ0["f1_out"] + gi + 1)


def tables():
    ident = np.eye(P, dtype=np.float32)
    rot = np.zeros((P, P), np.float32)
    half = ROPE // 2
    for m in range(P):
        b, r = divmod(m, ROPE)
        if r < half:
            rot[b * ROPE + r + half, m] = -1.0
        else:
            rot[b * ROPE + r - half, m] = 1.0
    invf = (np.float32(THETA) ** (-np.arange(half, dtype=np.float32) / half)).astype(np.float32)
    invf = np.tile(invf, P // half).reshape(P, 1)
    tri = np.where(np.arange(P)[None, :] <= np.arange(P)[:, None], 0.0, NEG).astype(np.float32)
    mask = np.concatenate([tri, np.zeros((P, P), np.float32), tri], axis=1)
    dist = 255 - np.arange(384)
    n = np.clip(dist, 0, WINDOW - 1)
    exact = BUCKETS // 2
    big = exact + (np.log(np.maximum(n, 1) / exact) / math.log(MAX_DIST / exact) * (BUCKETS - exact)).astype(np.int32)
    bucket = np.where(n < exact, n, np.minimum(big, BUCKETS - 1))
    valid = (dist >= 0) & (dist <= WINDOW - 1)
    onehot = np.zeros((BUCKETS + 1, 384), np.float32)
    onehot[bucket[valid], np.nonzero(valid)[0]] = 1.0
    onehot[BUCKETS, ~valid] = NEG
    return {"c_ident": ident, "c_rot": rot, "c_invf": invf, "c_mask": mask, "c_onehot": onehot}


def kernel(**inputs):
    import concourse.bacc as bacc
    from concourse.bass_utils import run_bass_kernel_spmd as run

    shape = {
        "x": (T, D), "positions": (1, T), "rel_bias": (BUCKETS, HEADS_B), "small": (PC_END0, P),
        "conv_par": (PC_END - PC_CONVW, P), "mla_w_in": (D, 2 * RANK + 2 * ROPE),
        "mla_w_qb": (RANK, HEADS_A * (NOPE + ROPE)), "mla_w_kvb": (RANK, HEADS_A * (NOPE + VDIM)),
        "mla_w_o": (HEADS_A * VDIM, D), "swa_w_qkv": (D, QKV_B), "swa_b_v": (1, T),
        "swa_sinks": (1, HEADS_B), "swa_w_o": (HEADS_B * DH, D),
        "ffn_w_in": (2, D, 2 * FF), "ffn_w_out": (2, FF, D),
    }
    nc = bacc.Bacc("TRN2", target_bir_lowering=False, num_devices=1)
    rows = lambda *names: np.concatenate([np.asarray(inputs[n]).reshape(-1, P) for n in names])
    inputs["small"] = rows("norm_mix", "norm_ffn", "final_norm", "mla_g_q", "mla_g_kv", "swa_b_qkv", "swa_b_o")
    inputs["conv_par"] = rows("ffn_conv_w", "ffn_conv_b")
    inputs["swa_b_v"] = np.asarray(inputs["swa_b_qkv"]).reshape(-1)[QKV_B - T:]
    w = np.asarray(inputs["mla_w_in"]).reshape(D, 2 * RANK + ROPE)
    inputs["mla_w_in"] = np.concatenate([w, w[:, 2 * RANK:]], axis=1)
    arrays, args = {}, []
    for name, s in shape.items():
        arrays[name] = np.ascontiguousarray(inputs[name]).reshape(s)
    w = arrays["mla_w_qb"].reshape(RANK, UNITS_A, 2, NOPE + ROPE)
    arrays["mla_w_qb"] = np.ascontiguousarray(np.concatenate(
        [w[..., :NOPE].reshape(RANK, UNITS_A, 2 * NOPE), w[..., NOPE:].reshape(RANK, UNITS_A, 2 * ROPE)],
        axis=2)).reshape(RANK, -1)
    arrays.update(tables())
    for name, a in arrays.items():
        args.append(nc.dram_tensor(name, a.shape, mybir.dt.from_np(a.dtype), kind="ExternalInput").ap())
    y = nc.dram_tensor("y", (T, D), F32, kind="ExternalOutput").ap()
    build(nc, *args, y)
    r = run(nc, [arrays], core_ids=[0])
    return r.results[0]["y"].reshape(1, T, D)
```
